# Optimizing a Trainium2 kernel written in Bass

```python
import math
import jax
import jax.numpy as jnp
from jax import lax
import numpy as np

D_MODEL = 1024
BATCH = 1
SEQ = 1024
DEPTH = 1
DEC_BATCH = 8
DEC_SEQ = 8
PAST_LEN = 4096
PAGE_SIZE = 128

S5_WIDTH = D_MODEL // 2
S5_GROUP = 16
S5_GROUPS = S5_WIDTH // S5_GROUP
S5_STATE = 64
HEAD_DIM = 64
NSA_HEADS = D_MODEL // 128
NSA_KV_HEADS = 2
Q_PER_KV = NSA_HEADS // NSA_KV_HEADS
NSA_WIDTH = NSA_HEADS * HEAD_DIM
KV_WIDTH = NSA_KV_HEADS * HEAD_DIM
CMP_LEN = 32
CMP_STRIDE = 16
CMP_HIDDEN = 2 * HEAD_DIM
SLC_BLOCK = 64
SLC_TOPK = 16
WINDOW = 512
WIN_QBLOCK = 128
SLC_QCHUNK = 32
D_FF = 4 * D_MODEL
ROPE_THETA = 10000.0
EPS = 1e-6
NEG_INF = -1e30
FORCED = 1e9
SCALE = HEAD_DIM ** -0.5
IN_SIZES = (S5_WIDTH, NSA_WIDTH) + (KV_WIDTH,) * 6 + (3 * NSA_HEADS, 2 * D_MODEL)
N_IN = sum(IN_SIZES)

kernel_name = 'hybrid_s5_nsa_decode_step'

def _rmsnorm(x, w):
    xf = x.astype(jnp.float32)
    r = lax.rsqrt(jnp.mean(xf * xf, axis=-1, keepdims=True) + EPS)
    return (xf * r * w.astype(jnp.float32)).astype(x.dtype)

def _rope(x, pos):
    half = HEAD_DIM // 2
    inv = ROPE_THETA ** (-jnp.arange(half, dtype=jnp.float32) / half)
    ang = pos.astype(jnp.float32)[:, None] * inv[None, :]
    cos, sin = jnp.cos(ang)[:, None, :], jnp.sin(ang)[:, None, :]
    x1 = x[..., :half].astype(jnp.float32)
    x2 = x[..., half:].astype(jnp.float32)
    return jnp.concatenate([x1 * cos - x2 * sin, x2 * cos + x1 * sin], axis=-1).astype(x.dtype)

def _masked_softmax(s, mask):
    s = jnp.where(mask, s.astype(jnp.float32), NEG_INF)
    m = jnp.max(s, axis=-1, keepdims=True)
    p = jnp.where(mask, jnp.exp(s - m), 0.0)
    return p / jnp.maximum(jnp.sum(p, axis=-1, keepdims=True), 1e-30)

def _project(x, pos, p):
    B, T, _ = x.shape
    z = _rmsnorm(x, p['norm_mix_w']) @ p['w_in']
    offs = [int(o) for o in np.cumsum(IN_SIZES)[:-1]]
    u, q, kc, vc, ks, vs, kw, vw, g_nsa, g_mix = jnp.split(z, offs, axis=-1)
    kv = lambda t: t.reshape(B, T, NSA_KV_HEADS, HEAD_DIM)
    q = _rope(_rmsnorm(q.reshape(B, T, NSA_HEADS, HEAD_DIM), p['q_norm_w']), pos)
    kc = _rope(_rmsnorm(kv(kc), p['k_norm_w'][0]), pos)
    ks = _rope(_rmsnorm(kv(ks), p['k_norm_w'][1]), pos)
    kw = _rope(_rmsnorm(kv(kw), p['k_norm_w'][2]), pos)
    return u, q, kc, kv(vc), ks, kv(vs), kw, kv(vw), g_nsa, g_mix

def _complex_affine_combine(earlier, later):
    a1r, a1i, b1r, b1i = earlier
    a2r, a2i, b2r, b2i = later
    ar = a1r * a2r - a1i * a2i
    ai = a1r * a2i + a1i * a2r
    br = a2r * b1r - a2i * b1i + b2r
    bi = a2r * b1i + a2i * b1r + b2i
    return ar, ai, br, bi

def _s5(u, state_re, state_im, p):
    B, T, _ = u.shape
    f32 = jnp.float32
    uf = u.astype(f32)
    ug = uf.reshape(B, T, S5_GROUPS, S5_GROUP)
    lr, li = p['s5_lam_re'].astype(f32), p['s5_lam_im'].astype(f32)
    dt = jnp.exp(p['s5_log_dt'].astype(f32))[:, None]
    mag = jnp.exp(lr * dt)
    ab_re, ab_im = mag * jnp.cos(li * dt), mag * jnp.sin(li * dt)
    den = lr * lr + li * li
    f_re = ((ab_re - 1.0) * lr + ab_im * li) / den
    f_im = (ab_im * lr - (ab_re - 1.0) * li) / den
    br, bi = p['s5_b_re'].astype(f32), p['s5_b_im'].astype(f32)
    bb_re = f_re[..., None] * br - f_im[..., None] * bi
    bb_im = f_re[..., None] * bi + f_im[..., None] * br
    bu_re = jnp.einsum('btgh,gph->btgp', ug, bb_re)
    bu_im = jnp.einsum('btgh,gph->btgp', ug, bb_im)
    if state_re is not None:
        sr, si = state_re.astype(f32), state_im.astype(f32)
        bu_re = bu_re.at[:, 0].add(ab_re * sr - ab_im * si)
        bu_im = bu_im.at[:, 0].add(ab_re * si + ab_im * sr)
    a_re = jnp.broadcast_to(ab_re, bu_re.shape)
    a_im = jnp.broadcast_to(ab_im, bu_re.shape)
    _, _, x_re, x_im = lax.associative_scan(_complex_affine_combine, (a_re, a_im, bu_re, bu_im), axis=1)
    y = (jnp.einsum('btgp,ghp->btgh', x_re, p['s5_c_re'].astype(f32))
         - jnp.einsum('btgp,ghp->btgh', x_im, p['s5_c_im'].astype(f32)))
    y = y.reshape(B, T, S5_WIDTH) + p['s5_d'].astype(f32) * uf
    return y.astype(u.dtype), x_re[:, -1], x_im[:, -1]

def _compress(rows, pe, w1, w2):
    L = rows.shape[1]
    n_cmp = (L - CMP_LEN) // CMP_STRIDE + 1
    idx = np.arange(n_cmp)[:, None] * CMP_STRIDE + np.arange(CMP_LEN)[None, :]
    blk = rows[:, idx] + pe[None, None, :, None, :]
    hid = jax.nn.gelu(jnp.einsum('bnlhd,ldf->bnhf', blk, w1))
    return hid @ w2

def _cmp_attention(q, k_rows, v_rows, q_pos, p):
    B, T = q.shape[:2]
    kc = _compress(k_rows, p['cmp_pe_k'], p['cmp_wk1'], p['cmp_wk2'])
    vc = _compress(v_rows, p['cmp_pe_v'], p['cmp_wv1'], p['cmp_wv2'])
    n_cmp = kc.shape[1]
    qg = q.reshape(B, T, NSA_KV_HEADS, Q_PER_KV, HEAD_DIM)
    s = jnp.einsum('bthgd,bnhd->bthgn', qg, kc) * SCALE
    blk_end = jnp.arange(n_cmp) * CMP_STRIDE + CMP_LEN - 1
    mask = (blk_end[None, :] <= q_pos[:, None])[None, :, None, None, :]
    prob = _masked_softmax(s, mask)
    o = jnp.einsum('bthgn,bnhd->bthgd', prob.astype(vc.dtype), vc)
    return o.reshape(B, T, NSA_HEADS, HEAD_DIM), jnp.sum(prob, axis=3)

def _slc_attention(q, k_rows, v_rows, q_pos, p_grp):
    B, T = q.shape[:2]
    L = k_rows.shape[1]
    n_slc = -(-L // SLC_BLOCK)
    n_cmp = p_grp.shape[-1]
    topk = min(SLC_TOPK, n_slc)
    cs = np.arange(n_cmp) * CMP_STRIDE
    ss = np.arange(n_slc) * SLC_BLOCK
    ov = np.clip(np.minimum(cs[:, None] + CMP_LEN, ss[None, :] + SLC_BLOCK)
                 - np.maximum(cs[:, None], ss[None, :]), 0, None) / CMP_LEN
    imp = jnp.einsum('bthn,nj->bthj', p_grp, jnp.asarray(ov, jnp.float32))
    q_blk = q_pos // SLC_BLOCK
    j = jnp.arange(n_slc)
    valid = (j[None, :] <= q_blk[:, None])[None, :, None, :]
    forced = ((j[None, :] == 0) | (j[None, :] == q_blk[:, None])
              | (j[None, :] == q_blk[:, None] - 1))[None, :, None, :]
    score = jnp.where(forced, FORCED, jnp.where(valid, imp, NEG_INF))
    _, idx = lax.top_k(score, topk)
    sel_valid = jnp.take_along_axis(jnp.broadcast_to(valid, score.shape), idx, axis=-1)
    pad = n_slc * SLC_BLOCK - L
    to_blocks = lambda t: jnp.pad(t, ((0, 0), (0, pad), (0, 0), (0, 0))).reshape(
        B, n_slc, SLC_BLOCK, NSA_KV_HEADS, HEAD_DIM).transpose(0, 3, 1, 2, 4)
    kb, vb = to_blocks(k_rows), to_blocks(v_rows)
    qg = q.reshape(B, T, NSA_KV_HEADS, Q_PER_KV, HEAD_DIM)
    C = SLC_QCHUNK if T % SLC_QCHUNK == 0 else T
    nc = T // C
    bi = jnp.arange(B)[:, None, None, None]
    hi = jnp.arange(NSA_KV_HEADS)[None, None, :, None]

    def chunk(args):
        qc, ic, vc_, pc = args
        kg = kb[bi, hi, ic]
        vg = vb[bi, hi, ic]
        s = jnp.einsum('bchgd,bchkrd->bchgkr', qc, kg) * SCALE
        kpos = ic[..., None] * SLC_BLOCK + jnp.arange(SLC_BLOCK)
        mask = vc_[..., None] & (kpos <= pc[None, :, None, None, None])
        prob = _masked_softmax(s.reshape(B, C, NSA_KV_HEADS, Q_PER_KV, -1),
                               mask.reshape(B, C, NSA_KV_HEADS, 1, -1)).reshape(s.shape)
        return jnp.einsum('bchgkr,bchkrd->bchgd', prob.astype(vg.dtype), vg)

    to_chunks = lambda t: t.reshape((B, nc, C) + t.shape[2:]).swapaxes(0, 1)
    o = lax.map(chunk, (to_chunks(qg), to_chunks(idx), to_chunks(sel_valid), q_pos.reshape(nc, C)))
    return o.swapaxes(0, 1).reshape(B, T, NSA_HEADS, HEAD_DIM)

def _win_prompt(q, k, v):
    B, T = q.shape[:2]
    nb = T // WIN_QBLOCK
    span = WINDOW + WIN_QBLOCK
    padw = ((0, 0), (WINDOW, 0), (0, 0), (0, 0))
    kp, vp = jnp.pad(k, padw), jnp.pad(v, padw)
    idx = np.arange(nb)[:, None] * WIN_QBLOCK + np.arange(span)[None, :]
    kband, vband = kp[:, idx], vp[:, idx]
    kpos = idx - WINDOW
    qpos = np.arange(T).reshape(nb, WIN_QBLOCK)
    rel = qpos[:, :, None] - kpos[:, None, :]
    mask = (rel >= 0) & (rel < WINDOW) & (kpos[:, None, :] >= 0)
    qg = q.reshape(B, nb, WIN_QBLOCK, NSA_KV_HEADS, Q_PER_KV, HEAD_DIM)
    s = jnp.einsum('bnqhgd,bnkhd->bnqhgk', qg, kband) * SCALE
    prob = _masked_softmax(s, mask[None, :, :, None, None, :])
    o = jnp.einsum('bnqhgk,bnkhd->bnqhgd', prob.astype(vband.dtype), vband)
    return o.reshape(B, T, NSA_HEADS, HEAD_DIM)

def _win_sample(q, k_all, v_all, q_pos, k_pos):
    B, T = q.shape[:2]
    qg = q.reshape(B, T, NSA_KV_HEADS, Q_PER_KV, HEAD_DIM)
    s = jnp.einsum('bthgd,bkhd->bthgk', qg, k_all) * SCALE
    rel = q_pos[:, None] - k_pos[None, :]
    mask = ((rel >= 0) & (rel < WINDOW))[None, :, None, None, :]
    prob = _masked_softmax(s, mask)
    o = jnp.einsum('bthgk,bkhd->bthgd', prob.astype(v_all.dtype), v_all)
    return o.reshape(B, T, NSA_HEADS, HEAD_DIM)

def _layer(x, pos, p, past):
    B, T, _ = x.shape
    u, q, kc, vc, ks, vs, kw, vw, g_nsa, g_mix = _project(x, pos, p)
    if past is None:
        s5_y, s5_re, s5_im = _s5(u, None, None, p)
        kc_all, vc_all, ks_all, vs_all = kc, vc, ks, vs
        o_win = _win_prompt(q, kw, vw)
        keep = min(WINDOW, T)
        win_k, win_v = kw[:, T - keep:], vw[:, T - keep:]
    else:
        s5_y, s5_re, s5_im = _s5(u, past['s5_re'], past['s5_im'], p)
        kc_all = jnp.concatenate([past['k_cmp'], kc], axis=1)
        vc_all = jnp.concatenate([past['v_cmp'], vc], axis=1)
        ks_all = jnp.concatenate([past['k_slc'], ks], axis=1)
        vs_all = jnp.concatenate([past['v_slc'], vs], axis=1)
        wb = past['k_win'].shape[1]
        kw_all = jnp.concatenate([past['k_win'], kw], axis=1)
        vw_all = jnp.concatenate([past['v_win'], vw], axis=1)
        k_pos = pos[0] - wb + jnp.arange(wb + T)
        o_win = _win_sample(q, kw_all, vw_all, pos, k_pos)
        win_k, win_v = kw_all[:, T:], vw_all[:, T:]
    o_cmp, p_grp = _cmp_attention(q, kc_all, vc_all, pos, p)
    o_slc = _slc_attention(q, ks_all, vs_all, pos, p_grp)
    g = jax.nn.sigmoid(g_nsa.reshape(B, T, NSA_HEADS, 3))
    o = g[..., 0:1] * o_cmp + g[..., 1:2] * o_slc + g[..., 2:3] * o_win
    nsa_out = o.reshape(B, T, NSA_WIDTH) @ p['nsa_w_up']
    yg = jax.nn.gelu(s5_y)
    s5_out = (yg * jax.nn.sigmoid(yg @ p['s5_w_glu'])) @ p['s5_w_up']
    gate = jax.nn.sigmoid(g_mix)
    merged = gate[..., :D_MODEL] * s5_out + gate[..., D_MODEL:] * nsa_out
    x = x + merged @ p['w_out']
    h = _rmsnorm(x, p['norm_ffn_w'])
    x = x + jnp.square(jax.nn.relu(h @ p['w_ffn1'])) @ p['w_ffn2']
    return x, (kc, vc, ks, vs, win_k, win_v, s5_re, s5_im)

def setup_inputs(seed: int = 0) -> dict:
    key = jax.random.key(seed)
    keys = iter(jax.random.split(key, 48))

    def nrm(shape, scale=1.0):
        return scale * jax.random.normal(next(keys), shape, jnp.float32)

    n_pages = PAST_LEN // PAGE_SIZE
    n_used = DEC_BATCH * n_pages
    n_pool = n_used + max(1, n_used // 4)
    win_buf = min(WINDOW, PAST_LEN)
    kv_page = (DEPTH, n_pool, PAGE_SIZE, NSA_KV_HEADS, HEAD_DIM)
    kv_win = (DEPTH, DEC_BATCH, win_buf, NSA_KV_HEADS, HEAD_DIM)
    s5_st = (DEPTH, DEC_BATCH, S5_GROUPS, S5_STATE)
    lam = (DEPTH, S5_GROUPS, S5_STATE)
    n_idx = jnp.arange(S5_STATE, dtype=jnp.float32)
    inputs = {}
    inputs['x_prompt'] = nrm((BATCH, SEQ, D_MODEL))
    inputs['x_sample'] = nrm((DEC_BATCH, DEC_SEQ, D_MODEL))
    inputs['cache_k_cmp'] = nrm(kv_page)
    inputs['cache_v_cmp'] = nrm(kv_page)
    inputs['cache_k_slc'] = nrm(kv_page)
    inputs['cache_v_slc'] = nrm(kv_page)
    inputs['state_k_win'] = nrm(kv_win)
    inputs['state_v_win'] = nrm(kv_win)
    inputs['state_s5_re'] = nrm(s5_st, 0.3)
    inputs['state_s5_im'] = nrm(s5_st, 0.3)
    inputs['page_table'] = jax.random.permutation(next(keys), n_pool)[:n_used].reshape(
        DEC_BATCH, n_pages).astype(jnp.int32)
    inputs['norm_mix_w'] = 1.0 + nrm((DEPTH, D_MODEL), 0.02)
    inputs['w_in'] = nrm((DEPTH, D_MODEL, N_IN), D_MODEL ** -0.5)
    inputs['s5_lam_re'] = -0.5 + nrm(lam, 0.02)
    inputs['s5_lam_im'] = math.pi * n_idx + nrm(lam, 0.02)
    inputs['s5_log_dt'] = jax.random.uniform(next(keys), (DEPTH, S5_GROUPS), jnp.float32,
                                             math.log(1e-3), math.log(1e-1))
    inputs['s5_b_re'] = nrm((DEPTH, S5_GROUPS, S5_STATE, S5_GROUP), (2 * S5_GROUP) ** -0.5)
    inputs['s5_b_im'] = nrm((DEPTH, S5_GROUPS, S5_STATE, S5_GROUP), (2 * S5_GROUP) ** -0.5)
    inputs['s5_c_re'] = nrm((DEPTH, S5_GROUPS, S5_GROUP, S5_STATE), S5_STATE ** -0.5)
    inputs['s5_c_im'] = nrm((DEPTH, S5_GROUPS, S5_GROUP, S5_STATE), S5_STATE ** -0.5)
    inputs['s5_d'] = nrm((DEPTH, S5_WIDTH))
    inputs['s5_w_glu'] = nrm((DEPTH, S5_WIDTH, S5_WIDTH), S5_WIDTH ** -0.5)
    inputs['s5_w_up'] = nrm((DEPTH, S5_WIDTH, D_MODEL), S5_WIDTH ** -0.5)
    inputs['q_norm_w'] = 1.0 + nrm((DEPTH, HEAD_DIM), 0.02)
    inputs['k_norm_w'] = 1.0 + nrm((DEPTH, 3, HEAD_DIM), 0.02)
    inputs['cmp_pe_k'] = nrm((DEPTH, CMP_LEN, HEAD_DIM), 0.1)
    inputs['cmp_wk1'] = nrm((DEPTH, CMP_LEN, HEAD_DIM, CMP_HIDDEN), (CMP_LEN * HEAD_DIM) ** -0.5)
    inputs['cmp_wk2'] = nrm((DEPTH, CMP_HIDDEN, HEAD_DIM), CMP_HIDDEN ** -0.5)
    inputs['cmp_pe_v'] = nrm((DEPTH, CMP_LEN, HEAD_DIM), 0.1)
    inputs['cmp_wv1'] = nrm((DEPTH, CMP_LEN, HEAD_DIM, CMP_HIDDEN), (CMP_LEN * HEAD_DIM) ** -0.5)
    inputs['cmp_wv2'] = nrm((DEPTH, CMP_HIDDEN, HEAD_DIM), CMP_HIDDEN ** -0.5)
    inputs['nsa_w_up'] = nrm((DEPTH, NSA_WIDTH, D_MODEL), NSA_WIDTH ** -0.5)
    inputs['w_out'] = nrm((DEPTH, D_MODEL, D_MODEL), D_MODEL ** -0.5)
    inputs['norm_ffn_w'] = 1.0 + nrm((DEPTH, D_MODEL), 0.02)
    inputs['w_ffn1'] = nrm((DEPTH, D_MODEL, D_FF), D_MODEL ** -0.5)
    inputs['w_ffn2'] = nrm((DEPTH, D_FF, D_MODEL), D_FF ** -0.5)
    return inputs

def reference(x_prompt, x_sample, cache_k_cmp, cache_v_cmp, cache_k_slc, cache_v_slc,
              state_k_win, state_v_win, state_s5_re, state_s5_im, page_table,
              norm_mix_w, w_in, s5_lam_re, s5_lam_im, s5_log_dt, s5_b_re, s5_b_im,
              s5_c_re, s5_c_im, s5_d, s5_w_glu, s5_w_up, q_norm_w, k_norm_w,
              cmp_pe_k, cmp_wk1, cmp_wk2, cmp_pe_v, cmp_wv1, cmp_wv2, nsa_w_up,
              w_out, norm_ffn_w, w_ffn1, w_ffn2):
    n_seq, n_pages = page_table.shape
    past_len = n_pages * PAGE_SIZE
    pos_p = jnp.arange(x_prompt.shape[1], dtype=jnp.int32)
    pos_s = past_len + jnp.arange(x_sample.shape[1], dtype=jnp.int32)
    y_prompt, y_sample = x_prompt, x_sample
    outs_p, outs_s = [], []
    for l in range(DEPTH):
        prm = dict(norm_mix_w=norm_mix_w[l], w_in=w_in[l], s5_lam_re=s5_lam_re[l],
                   s5_lam_im=s5_lam_im[l], s5_log_dt=s5_log_dt[l], s5_b_re=s5_b_re[l],
                   s5_b_im=s5_b_im[l], s5_c_re=s5_c_re[l], s5_c_im=s5_c_im[l], s5_d=s5_d[l],
                   s5_w_glu=s5_w_glu[l], s5_w_up=s5_w_up[l], q_norm_w=q_norm_w[l],
                   k_norm_w=k_norm_w[l], cmp_pe_k=cmp_pe_k[l], cmp_wk1=cmp_wk1[l],
                   cmp_wk2=cmp_wk2[l], cmp_pe_v=cmp_pe_v[l], cmp_wv1=cmp_wv1[l],
                   cmp_wv2=cmp_wv2[l], nsa_w_up=nsa_w_up[l], w_out=w_out[l],
                   norm_ffn_w=norm_ffn_w[l], w_ffn1=w_ffn1[l], w_ffn2=w_ffn2[l])
        gather = lambda c: c[l][page_table].reshape(n_seq, past_len, NSA_KV_HEADS, HEAD_DIM)
        past = dict(k_cmp=gather(cache_k_cmp), v_cmp=gather(cache_v_cmp),
                    k_slc=gather(cache_k_slc), v_slc=gather(cache_v_slc),
                    k_win=state_k_win[l], v_win=state_v_win[l],
                    s5_re=state_s5_re[l], s5_im=state_s5_im[l])
        y_prompt, st_p = _layer(y_prompt, pos_p, prm, None)
        y_sample, st_s = _layer(y_sample, pos_s, prm, past)
        outs_p.append(st_p)
        outs_s.append(st_s)
    k_cmp_p, v_cmp_p, k_slc_p, v_slc_p, k_win_p, v_win_p, s5_re_p, s5_im_p = [
        jnp.stack([o[i] for o in outs_p]) for i in range(8)]
    k_cmp_s, v_cmp_s, k_slc_s, v_slc_s, k_win_s, v_win_s, s5_re_s, s5_im_s = [
        jnp.stack([o[i] for o in outs_s]) for i in range(8)]
    return (y_prompt, y_sample, k_cmp_p, k_cmp_s, v_cmp_p, v_cmp_s, k_slc_p, k_slc_s,
            v_slc_p, v_slc_s, k_win_p, k_win_s, v_win_p, v_win_s,
            s5_re_p, s5_re_s, s5_im_p, s5_im_s)


_drawn_inputs = setup_inputs


def setup_inputs(seed=0):
    import zlib

    import numpy as np

    out = dict(_drawn_inputs(seed))
    spreads = {}
    factors = {'cache_k_cmp': 3.631,
     'cache_v_cmp': 4.122,
     'cache_k_slc': 4.325,
     'cache_v_slc': 3.417,
     'norm_mix_w': 2.681,
     'q_norm_w': 8.0,
     'cmp_pe_k': 8.0,
     'cmp_pe_v': 3.428,
     'norm_ffn_w': 3.192}
    for name, (base, spread) in spreads.items():
        noise = np.random.default_rng([zlib.crc32(name.encode()), seed]).standard_normal(out[name].shape)
        drawn = base * np.exp(spread * noise) if base else spread * noise
        out[name] = jnp.asarray(drawn.astype(out[name].dtype))
    for name, factor in factors.items():
        out[name] = (out[name] * factor).astype(out[name].dtype)
    return out
```

```python
from contextlib import ExitStack

import numpy as np
import concourse.bass as bass
from concourse import mybir

F32 = mybir.dt.float32
I32 = mybir.dt.int32
ALU = mybir.AluOpType
ACT = mybir.ActivationFunctionType
X = mybir.AxisListType.X
XY = mybir.AxisListType.XY
ds = bass.ds

P = 128
D = 1024
SEQ = 1024
NB, TS = 8, 8
NS = NB * TS
PAST, PAGE = 4096, 128
PAGES = PAST // PAGE
S5W, S5G, S5H, S5P = 512, 32, 16, 64
DH, NH, NKV, NG = 64, 8, 2, 4
KVW = NKV * DH
CL, CS, CH = 32, 16, 128
NSLC, TOPK = 65, 16
WIN = 512
DFF = 4096
EPS = 1e-6
NEG = -1e30
SCALE = DH ** -0.5
DT = D // P
TT = SEQ // P
NT = TT + 1
TOK = SEQ + NS
TPAD = NT * P
OFF_Q = S5W
N_QKV = NH * DH + 6 * KVW + 3 * NH
OFF_MIX = OFF_Q + N_QKV
HN = NH + 6
C_TANH = 0.7978845608028654
C_CUBE = 0.044715


class Chain:

    def __init__(self, eng, sem):
        self.eng, self.sem, self.n = eng, sem, 0

    def put(self, ins):
        ins.then_inc(self.sem, 1)
        self.n += 1

    def sync(self):
        self.eng.wait_ge(self.sem, self.n)

    def __call__(self, ins):
        self.put(ins)
        self.sync()

    def restart(self):
        self.eng.sem_clear(self.sem)
        self.n = 0


class Semaphores:

    def __init__(self, nc, prefix):
        self.nc, self.prefix, self.held, self.stack = nc, prefix, [], ExitStack()

    def __enter__(self):
        return self

    def __call__(self, name):
        self.held.append(self.stack.enter_context(self.nc.semaphore(self.prefix + name)))
        return self.held[-1]

    def __exit__(self, *failure):
        if failure[0] is None:
            with self.nc.Block() as block:
                @block.sync
                def _(sp):
                    for s in self.held:
                        sp.sem_clear(s)
        self.stack.close()


def row(ap):
    return ap.rearrange("p a n -> p (a n)")


def token_tiles(eng, body):
    body(0, 0)
    body(1, 1)
    with eng.Fori(1, TT // 2) as i:
        for k in range(2):
            body(2 * i + k, k)
    body(TT, 0)


def behind(t, n):
    return not isinstance(t, int) or t >= n


def phase_project(nc, d, r):
    with ExitStack() as ctx:
        sb = lambda name, shape: ctx.enter_context(nc.sbuf_tensor(name, shape, F32))
        pb = lambda name, shape: ctx.enter_context(nc.psum_tensor(name, shape, F32))
        sem = ctx.enter_context(Semaphores(nc, "p_"))
        w_qkv = sb("w_qkv", [P, DT, N_QKV])
        mixw = sb("mixw", [P, DT])
        normw = sb("normw", [P, HN, DH])
        rope = sb("rope", [P, NT, 2, DH // 2])
        xt = [sb(f"xt{k}", [P, D]) for k in range(2)]
        xn = [sb(f"xn{k}", [P, D]) for k in range(2)]
        sq_junk = sb("sq_junk", [P, D])
        ssum = sb("ssum", [P, 2])
        rstd = sb("rstd", [P, 2])
        hs = [sb(f"hs{k}", [P, DT, P]) for k in range(2)]
        qk = [sb(f"qk{k}", [P, HN, DH]) for k in range(2)]
        roped = [sb(f"roped{k}", [P, HN, DH]) for k in range(2)]
        tmp = sb("tmp", [P, HN, DH])
        tmp2 = sb("tmp2", [P, HN, DH])
        hsum = sb("hsum", [P, HN])
        hrms = sb("hrms", [P, HN])
        rms = sb("rms", [P, 2])
        eps = sb("eps", [P, 1])
        k_nat = sb("k_nat", [P, NT, 3, KVW])
        xT_ps = pb("xT_ps", [P, DT, P])
        z_ps = pb("z_ps", [P, 3, 512])
        qT_ps = pb("qT_ps", [P, 8, P])

        w_ld = [sem(f"w_ld{c}") for c in range(DT)]
        c_ld = [sem(f"c_ld{c}") for c in range(6)]
        x_ld = [sem("x_ld0"), sem("x_ld1")]
        squared, xn_ready, xT_done, hs_ready = sem("squared"), sem("xn_ready"), sem("xT_done"), sem("hs_ready")
        hT_copied, z_done, z_evac = sem("hT_copied"), sem("z_done"), sem("z_evac")
        rope_done, k_copied, qT_done, qT_evac = sem("rope_done"), sem("k_copied"), sem("qT_done"), sem("qT_evac")
        x_rms, head_sums, head_rms, eps_set = sem("x_rms"), sem("head_sums"), sem("head_rms"), sem("eps_set")
        tanh_done, gates_ready = sem("tanh_done"), sem("gates_ready")
        ch_v, stored, copied = sem("ch_v"), sem("stored"), sem("copied")
        block = ctx.enter_context(nc.Block())
        hT, qkT, v_nat, gates, ident = r["hT"], r["qkT"], r["v_nat"], r["gates"], r["ident"]

        @block.sync
        def _(sp):
            x_p = d["x_prompt"].rearrange("a (t p) n -> (a t) p n", p=P)
            sp.dma_start(xt[0][:], x_p[0]).then_inc(x_ld[0], 16)
            sp.dma_start(xt[1][:], x_p[1]).then_inc(x_ld[1], 16)
            w = d["w_in"][0, :, OFF_Q:OFF_MIX].rearrange("(c p) n -> p c n", p=P)
            for c in range(DT):
                sp.dma_start(w_qkv[:, c, :], w[:, c, :]).then_inc(w_ld[c], 16)
            with sp.Fori(0, TT // 2 - 1) as i:
                for k in range(2):
                    sp.wait_ge(xn_ready, 2 * i + k + 1)
                    sp.dma_start(xt[k][:], x_p[ds(2 * i + k + 2, 1)].rearrange("t p n -> (t p) n")).then_inc(x_ld[k], 16)
            sp.wait_ge(xn_ready, TT - 1)
            sp.dma_start(xt[0][0:NS, :], d["x_sample"].rearrange("b t n -> (b t) n")).then_inc(x_ld[0], 16)
            sp.wait_ge(z_evac, 3 * NT)
            sp.wait_ge(k_copied, NT)
            n = 0
            flat = lambda name: d[name].rearrange("z a t h c -> (z a t) (h c)")
            for src, c, names in ((k_nat, 0, "k_cmp"), (v_nat, 0, "v_cmp"), (k_nat, 1, "k_slc"), (v_nat, 1, "v_slc")):
                sp.dma_start(flat(names + "_p").rearrange("(t p) c -> p t c", p=P), src[:, 0:TT, c, :]).then_inc(stored, 16)
                sp.dma_start(flat(names + "_s"), src[0:NS, TT, c, :]).then_inc(stored, 16)
                n += 2
            for src, names in ((k_nat, "k_win"), (v_nat, "v_win")):
                sp.dma_start(flat(names + "_p").rearrange("(t p) c -> p t c", p=P),
                             src[:, TT - WIN // P:TT, 2, :]).then_inc(stored, 16)
                new = d[names + "_s"].rearrange("z b w h c -> (z b) w (h c)")
                for b in range(NB):
                    sp.dma_start(new[b, WIN - TS:WIN, :], src[TS * b:TS * b + TS, TT, 2, :]).then_inc(stored, 16)
                    n += 1
                n += 1
            sp.dma_start(d["v_new"].rearrange("n (c w) -> n c w", c=2), v_nat[0:NS, TT, 1:3, :]).then_inc(stored, 16)
            sp.wait_ge(gates_ready, 1)
            sp.dma_start(d["g_new"], gates[0:NS, TT, :]).then_inc(stored, 16)
            sp.wait_ge(stored, 16 * (n + 2))

        @block.scalar
        def _(act):
            act.dma_start(mixw[:], d["norm_mix_w"].rearrange("z (c p) -> p (z c)", p=P),
                          allow_slow_non_contiguous=True).then_inc(c_ld[0], 16)
            act.dma_start(normw[:, 0:NH, :], d["normw_q"]).then_inc(c_ld[1], 16)
            for h in range(NKV):
                act.dma_start(normw[:, NH:HN, :].rearrange("p (b h) c -> p b h c", h=NKV)[:, :, h, :],
                              d["normw_k"]).then_inc(c_ld[4 + h], 16)
            act.dma_start(rope[:], d["rope"].rearrange("(t p) c f -> p t c f", p=P)).then_inc(c_ld[3], 16)
            act.dma_start(ident[:], d["identity"]).then_inc(c_ld[2], 16)
            for n, (state, out) in enumerate((("state_k_win", "k_win_s"), ("state_v_win", "v_win_s"))):
                keep = lambda ap, at: ap.rearrange("z b w h c -> (z b) w (h c)")[:, at:at + WIN - TS, :]
                act.dma_start(keep(d[out], 0), keep(d[state], TS)).then_inc(copied, 16)

            def evac(t, k):
                act.wait_ge(z_done, 3 * t + 1)
                if behind(t, 2):
                    act.wait_ge(rope_done, t - 1)
                pair = lambda ap: ap.rearrange("p (c w) -> p c w", w=KVW)
                act.activation(qk[k][:, 0:NH, :].rearrange("p (j g) c -> p g j c", g=NKV),
                               z_ps[:, 0, :].rearrange("p (g j c) -> p g j c", g=NKV, c=DH), ACT.Copy).then_inc(z_evac, 1)
                act.wait_ge(z_done, 3 * t + 2)
                kv = z_ps[:, 1, :].rearrange("p (b c w) -> p b c w", b=2, c=2)
                act.activation(qk[k][:, NH:NH + 4, :].rearrange("p (b h) c -> p b (h c)", b=2), kv[:, :, 0, :], ACT.Copy)
                v_at = v_nat[:, ds(t, 1), :, :].rearrange("p t c w -> p (t c) w")
                act.activation(v_at[:, 0:2, :], kv[:, :, 1, :], ACT.Copy).then_inc(z_evac, 1)
                act.wait_ge(z_done, 3 * t + 3)
                act.activation(qk[k][:, NH + 4:HN, :].rearrange("p h c -> p (h c)"), z_ps[:, 2, 0:KVW], ACT.Copy)
                act.activation(v_at[:, 2, :], z_ps[:, 2, KVW:2 * KVW], ACT.Copy)
                act.activation(row(gates[:, ds(t, 1), :]), z_ps[:, 2, 2 * KVW:2 * KVW + 3 * NH],
                               ACT.Copy).then_inc(z_evac, 1)

            def head_root(t):
                act.wait_ge(head_sums, t + 1)
                act.activation(hrms[:], hsum[:], ACT.Sqrt, bias=eps[:], scale=1.0 / DH).then_inc(head_rms, 1)

            def evac_qT(t, k):
                act.wait_ge(qT_done, t + 1)
                act.activation(qkT[:, 0:NG, ds(t * P, P)], qT_ps[:, 0:NG, :], ACT.Copy, scale=SCALE)
                act.activation(qkT[:, NG:NG + 2, ds(t * P, P)], qT_ps[:, NG:NG + 2, :], ACT.Copy).then_inc(qT_evac, 1)

            def square(t, k, turn):
                act.wait_ge(x_ld[k], 16 * turn + 16)
                if behind(t, 2):
                    act.wait_ge(xn_ready, t - 1)
                act.activation(sq_junk[:], xt[k][:], ACT.Square, accum_out=ssum[:, k:k + 1]).then_inc(squared, 1)
                act.wait_ge(squared, t + 1)
                act.activation(rms[:, k:k + 1], ssum[:, k:k + 1], ACT.Sqrt, bias=eps[:], scale=1.0 / D).then_inc(x_rms, 1)

            act.wait_ge(eps_set, 1)
            square(0, 0, 0)
            square(1, 1, 0)

            def body(t, k, turn):
                if not isinstance(t, int) or t + 2 < NT:
                    square(t + 2, k, turn + 1)
                if behind(t, 1):
                    head_root(t - 1)
                evac(t, k)
                if behind(t, 2):
                    evac_qT(t - 2, k)

            body(0, 0, 0)
            body(1, 1, 0)
            with act.Fori(1, TT // 2 - 1) as i:
                for k in range(2):
                    body(2 * i + k, k, i)
            for t in range(TT - 2, NT):
                body(t, t % 2, t // 2)
            head_root(TT)
            evac_qT(TT - 1, 1)
            evac_qT(TT, 0)
            act.wait_ge(z_evac, 3 * NT)
            act.activation(gates[:], gates[:], ACT.Tanh, scale=0.5).then_inc(tanh_done, 1)
            act.wait_ge(copied, 32)

        @block.vector
        def _(dve):
            link = Chain(dve, ch_v)
            dve.memset(eps[:], EPS).then_inc(eps_set, 1)
            for c in (0, 1, 3, 4, 5):
                dve.wait_ge(c_ld[c], 16)

            def normalise(t, k):
                dve.wait_ge(x_rms, t + 1)
                link(dve.reciprocal(rstd[:, k:k + 1], rms[:, k:k + 1]))
                if behind(t, 2):
                    dve.wait_ge(xT_done, t - 1)
                dve.tensor_scalar(xn[k][:], xt[k][:], rstd[:, k:k + 1], None, ALU.mult).then_inc(xn_ready, 1)

            def weigh(t, k):
                dve.wait_ge(xT_done, t + 1)
                if behind(t, 2):
                    dve.wait_ge(z_done, 3 * t - 3)
                    dve.wait_ge(hT_copied, t - 1)
                dve.tensor_tensor(hs[k][:], xT_ps[:], mixw[:].unsqueeze(2).to_broadcast([P, DT, P]),
                                  ALU.mult).then_inc(hs_ready, 1)

            def rotate(t, k):
                dve.wait_ge(z_evac, 3 * t + 3)
                q = qk[k]
                link(dve.tensor_tensor(tmp[:], q[:], q[:], ALU.mult))
                link(dve.tensor_reduce(hsum[:], tmp[:], X, ALU.add))
                dve.sem_inc(head_sums, 1)
                dve.wait_ge(head_rms, t + 1)
                link(dve.reciprocal(hsum[:], hrms[:]))
                link(dve.tensor_tensor(tmp[:], q[:], hsum[:].unsqueeze(2).to_broadcast([P, HN, DH]), ALU.mult))
                link(dve.tensor_tensor(tmp2[:], tmp[:], normw[:], ALU.mult))
                half = DH // 2
                cos = rope[:, ds(t, 1), 0, :].to_broadcast([P, HN, half])
                sin = rope[:, ds(t, 1), 1, :].to_broadcast([P, HN, half])
                link.put(dve.tensor_tensor(q[:, :, 0:half], tmp2[:, :, 0:half], cos, ALU.mult))
                link.put(dve.tensor_tensor(tmp[:, :, 0:half], tmp2[:, :, half:DH], sin, ALU.mult))
                link.put(dve.tensor_tensor(q[:, :, half:DH], tmp2[:, :, half:DH], cos, ALU.mult))
                link(dve.tensor_tensor(tmp[:, :, half:DH], tmp2[:, :, 0:half], sin, ALU.mult))
                if behind(t, 2):
                    dve.wait_ge(qT_done, t - 1)
                    dve.wait_ge(k_copied, t - 1)
                link.put(dve.tensor_tensor(roped[k][:, :, 0:half], q[:, :, 0:half], tmp[:, :, 0:half], ALU.subtract))
                link(dve.tensor_tensor(roped[k][:, :, half:DH], q[:, :, half:DH], tmp[:, :, half:DH], ALU.add))
                link.restart()
                dve.sem_inc(rope_done, 1)

            normalise(0, 0)
            weigh(0, 0)
            normalise(1, 1)

            def body(t, k):
                if not isinstance(t, int) or t + 1 < NT:
                    weigh(t + 1, 1 - k)
                if not isinstance(t, int) or t + 2 < NT:
                    normalise(t + 2, k)
                if behind(t, 1):
                    rotate(t - 1, 1 - k)

            body(0, 0)
            body(1, 1)
            with dve.Fori(1, TT // 2 - 1) as i:
                for k in range(2):
                    body(2 * i + k, k)
            for t in range(TT - 2, NT):
                body(t, t % 2)
            rotate(TT, 0)
            dve.wait_ge(tanh_done, 1)
            dve.tensor_scalar(gates[:], gates[:], 0.5, 0.5, ALU.mult, ALU.add).then_inc(gates_ready, 1)

        @block.gpsimd
        def _(pool):
            def body(t, k):
                pool.wait_ge(hs_ready, t + 1)
                pool.tensor_copy(hT[:, :, ds(t * P, P)], hs[k][:]).then_inc(hT_copied, 1)
                pool.wait_ge(rope_done, t + 1)
                pool.tensor_copy(k_nat[:, ds(t, 1), :, :].rearrange("p t c w -> p (t c w)"),
                                 roped[k][:, NH:HN, :].rearrange("p h c -> p (h c)")).then_inc(k_copied, 1)

            token_tiles(pool, body)

        @block.tensor
        def _(pe):
            def transpose_x(t, k):
                pe.wait_ge(xn_ready, t + 1)
                if behind(t, 1):
                    pe.wait_ge(hs_ready, t)
                for c in range(DT):
                    ins = pe.transpose(xT_ps[:, c, :], xn[k][:, c * P:(c + 1) * P], ident[:])
                ins.then_inc(xT_done, 1)

            def project(t, k):
                pe.wait_ge(hs_ready, t + 1)
                parts = ((0, 512), (512, 512), (1024, N_QKV - 1024))
                multiply = lambda b, c: pe.matmul(z_ps[:, b, 0:parts[b][1]], hs[k][:, c, :],
                                                  w_qkv[:, c, parts[b][0]:sum(parts[b])], start=(c == 0), stop=(c == DT - 1))
                if not behind(t, 1):
                    for c in range(DT):
                        pe.wait_ge(w_ld[c], 16)
                        for b in range(3):
                            ins = multiply(b, c)
                            if c == DT - 1:
                                ins.then_inc(z_done, 1)
                    return
                for b in range(3):
                    pe.wait_ge(z_evac, 3 * t - 2 + b)
                    for c in range(DT):
                        ins = multiply(b, c)
                    ins.then_inc(z_done, 1)

            def transpose_qk(t, k):
                pe.wait_ge(rope_done, t + 1)
                if behind(t, 1):
                    pe.wait_ge(qT_evac, t)
                for j in range(NG):
                    pe.transpose(qT_ps[:, j, :], roped[k][:, 2 * j:2 * j + 2, :].rearrange("p h c -> p (h c)"), ident[:])
                for j in range(2):
                    ins = pe.transpose(qT_ps[:, NG + j, :],
                                       roped[k][:, NH + 2 + 2 * j:NH + 4 + 2 * j, :].rearrange("p h c -> p (h c)"), ident[:])
                ins.then_inc(qT_done, 1)

            pe.wait_ge(c_ld[2], 16)
            transpose_x(0, 0)

            def body(t, k):
                if not isinstance(t, int) or t + 1 < NT:
                    transpose_x(t + 1, 1 - k)
                project(t, k)
                if behind(t, 2):
                    transpose_qk(t - 2, k)

            token_tiles(pe, body)
            transpose_qk(TT - 1, 1)
            transpose_qk(TT, 0)


CHUNKS = [(0, 384), (384, 384), (768, 320)]
assert sum(n for _, n in CHUNKS) == TOK


def phase_gemm(nc, name, weights, n_pairs, kt, src, act_step, dve_step=None):
    with ExitStack() as ctx:
        sem = ctx.enter_context(Semaphores(nc, name))
        w = [ctx.enter_context(nc.sbuf_tensor(f"{name}_w{k}", [P, kt, 256], F32)) for k in range(2)]
        ps = [ctx.enter_context(nc.psum_tensor(f"{name}_ps{f}", [P, 3, 512], F32)) for f in range(2)]
        w_ld = [sem("w_ld0"), sem("w_ld1")]
        multiplied, taken, finished, ch_v = sem("multiplied"), sem("taken"), sem("finished"), sem("ch_v")
        block = ctx.enter_context(nc.Block())

        @block.sync
        def _(sp):
            for k in range(2):
                sp.dma_start(w[k][:], weights(k)).then_inc(w_ld[k], 16)
            if n_pairs > 1:
                with sp.Fori(0, n_pairs - 1) as i:
                    for k in range(2):
                        sp.wait_ge(multiplied, 4 * i + 2 * k + 2)
                        sp.dma_start(w[k][:], weights(2 * i + k + 2)).then_inc(w_ld[k], 16)

        def turns(eng, body):
            for k in range(2):
                for f in range(2):
                    body(0, k, f, k == 0)
            if n_pairs > 1:
                with eng.Fori(1, n_pairs) as i:
                    for k in range(2):
                        for f in range(2):
                            body(i, k, f, False)

        @block.tensor
        def _(pe):
            def body(i, k, f, first):
                if f == 0:
                    pe.wait_ge(w_ld[k], 16 * i + 16)
                if not first:
                    pe.wait_ge(taken, 4 * i + 2 * k + f - 1)
                for c in range(kt):
                    for b, (at, n) in enumerate(CHUNKS):
                        ins = pe.matmul(ps[f][:, b, 0:n], w[k][:, c, f * P:(f + 1) * P], src[:, c, at:at + n],
                                        start=(c == 0), stop=(c == kt - 1))
                ins.then_inc(multiplied, 1)

            turns(pe, body)

        @block.scalar
        def _(act):
            def body(i, k, f, first):
                act.wait_ge(multiplied, 4 * i + 2 * k + f + 1)
                ft = 4 * i + 2 * k + f
                for c, (at, n) in enumerate(CHUNKS):
                    ins = act_step(act, ft, c, at, n, ps[f][:, c, 0:n])
                ins.then_inc(taken, 1)

            turns(act, body)

        if dve_step is not None:
            @block.vector
            def _(dve):
                link = Chain(dve, ch_v)

                def body(i, k, f, first):
                    dve.wait_ge(taken, 4 * i + 2 * k + f + 1)
                    for c, (at, n) in enumerate(CHUNKS):
                        dve_step(dve, 4 * i + 2 * k + f, c, at, n, link)
                    link.restart()

                turns(dve, body)


ST = S5G * S5P // P
FT = S5W // P
SJ = ST // FT
LB = 256
ROUND = 12582912.0
TWO_PI_HI, TWO_PI_LO = 6.28125, 0.0019353071795864769
NEARLY_PI = 3.1415925


def phase_s5(nc, d, r):
    with ExitStack() as ctx:
        sb = lambda name, shape: ctx.enter_context(nc.sbuf_tensor("s5_" + name, shape, F32))
        pb = lambda name, shape: ctx.enter_context(nc.psum_tensor("s5_" + name, shape, F32))
        sem = ctx.enter_context(Semaphores(nc, "s5_"))
        uT, yT, ident = r["uT"], r["yT"], r["ident"]
        ldt = sb("ldt", [ST, 2])
        dt = sb("dt", [ST, 2])
        prm = sb("prm", [P, 5, ST])
        bz = sb("bz", [P, 2, P])
        bbT = sb("bbT", [P, 2, ST, P])
        cz = sb("cz", [P, 2, ST, 2, S5H])
        rot = sb("rot", [P, 2, ST, LB])
        dvec = sb("dvec", [P, FT])
        snat = sb("snat", [P, 2, P])
        state = sb("state", [P, 2, NB, ST])
        bbs = sb("bbs", [P, 2, SJ, P])
        czs = sb("czs", [P, 3, SJ, 2 * S5H])
        pms = sb("pms", [P, 5, SJ])
        m_row = sb("m_row", [P, LB])
        m9 = sb("m9", [P, NB, TS + 1])
        ones9 = sb("ones9", [P, NB, TS + 1])
        t4 = sb("t4", [P, 4, 2, LB])
        yin = sb("yin", [P, 2, 2, LB])
        yout = sb("yout", [P, 2, 2, 2, LB])
        xs = sb("xs", [P, 2, 4, 2, LB])
        flatten = lambda t, dims: t[:].rearrange(dims)
        bnat = flatten(yin, "p q b n -> p (q b n)")[:, 0:2 * ST * S5H].rearrange("p (c t h) -> p c t h", c=2, h=S5H)
        bt = flatten(yout, "p k q b n -> p (k q b n)")[:, 0:1024].rearrange("p (c t h) -> p c t h", c=4, h=S5H)
        cnat = flatten(t4, "p q b n -> p (q b n)")[:, 0:2 * FT * P].rearrange("p (c f k q) -> p c f k q", c=2, f=FT, k=2)
        rt = flatten(xs, "p c q b n -> p (c q b n)")[:, 0:ST * P].rearrange("p (t n) -> p t n", t=ST)
        small = flatten(xs, "p c q b n -> p (c q b n)")[0:ST, ST * P:2 * ST * P].rearrange("t (n q) -> t n q", q=P)
        lam, ab, pk = small[:, 0:2, :], small[:, 2:4, :], small[:, 4:9, :]
        th, ldm, turns, cosarg, den, s1, s2 = (small[:, n, :] for n in range(9, 16))
        e4 = sb("e4", [P, 2])
        carry = sb("carry", [P, 2])
        in9 = sb("in9", [P, 2, NB, TS + 1])
        out9 = sb("out9", [P, 2, NB, TS + 1])
        q4 = sb("q4", [P, 4, NB, TS])
        x9 = sb("x9", [P, 2, NB, TS])
        r4 = sb("r4", [P, 4, NB, TS])
        fin_p = sb("fin_p", [P, 2, ST])
        fin_s = sb("fin_s", [P, 2, NB, ST])
        fo_p = sb("fo_p", [ST, 2, P])
        fo_s = sb("fo_s", [P, 2, P])
        bu = [pb(f"bu{k}", [P, 2, 512]) for k in range(2)]
        bus = pb("bus", [P, 2, NS])
        y_ps = pb("y_ps", [P, 3, 512])

        ld = [sem(f"ld{n}") for n in range(11)]
        a_dt, a_th, a_mag, a_sin = sem("a_dt"), sem("a_th"), sem("a_mag"), sem("a_sin")
        pk_set, pkT, prm_set, bz_set, bzT, bbT_set = (sem(n) for n in ("pk_set", "pkT", "prm_set", "bz_set", "bzT", "bbT_set"))
        cT, cz_set, sT, s_set = sem("cT"), sem("cz_set"), sem("sT"), sem("s_set")
        staged, bu_done, bu_used, bus_done, bus_used = (sem(n) for n in ("staged", "bu_done", "bu_used", "bus_done", "bus_used"))
        x_ready, x_used, x9_ready, y_done, y_used = (sem(n) for n in ("x_ready", "x_used", "x9_ready", "y_done", "y_used"))
        fin_set, finT, fo_set, stored, ch_v = (sem(n) for n in ("fin_set", "finT", "fo_set", "stored", "ch_v"))
        scanned, scanned9, ch_g = sem("scanned"), sem("scanned9"), sem("ch_g")
        block = ctx.enter_context(nc.Block())

        @block.sync
        def _(sp):
            tile = lambda ap: ap.rearrange("z (t g) q -> (z t) (g q)", g=2)
            sp.dma_start(lam[:, 0, :], tile(d["s5_lam_re"])).then_inc(ld[0], 16)
            sp.dma_start(lam[:, 1, :], tile(d["s5_lam_im"])).then_inc(ld[1], 16)
            sp.dma_start(ldt[:], d["s5_log_dt"].rearrange("z (t g) -> (z t) g", g=2)).then_inc(ld[2], 16)
            for n, name in enumerate(("s5_b_re", "s5_b_im")):
                sp.dma_start(bnat[:, n, :, :], bass.AP(d[name].tensor, 0, [(S5H, P), (P * S5H, ST), (1, S5H)])).then_inc(ld[3 + n], 16)
            for n, name in enumerate(("s5_c_re", "s5_c_im")):
                c = d[name].rearrange("z g h q -> (z g h) q").rearrange("(f p) q -> p f q", p=P)
                for k in range(2):
                    sp.dma_start(cnat[:, n, :, k, :], c).then_inc(ld[5 + n], 16)
            sp.dma_start(dvec[:], d["s5_d"].rearrange("z (f p) -> p (z f)", p=P), allow_slow_non_contiguous=True).then_inc(ld[7], 16)
            for n, name in enumerate(("state_s5_re", "state_s5_im")):
                sp.dma_start(snat[:, n, :], d[name].rearrange("z b (t g) q -> (z b t) (g q)", g=2)).then_inc(ld[8 + n], 16)
            sp.wait_ge(fo_set, 4)
            for n, name in enumerate(("s5_re", "s5_im")):
                sp.dma_start(d[name + "_p"].rearrange("z b (t g) q -> (z b t) (g q)", g=2), fo_p[:, n, :]).then_inc(stored, 16)
                sp.dma_start(d[name + "_s"].rearrange("z b (t g) q -> (z b t) (g q)", g=2), fo_s[:, n, :]).then_inc(stored, 16)
            sp.wait_ge(stored, 64)

        @block.scalar
        def _(act):
            act.wait_ge(ld[2], 16)
            act.activation(dt[:], ldt[:], ACT.Exp).then_inc(a_dt, 1)
            act.wait_ge(a_th, 1)
            act.activation(pk[:, 0, :], ldm[:], ACT.Exp).then_inc(a_mag, 1)
            act.wait_ge(a_th, 2)
            act.activation(pk[:, 1, :], cosarg[:], ACT.Sin).then_inc(a_sin, 1)
            act.activation(pk[:, 2, :], th[:], ACT.Sin).then_inc(a_sin, 1)
            for s in range(ST):
                act.wait_ge(bzT, s + 1)
                act.activation(bbT[:, :, s, :], bu[s % 2][:, :, 0:P], ACT.Copy).then_inc(bbT_set, 1)
            act.wait_ge(sT, 1)
            act.activation(state[:].rearrange("p c b t -> p c (b t)"), y_ps[:, 0, 0:2 * P].rearrange("p (c n) -> p c n", c=2),
                           ACT.Copy).then_inc(s_set, 1)
            act.wait_ge(bbT_set, ST)
            act.wait_ge(cz_set, 4)
            act.wait_ge(prm_set, 1)

            def stage(i, first):
                if not first:
                    act.wait_ge(y_done, i)
                    act.wait_ge(y_used, i)
                act.activation(bbs[:], bbT[:, :, ds(SJ * i, SJ), :], ACT.Copy)
                act.activation(czs[:, 0:2], cz[:, :, ds(SJ * i, SJ), :, :].rearrange("p c j g h -> p c j (g h)"), ACT.Copy)
                act.activation(czs[:, 2], cz[:, 0, ds(SJ * i, SJ), :, :].rearrange("p j g h -> p j (g h)"), ACT.Copy, scale=-1.0)
                act.activation(pms[:], prm[:, :, ds(SJ * i, SJ)], ACT.Copy).then_inc(staged, 1)

            stage(0, True)
            with act.Fori(1, FT) as i:
                stage(i, False)

        @block.vector
        def _(dve):
            link = Chain(dve, ch_v)
            tt = dve.tensor_tensor
            for n in range(3):
                dve.wait_ge(ld[n], 16)
            dve.wait_ge(a_dt, 1)
            half = lambda ap: ap.rearrange("t (g q) -> t g q", g=2)
            dtb = dt[:].unsqueeze(2).to_broadcast([ST, 2, S5P])
            lr, li = lam[:, 0, :], lam[:, 1, :]
            link(tt(half(ldm[:]), half(lr), dtb, ALU.mult))
            dve.sem_inc(a_th, 1)
            link(tt(half(th[:]), half(li), dtb, ALU.mult))
            link(dve.tensor_scalar(turns[:], th[:], float(1 / (2 * np.pi)), ROUND, ALU.mult, ALU.add))
            link(dve.tensor_scalar(turns[:], turns[:], -ROUND, None, ALU.add))
            link(dve.scalar_tensor_tensor(th[:], turns[:], -TWO_PI_HI, th[:], ALU.mult, ALU.add))
            link(dve.scalar_tensor_tensor(th[:], turns[:], -TWO_PI_LO, th[:], ALU.mult, ALU.add))
            link(dve.tensor_scalar(th[:], th[:], NEARLY_PI, -NEARLY_PI, ALU.min, ALU.max))
            link(dve.scalar_tensor_tensor(cosarg[:], th[:], -1.0, th[:], ALU.mult, ALU.max))
            link(dve.tensor_scalar(cosarg[:], cosarg[:], -1.0, float(np.pi / 2), ALU.mult, ALU.add))
            dve.sem_inc(a_th, 1)
            dve.wait_ge(a_mag, 1)
            dve.wait_ge(a_sin, 2)
            link(tt(ab[:, 0, :], pk[:, 0, :], pk[:, 1, :], ALU.mult))
            link(tt(ab[:, 1, :], pk[:, 0, :], pk[:, 2, :], ALU.mult))
            link(tt(s1[:], lr, lr, ALU.mult))
            link(tt(s2[:], li, li, ALU.mult))
            link(tt(den[:], s1[:], s2[:], ALU.add))
            link(dve.reciprocal(den[:], den[:]))
            link(dve.tensor_scalar(ab[:, 0, :], ab[:, 0, :], -1.0, None, ALU.add))
            link(tt(s1[:], ab[:, 0, :], lr, ALU.mult))
            link(tt(s2[:], ab[:, 1, :], li, ALU.mult))
            link(tt(s1[:], s1[:], s2[:], ALU.add))
            link(tt(pk[:, 3, :], s1[:], den[:], ALU.mult))
            link(tt(s1[:], ab[:, 1, :], lr, ALU.mult))
            link(tt(s2[:], ab[:, 0, :], li, ALU.mult))
            link(tt(s1[:], s1[:], s2[:], ALU.subtract))
            link(tt(pk[:, 4, :], s1[:], den[:], ALU.mult))
            dve.sem_inc(pk_set, 1)
            dve.wait_ge(pkT, 1)
            link(dve.tensor_copy(prm[:], y_ps[:, 0, 0:5 * ST].rearrange("p (c t) -> p c t", c=5)))
            dve.sem_inc(prm_set, 1)
            dve.wait_ge(ld[3], 16)
            dve.wait_ge(ld[4], 16)
            fb = lambda n: prm[:, 3 + n, :].unsqueeze(2).to_broadcast([P, ST, S5H])
            link.put(tt(bt[:, 0], bnat[:, 0], fb(0), ALU.mult))
            link.put(tt(bt[:, 1], bnat[:, 1], fb(1), ALU.mult))
            link.put(tt(bt[:, 2], bnat[:, 1], fb(0), ALU.mult))
            link(tt(bt[:, 3], bnat[:, 0], fb(1), ALU.mult))
            link.put(tt(bt[:, 0], bt[:, 0], bt[:, 1], ALU.subtract))
            link(tt(bt[:, 2], bt[:, 2], bt[:, 3], ALU.add))
            for s in range(ST):
                if s:
                    dve.wait_ge(bzT, s)
                link(dve.memset(bz[:], 0.0))
                at = s % SJ * 2 * S5H
                for g in range(2):
                    link.put(dve.tensor_copy(bz[g * S5P:(g + 1) * S5P, :, at + g * S5H:at + (g + 1) * S5H],
                                             bt[g * S5P:(g + 1) * S5P, 0:4:2, s, :]))
                link.sync()
                dve.sem_inc(bz_set, 1)
            link(dve.memset(cz[:], 0.0))
            dve.wait_ge(cT, 1)
            for n in range(2):
                for g in range(2):
                    rows = slice(g * S5P, (g + 1) * S5P)
                    src = bu[n][rows, 0, :].rearrange("p (s g h) -> p s g h", g=2, h=S5H)[:, :, g, :]
                    dve.tensor_scalar(cz[rows, n, :, g, :], src, 1.0 - 2.0 * n, None, ALU.mult).then_inc(cz_set, 1)
            link(dve.tensor_copy(rot[:, 0, :, 0:1], prm[:, 1, :].unsqueeze(2)))
            link(dve.tensor_copy(rot[:, 1, :, 0:1], prm[:, 2, :].unsqueeze(2)))
            n = 1
            while n < LB:
                co, si = rot[:, 0, :, 0:n], rot[:, 1, :, 0:n]
                cn = rot[:, 0, :, n - 1:n].to_broadcast([P, ST, n])
                sn = rot[:, 1, :, n - 1:n].to_broadcast([P, ST, n])
                link.put(tt(rot[:, 0, :, n:2 * n], co, cn, ALU.mult))
                link(tt(rt[:, :, 0:n], si, sn, ALU.mult))
                link(tt(rot[:, 0, :, n:2 * n], rot[:, 0, :, n:2 * n], rt[:, :, 0:n], ALU.subtract))
                link.put(tt(rot[:, 1, :, n:2 * n], si, cn, ALU.mult))
                link(tt(rt[:, :, 0:n], co, sn, ALU.mult))
                link(tt(rot[:, 1, :, n:2 * n], rot[:, 1, :, n:2 * n], rt[:, :, 0:n], ALU.add))
                n *= 2
            link(dve.memset(ones9[:], 1.0))
            link(dve.memset(ones9[:, :, 0:1], 0.0))
            dve.wait_ge(ld[7], 16)
            dve.wait_ge(s_set, 1)
            link.restart()

            def rotated(o_re, o_im, re, im, co, si, tmp, release):
                link.put(tt(tmp[0], re, co, ALU.mult))
                link.put(tt(tmp[1], im, si, ALU.mult))
                link.put(tt(tmp[2], im, co, ALU.mult))
                link(tt(tmp[3], re, si, ALU.mult))
                release()
                link.put(tt(o_re, tmp[0], tmp[1], ALU.add))
                link(tt(o_im, tmp[2], tmp[3], ALU.subtract))

            with dve.Fori(0, FT) as i:
                dve.wait_ge(staged, i + 1)
                for j in range(SJ):
                    s = SJ * i + j
                    m = pms[:, 0, j:j + 1]
                    table = lambda c, n, reps: rot[:, c, ds(s, 1), 0:n].to_broadcast([P, reps, n])
                    link(dve.tensor_scalar(m_row[:], rot[:, 0, ds(s, 1), :].rearrange("p a n -> p (a n)"), 0.0, m, ALU.mult, ALU.add))
                    link(dve.memset(carry[:], 0.0))
                    end = [row(rot[:, c, ds(s, 1), LB - 1:LB]) for c in range(2)]
                    for c in range(2):
                        turn = 8 * i + 2 * j + c
                        dve.wait_ge(bu_done, turn + 1)
                        rotated(yin[:, 0], yin[:, 1], bu[c][:, 0, :].rearrange("p (b n) -> p b n", n=LB),
                                bu[c][:, 1, :].rearrange("p (b n) -> p b n", n=LB), table(0, LB, 2), table(1, LB, 2),
                                [t4[:, q] for q in range(4)], lambda: dve.sem_inc(bu_used, 1))
                        if j:
                            dve.wait_ge(x_ready, turn - 1)
                        for blk in range(2):
                            for q in range(2):
                                link.put(dve.tensor_tensor_scan(yout[:, c, q, blk, :], m_row[:], yin[:, q, blk, :],
                                                                carry[:, q:q + 1], ALU.mult, ALU.add))
                            link.sync()
                            ye = [yout[:, c, q, blk, LB - 1:LB] for q in range(2)]
                            link.put(tt(e4[:, 0:1], ye[1], end[1], ALU.mult))
                            link(tt(e4[:, 1:2], ye[1], end[0], ALU.mult))
                            link.put(dve.scalar_tensor_tensor(carry[:, 0:1], ye[0], end[0], e4[:, 0:1], ALU.mult, ALU.subtract))
                            link(dve.scalar_tensor_tensor(carry[:, 1:2], ye[0], end[1], e4[:, 1:2], ALU.mult, ALU.add))
                        dve.sem_inc(scanned, 1)
                    link(dve.tensor_copy(fin_p[:, :, ds(s, 1)], carry[:].unsqueeze(2)))
                    link(dve.tensor_scalar(m9[:], ones9[:], m, None, ALU.mult))
                    link(dve.tensor_copy(in9[:, :, :, 0:1], state[:, :, :, ds(s, 1)]))
                    dve.wait_ge(bus_done, s + 1)
                    b = bus[:].rearrange("p c (b t) -> p c b t", t=TS)
                    rotated(in9[:, 0, :, 1:TS + 1], in9[:, 1, :, 1:TS + 1], b[:, 0], b[:, 1], table(0, TS, NB), table(1, TS, NB),
                            [q4[:, q] for q in range(4)], lambda: dve.sem_inc(bus_used, 1))
                    flat = lambda ap: ap.rearrange("p b t -> p (b t)")
                    if j:
                        dve.wait_ge(x9_ready, s)
                    for q in range(2):
                        link.put(dve.tensor_tensor_scan(flat(out9[:, q]), flat(m9[:]), flat(in9[:, q]), 0.0, ALU.mult, ALU.add))
                    link.sync()
                    dve.sem_inc(scanned9, 1)
                dve.wait_ge(y_done, i + 1)
                for at, n, c in ((0, 512, 0), (512, 512, 1), (SEQ, NS, 2)):
                    link.put(dve.scalar_tensor_tensor(row(yT[:, ds(i, 1), at:at + n]), row(uT[:, ds(i, 1), at:at + n]),
                                                      row(dvec[:, ds(i, 1)].unsqueeze(2)), y_ps[:, c, 0:n], ALU.mult, ALU.add))
                link.sync()
                link.restart()
                dve.sem_inc(y_used, 1)
            dve.sem_inc(fin_set, 1)
            dve.wait_ge(finT, 1)
            for n in range(2):
                dve.tensor_copy(fo_p[:, n, :], y_ps[0:ST, 0, n * P:(n + 1) * P]).then_inc(fo_set, 1)
                dve.tensor_copy(fo_s[:, n, :], y_ps[:, 1, n * P:(n + 1) * P]).then_inc(fo_set, 1)

        @block.gpsimd
        def _(pool):
            link = Chain(pool, ch_g)
            tt = pool.tensor_tensor
            with pool.Fori(0, FT) as i:
                for j in range(SJ):
                    s = SJ * i + j
                    table = lambda c, n, reps: rot[:, c, ds(s, 1), 0:n].to_broadcast([P, reps, n])
                    for c in range(2):
                        turn = 8 * i + 2 * j + c
                        pool.wait_ge(scanned, turn + 1)
                        if j:
                            pool.wait_ge(x_used, turn - 1)
                        pool.nop(nofuse=True)
                        for n, (part, t) in enumerate(((0, 0), (1, 1), (0, 1), (1, 0))):
                            ins = tt(xs[:, c, n], yout[:, c, part], table(t, LB, 2), ALU.mult)
                        ins.then_inc(x_ready, 1)
                    pool.wait_ge(scanned9, s + 1)
                    pool.wait_ge(x_used, 8 * i + 2 * j + 1)
                    pool.nop(nofuse=True)
                    for n, (part, t) in enumerate(((0, 0), (1, 1), (0, 1), (1, 0))):
                        link.put(tt(r4[:, n], out9[:, part, :, 1:TS + 1], table(t, TS, NB), ALU.mult))
                    link.sync()
                    link.put(tt(x9[:, 0], r4[:, 0], r4[:, 1], ALU.subtract))
                    link(tt(x9[:, 1], r4[:, 2], r4[:, 3], ALU.add))
                    link(pool.tensor_copy(fin_s[:, :, :, ds(s, 1)], x9[:, :, :, TS - 1:TS]))
                    pool.sem_inc(x9_ready, 1)
                link.restart()

        @block.tensor
        def _(pe):
            pe.wait_ge(pk_set, 1)
            for n in range(5):
                ins = pe.transpose(y_ps[:, 0, n * ST:(n + 1) * ST], pk[:, n, :], ident[0:ST, 0:ST])
            ins.then_inc(pkT, 1)
            for s in range(ST):
                pe.wait_ge(bz_set, s + 1)
                if s > 1:
                    pe.wait_ge(bbT_set, s - 1)
                for n in range(2):
                    ins = pe.transpose(bu[s % 2][:, n, 0:P], bz[:, n, :], ident[:])
                ins.then_inc(bzT, 1)
            for n in range(2):
                pe.wait_ge(ld[5 + n], 32)
                pe.wait_ge(bbT_set, ST)
                for f in range(FT):
                    ins = pe.transpose(bu[n][:, 0, f * P:(f + 1) * P], cnat[:, n, f, :, :].rearrange("p k q -> p (k q)"), ident[:])
            ins.then_inc(cT, 1)
            pe.wait_ge(prm_set, 1)
            for n in range(2):
                pe.wait_ge(ld[8 + n], 16)
                ins = pe.transpose(y_ps[:, 0, n * P:(n + 1) * P], snat[:, n, :], ident[:])
            ins.then_inc(sT, 1)
            pe.wait_ge(s_set, 1)
            pe.wait_ge(cz_set, 4)

            def feature_tile(i, first):
                pe.wait_ge(staged, i + 1)

                def inputs(j, c):
                    if c < 2:
                        if not (first and j == 0):
                            pe.wait_ge(bu_used, 8 * i + 2 * j + c - 1)
                        for n in range(2):
                            ins = pe.matmul(bu[c][:, n, :], bbs[:, n, j, :], row(uT[:, ds(i, 1), c * 512:(c + 1) * 512]),
                                            start=True, stop=True)
                        ins.then_inc(bu_done, 1)
                    else:
                        if not (first and j == 0):
                            pe.wait_ge(bus_used, SJ * i + j)
                        for n in range(2):
                            ins = pe.matmul(bus[:, n, :], bbs[:, n, j, :], row(uT[:, ds(i, 1), SEQ:TOK]), start=True, stop=True)
                        ins.then_inc(bus_done, 1)

                for c in range(3):
                    inputs(0, c)
                for j in range(SJ):
                    if j + 1 < SJ:
                        inputs(j + 1, 0)
                    rows = slice(32 * j, 32 * j + 32)
                    for c in range(3):
                        if c < 2:
                            pe.wait_ge(x_ready, 8 * i + 2 * j + c + 1)
                        else:
                            pe.wait_ge(x9_ready, SJ * i + j + 1)
                        if not first and j == 0 and c == 0:
                            pe.wait_ge(y_used, i)
                        n = 512 if c < 2 else NS
                        if c < 2:
                            terms = [(q, xs[:, c, k, :, :].rearrange("p b n -> p (b n)")) for k, q in enumerate((0, 2, 1, 1))]
                        else:
                            terms = [(q, x9[:, q, :, :].rearrange("p b t -> p (b t)")) for q in range(2)]
                        for k, (q, x) in enumerate(terms):
                            ins = pe.matmul(y_ps[rows, c, 0:n], czs[:, q, j, :], x, start=(k == 0), stop=(k == len(terms) - 1))
                        if c < 2:
                            ins.then_inc(x_used, 1)
                        elif j == SJ - 1:
                            ins.then_inc(y_done, 1)
                        if c == 1 and j + 1 < SJ:
                            inputs(j + 1, 1)
                            inputs(j + 1, 2)

            feature_tile(0, True)
            with pe.Fori(1, FT) as i:
                feature_tile(i, False)
            pe.wait_ge(fin_set, 1)
            for n in range(2):
                pe.transpose(y_ps[0:ST, 0, n * P:(n + 1) * P], fin_p[:, n, :], ident[:])
                ins = pe.transpose(y_ps[:, 1, n * P:(n + 1) * P], fin_s[:, n, :, :].rearrange("p b t -> p (b t)"), ident[:])
            ins.then_inc(finT, 1)


def phase_gelu(nc, yT):
    with ExitStack() as ctx:
        sem = ctx.enter_context(Semaphores(nc, "ge_"))
        sq = ctx.enter_context(nc.sbuf_tensor("ge_sq", [P, FT, TOK], F32))
        squared, inner, tanhed, done = sem("squared"), sem("inner"), sem("tanhed"), sem("done")
        chain, half = sem("chain"), sem("half")
        block = ctx.enter_context(nc.Block())

        @block.scalar
        def _(act):
            for f in range(FT):
                act.activation(sq[:, f, :], yT[:, f, 0:TOK], ACT.Square).then_inc(squared, 1)
            for f in range(FT):
                act.wait_ge(inner, f + 1)
                act.activation(sq[:, f, :], sq[:, f, :], ACT.Tanh, scale=C_TANH).then_inc(tanhed, 1)
            for f in range(FT):
                act.wait_ge(done, f + 1)
                act.activation(yT[:, f, 0:TOK], yT[:, f, 0:TOK], ACT.Copy, scale=0.5).then_inc(half, 1)

        @block.vector
        def _(dve):
            link = Chain(dve, chain)
            for f in range(FT):
                dve.wait_ge(squared, f + 1)
                link(dve.tensor_scalar(sq[:, f, :], sq[:, f, :], C_CUBE, 1.0, ALU.mult, ALU.add))
                dve.tensor_tensor(sq[:, f, :], sq[:, f, :], yT[:, f, 0:TOK], ALU.mult).then_inc(inner, 1)
            for f in range(FT):
                dve.wait_ge(tanhed, f + 1)
                dve.scalar_tensor_tensor(yT[:, f, 0:TOK], sq[:, f, :], 1.0, yT[:, f, 0:TOK], ALU.add, ALU.mult).then_inc(done, 1)


LP = CL // 2
NC_S = (PAST + TS - CL) // CS + 1
NC_P = (SEQ - CL) // CS + 1
NCP = 2 * P
GT = NKV * TS
MR = NH * TS


def phase_compress(nc, d, r):
    with ExitStack() as ctx:
        sb = lambda name, shape, dt=F32: ctx.enter_context(nc.sbuf_tensor("c_" + name, shape, dt))
        pb = lambda name, shape: ctx.enter_context(nc.psum_tensor("c_" + name + "_ps", shape, F32))
        sem = ctx.enter_context(Semaphores(nc, "c_"))
        ident, qkT, qbd, g_rows, osum, sel_bias = (r[n] for n in ("ident", "qkT", "qbd", "g_rows", "osum", "sel_bias"))
        w1 = sb("w1", [P, 2, LP, CH])
        w2 = sb("w2", [P, 2, DH])
        pe_nat = sb("pe_nat", [LP, 2, P])
        peT = sb("peT", [P, 2, LP])
        hbias = sb("hbias", [P, 2])
        pages = sb("pages", [P, 2 * NB], I32)
        in_page = sb("in_page", [P, 1], I32)
        rows_of = sb("rows_of", [P, 2 * NB], I32)
        row_now = sb("row_now", [P, 4], I32)
        gsum = sb("gsum", [MR, GT])
        gspread = sb("gspread", [GT, MR])
        x = [sb(f"x{s}", [P, CS * KVW]) for s in range(4)]
        xT = [sb(f"xT{v}", [P, CS // 2, 2, NCP]) for v in range(2)]
        xb = [sb(f"xb{v}", [P, 2, NC_S]) for v in range(2)]
        sq = [sb(f"sq{v}", [P, 2, NC_S]) for v in range(2)]
        g = [sb(f"g{v}", [P, 2, NC_S]) for v in range(2)]
        kc = sb("kc", [P, NC_S])
        vc = sb("vc", [P, 2, KVW])
        qs = sb("qs", [P, MR])
        prob = sb("prob", [MR, NC_S])
        stat = sb("stat", [MR, 4])
        pT = sb("pT", [P, 2, MR])
        pg = sb("pg", [GT, 4 * NSLC + 1])
        imp = sb("imp", [GT, NSLC - 1])
        score = sb("score", [GT, NSLC])
        top = sb("top", [GT, 8])
        t_ps = [pb(f"t{k}", [P, 4, P]) for k in range(2)]
        h_ps = [pb(f"h{v}", [P, 512]) for v in range(2)]
        w2_ps = pb("w2", [P, 512])
        s_ps = pb("s", [P, 512])
        pT_ps = pb("pT", [P, 2, MR])
        o_ps = pb("o", [MR, P])

        w_ld, k_ld, pt_ld, g_ld = sem("w_ld"), sem("k_ld"), sem("pt_ld"), sem("g_ld")
        x_ld = [sem(f"x_ld{s}") for s in range(4)]
        peT_done, peT_set, hb_done, hb_set = (sem(n) for n in ("peT_done", "peT_set", "hb_done", "hb_set"))
        rows_set, row_set, ch_p, ch_v, zeroed = (sem(n) for n in ("rows_set", "row_set", "ch_p", "ch_v", "zeroed"))
        x_used, t_done, t_dve, t_act = (sem(n) for n in ("x_used", "t_done", "t_dve", "t_act"))
        h_done, h_read, inner, tanhed, g_rdy = (sem(n) for n in ("h_done", "h_read", "inner", "tanhed", "g_rdy"))
        kc_done, vc_done, kc_set, vc_set = (sem(n) for n in ("kc_done", "vc_done", "kc_set", "vc_set"))
        q_set, s_done, max_set, exp_done, p_set = (sem(n) for n in ("q_set", "s_done", "max_set", "exp_done", "p_set"))
        pt_done, pt_set, sel_set, pv_done, o_set = (sem(n) for n in ("pt_done", "pt_set", "sel_set", "pv_done", "o_set"))
        sel_used, prompt_ld = sem("sel_used"), [sem("prompt_ld0"), sem("prompt_ld1")]
        block = ctx.enter_context(nc.Block())
        PR = NB

        first = lambda b: isinstance(b, int) and b == 0
        prompt = lambda b: isinstance(b, int) and b == PR

        def sequences(eng, step):
            step(0)
            with eng.Fori(1, NB) as b:
                step(b)
            step(PR)

        def fills(b, v):
            return 16 * b + (4 if prompt(b) else 8) * v

        def half_fills(b, v):
            return 8 * b + (2 if prompt(b) else 4) * v

        @block.sync
        def _(sp):
            for n, (a, b) in enumerate((("cmp_wk1", "cmp_wk2"), ("cmp_wv1", "cmp_wv2"))):
                sp.dma_start(w1[:, n, :, :], bass.AP(d[a].tensor, 0, [(CH, P), (P * CH, LP), (1, CH)])).then_inc(w_ld, 16)
                sp.dma_start(w2[:, n, :], d[b].rearrange("z f c -> (z f) c")).then_inc(w_ld, 16)
            sp.dma_start(pe_nat[:, 0, :], d["cmp_pe_k"].rearrange("z (c l) q -> (z c) (l q)", l=2)).then_inc(k_ld, 16)
            sp.dma_start(pe_nat[:, 1, :], d["cmp_pe_v"].rearrange("z (c l) q -> (z c) (l q)", l=2)).then_inc(k_ld, 16)
            sp.dma_start(gsum[:], d["gsum"]).then_inc(k_ld, 16)
            sp.dma_start(gspread[:], d["gspread"]).then_inc(k_ld, 16)
            for h in range(NH):
                sp.dma_start(g_rows[h * TS:(h + 1) * TS, :, :],
                             d["g_new"].rearrange("(b t) (h c) -> t b h c", t=TS, h=NH)[:, :, h, :]).then_inc(g_ld, 16)
            for v, name in ((0, "k_cmp_p"), (1, "v_cmp_p")):
                sp.wait_ge(x_used, 4 * NB - 3 + 2 * v)
                sp.dma_start(x[2 * v][0:SEQ // CS, :],
                             d[name].rearrange("z a (n r) h c -> (z a n) (r h c)", r=CS)).then_inc(prompt_ld[v], 16)

        @block.gpsimd
        def _(pool):
            link = Chain(pool, ch_p)
            for q in range(PAGE // CS):
                pool.dma_start(pages[q::PAGE // CS, :], bass.AP(d["page_table"].tensor, 0, [(1, P * CS // PAGE), (P * CS // PAGE, 2 * NB)]),
                               allow_slow_non_contiguous=True).then_inc(pt_ld, 16)
            pool.dma_start(in_page[:], d["in_page"]).then_inc(pt_ld, 16)
            pool.wait_ge(pt_ld, 16 * (PAGE // CS + 1))
            link(pool.tensor_scalar(rows_of[:], pages[:], PAGE // CS, None, ALU.mult))
            link(pool.tensor_tensor(rows_of[:], rows_of[:], in_page[:].to_broadcast([P, 2 * NB]), ALU.add))
            link.restart()

            def gather(b):
                for s in range(4):
                    if not first(b):
                        pool.wait_ge(x_used, 4 * b + s - 3)
                    pool.nop(nofuse=True)
                    link(pool.tensor_copy(row_now[:, s:s + 1], rows_of[:, ds(2 * b + s % 2, 1)]))
                    link.restart()
                    table = d["cache_k_cmp" if s < 2 else "cache_v_cmp"].rearrange("z n (q r) h c -> (z n q) (r h c)", r=CS)
                    pool.indirect_dma_start(x[s][:], None, table, bass.IndirectOffsetOnAxis(ap=row_now[:, s:s + 1], axis=0)
                                            ).then_inc(x_ld[s], 16)

            gather(0)
            with pool.Fori(1, NB) as b:
                gather(b)

        @block.tensor
        def _(pe):
            pe.wait_ge(k_ld, 64)
            pe.wait_ge(w_ld, 64)
            for v in range(2):
                ins = pe.transpose(t_ps[0][:, v, 0:LP], pe_nat[:, v, :], ident[0:LP, 0:LP])
            ins.then_inc(peT_done, 1)
            pe.wait_ge(peT_set, 1)
            for v in range(2):
                for c in range(LP):
                    ins = pe.matmul(w2_ps[:, v:v + 1], w1[:, v, c, :], peT[:, v, c:c + 1], start=(c == 0), stop=(c == LP - 1))
            ins.then_inc(hb_done, 1)
            pe.wait_ge(hb_set, 1)

            def transposes(b, v):
                halves, rows = (1, SEQ // CS) if prompt(b) else (2, P)
                for i in range(halves):
                    if prompt(b):
                        pe.wait_ge(prompt_ld[v], 16)
                    else:
                        pe.wait_ge(x_ld[2 * v + i], 16 * b + 16)
                    for q in range(4):
                        if not (first(b) and v == 0 and i == 0 and q < 2):
                            pe.wait_ge(t_act if q % 2 else t_dve, half_fills(b, v) + 2 * i + q // 2)
                        for l in range(4):
                            at = (4 * q + l) * KVW
                            ins = pe.transpose(t_ps[q % 2][:, l, 0:rows], x[2 * v + i][0:rows, at:at + KVW], ident[0:rows, 0:rows])
                        ins.then_inc(t_done, 1)
                    pe.wait_ge(t_done, fills(b, v) + 4 * i + 4)
                    pe.sem_inc(x_used, 1)

            def hidden(b, v):
                n = half_fills(b, v) + (2 if prompt(b) else 4)
                pe.wait_ge(t_dve, n)
                pe.wait_ge(t_act, n)
                if not first(b):
                    pe.wait_ge(h_read, 2 * b + v - 1)
                m = NC_P if prompt(b) else NC_S
                out = h_ps[v][:, 0:2 * m].rearrange("p (h n) -> p h n", h=2)
                for c in range(LP):
                    ins = pe.matmul(out, w1[:, v, c, :], xT[v][:, c % (LP // 2), :, c // (LP // 2):c // (LP // 2) + m],
                                    start=(c == 0), stop=(c == LP - 1))
                ins.then_inc(h_done, 1)

            def keys(b):
                m = NC_P if prompt(b) else NC_S
                pe.wait_ge(g_rdy, 2 * b + 1)
                if not first(b):
                    pe.wait_ge(vc_set, b)
                for h in range(NKV):
                    ins = pe.matmul(w2_ps[h * DH:(h + 1) * DH, 0:m], w2[:, 0, :], g[0][:, h, 0:m], start=True, stop=True)
                ins.then_inc(kc_done, 1)

            def values(b):
                m = NC_P if prompt(b) else NC_S
                pe.wait_ge(g_rdy, 2 * b + 2)
                pe.wait_ge(kc_set, b + 1)
                for c in range(1 if prompt(b) else 2):
                    n = min(P, m - c * P)
                    for h in range(NKV):
                        at = 256 + c * KVW + h * DH
                        ins = pe.matmul(w2_ps[0:n, at:at + DH], g[1][:, h, c * P:c * P + n], w2[:, 1, :], start=True, stop=True)
                ins.then_inc(vc_done, 1)

            def scores(b):
                pe.wait_ge(kc_set, b + 1)
                pe.wait_ge(q_set, b + 1)
                if not first(b):
                    pe.wait_ge(sel_used, b)
                pe.matmul(s_ps[0:MR, 0:NC_S], qs[:], kc[:], start=True, stop=True).then_inc(s_done, 1)

            def grouped(b):
                pe.wait_ge(p_set, b + 1)
                if not first(b):
                    pe.wait_ge(pt_set, b)
                pe.nop(nofuse=True)
                pe.matmul(s_ps[0:GT, 256:256 + NC_S], gsum[:], prob[:], start=True, stop=True)
                for c in range(2):
                    n = min(P, NC_S - c * P)
                    ins = pe.transpose(pT_ps[0:n, c, :], prob[:, c * P:c * P + n], ident[0:MR, 0:MR])
                ins.then_inc(pt_done, 1)

            def attend(b):
                pe.wait_ge(pt_set, b + 1)
                pe.wait_ge(vc_set, b + 1)
                if not first(b):
                    pe.wait_ge(o_set, b)
                for c in range(2):
                    n = min(P, NC_S - c * P)
                    ins = pe.matmul(o_ps[:], pT[0:n, c, :], vc[0:n, c, :], start=(c == 0), stop=(c == 1))
                ins.then_inc(pv_done, 1)
                pe.wait_ge(sel_set, b + 1)
                pe.matmul(s_ps[0:MR, 0:NSLC], gspread[:], score[:], start=True, stop=True).then_inc(pv_done, 1)

            def step(b):
                transposes(b, 0)
                hidden(b, 0)
                if not first(b):
                    values(b - 1)
                    scores(b - 1)
                transposes(b, 1)
                if not first(b):
                    grouped(b - 1)
                hidden(b, 1)
                keys(b)
                if not first(b):
                    attend(b - 1)

            sequences(pe, step)
            values(PR)

        def take(eng, copy, done, b, v):
            halves, rows = (1, SEQ // CS) if prompt(b) else (2, P)
            if not first(b):
                eng.wait_ge(h_done, 2 * b + v - 1)
            for i in range(halves):
                for q in range(1 if done is t_act else 0, 4, 2):
                    eng.wait_ge(t_done, fills(b, v) + 4 * i + q + 1)
                    src = t_ps[q % 2][:].rearrange("p (c l) n -> p c l n", l=2)
                    for h in range(NKV):
                        for l in range(2):
                            ins = copy(xT[v][l * DH:(l + 1) * DH, 2 * q:2 * q + 2, h, i * P:i * P + rows],
                                       src[h * DH:(h + 1) * DH, :, l, 0:rows])
                    ins.then_inc(done, 1)

        @block.scalar
        def _(act):
            copy = lambda out, in_: act.activation(out, in_, ACT.Copy)
            act.wait_ge(peT_done, 1)
            act.activation(peT[:], t_ps[0][:, 0:2, 0:LP], ACT.Copy).then_inc(peT_set, 1)
            act.wait_ge(hb_done, 1)
            act.activation(hbias[:], w2_ps[:, 0:2], ACT.Copy).then_inc(hb_set, 1)
            act.wait_ge(hb_set, 1)

            def gelu_in(b, v):
                m = NC_P if prompt(b) else NC_S
                act.wait_ge(h_done, 2 * b + v + 1)
                if not first(b):
                    act.wait_ge(g_rdy, 2 * b + v - 1)
                out = h_ps[v][:, 0:2 * m].rearrange("p (h n) -> p h n", h=2)
                act.activation(xb[v][:, :, 0:m], out, ACT.Identity, bias=hbias[:, v:v + 1])
                act.activation(sq[v][:, :, 0:m], out, ACT.Square, bias=hbias[:, v:v + 1]).then_inc(h_read, 1)

            def gelu_tanh(b, v):
                m = NC_P if prompt(b) else NC_S
                act.wait_ge(inner, 2 * b + v + 1)
                act.activation(sq[v][:, :, 0:m], sq[v][:, :, 0:m], ACT.Tanh, scale=C_TANH).then_inc(tanhed, 1)

            def take_values(b):
                act.wait_ge(vc_done, b + 1)
                if prompt(b):
                    act.activation(r["vc_p"][:], w2_ps[0:NC_P, 256:256 + KVW], ACT.Copy, scale=0.5).then_inc(vc_set, 1)
                    return
                if not first(b):
                    act.wait_ge(o_set, b)
                for c in range(2):
                    n = min(P, NC_S - c * P)
                    ins = act.activation(vc[0:n, c, :], w2_ps[0:n, 256 + c * KVW:256 + (c + 1) * KVW], ACT.Copy, scale=0.5)
                ins.then_inc(vc_set, 1)

            def exponentials(b):
                act.wait_ge(max_set, b + 1)
                if not first(b):
                    act.wait_ge(pt_done, b)
                act.activation(prob[:], s_ps[0:MR, 0:NC_S], ACT.Exp, bias=stat[:, 0:1],
                               accum_out=stat[:, 1:2]).then_inc(exp_done, 1)

            def take_keys(b):
                act.wait_ge(kc_done, b + 1)
                if prompt(b):
                    act.activation(r["kc_p"][:], w2_ps[:, 0:NC_P], ACT.Copy, scale=0.5).then_inc(kc_set, 1)
                    return
                if not first(b):
                    act.wait_ge(s_done, b)
                act.activation(kc[:], w2_ps[:, 0:NC_S], ACT.Copy, scale=0.5).then_inc(kc_set, 1)

            def step(b):
                if not first(b):
                    gelu_in(b - 1, 1)
                take(act, copy, t_act, b, 0)
                if not first(b):
                    gelu_tanh(b - 1, 1)
                gelu_in(b, 0)
                if not first(b):
                    take_values(b - 1)
                    exponentials(b - 1)
                take(act, copy, t_act, b, 1)
                gelu_tanh(b, 0)
                take_keys(b)

            sequences(act, step)
            gelu_in(PR, 1)
            gelu_tanh(PR, 1)
            take_values(PR)

        @block.vector
        def _(dve):
            link = Chain(dve, ch_v)
            copy = dve.tensor_copy
            tt = dve.tensor_tensor
            link(dve.memset(qbd[:], 0.0))
            for j in range(NG):
                for gg in range(NKV):
                    rows = slice(gg * DH, (gg + 1) * DH)
                    at = (gg * NG + j) * TS
                    link.put(copy(qbd[rows, 0:NB, at:at + TS], qkT[rows, j, SEQ:TOK].rearrange("p (b t) -> p b t", t=TS)))
            link.sync()
            link.put(dve.memset(pg[:], 0.0))
            link(copy(qs[:], qbd[:, 0, :]))
            dve.sem_inc(q_set, 1)
            dve.wait_ge(g_ld, 16 * NH)
            link.restart()

            def gelu_inner(b, v):
                m = NC_P if prompt(b) else NC_S
                dve.wait_ge(h_read, 2 * b + v + 1)
                s, xx = sq[v][:, :, 0:m], xb[v][:, :, 0:m]
                link(dve.tensor_scalar(s, s, C_CUBE, 1.0, ALU.mult, ALU.add))
                link(tt(s, s, xx, ALU.mult))
                dve.sem_inc(inner, 1)

            def gelu_out(b, v):
                m = NC_P if prompt(b) else NC_S
                dve.wait_ge(tanhed, 2 * b + v + 1)
                if not first(b):
                    dve.wait_ge(vc_done if v else kc_done, b)
                s, xx = sq[v][:, :, 0:m], xb[v][:, :, 0:m]
                dve.scalar_tensor_tensor(g[v][:, :, 0:m], s, 1.0, xx, ALU.add, ALU.mult).then_inc(g_rdy, 1)

            def softmax(b):
                dve.wait_ge(s_done, b + 1)
                link.put(copy(qs[:], row(qbd[:, ds(b + 1, 1), :])))
                link(dve.tensor_reduce(stat[:, 0:1], s_ps[0:MR, 0:NC_S], X, ALU.max, negate=True))
                dve.sem_inc(max_set, 1)
                dve.sem_inc(q_set, 1)
                dve.wait_ge(exp_done, b + 1)
                link(dve.tensor_scalar(stat[:, 2:3], stat[:, 1:2], 1e-30, None, ALU.max))
                link(dve.reciprocal(stat[:, 2:3], stat[:, 2:3]))
                link(dve.tensor_scalar(prob[:], prob[:], stat[:, 2:3], None, ALU.mult))
                dve.sem_inc(p_set, 1)

            def select(b):
                dve.wait_ge(pt_done, b + 1)
                for c in range(2):
                    n = min(P, NC_S - c * P)
                    link.put(copy(pT[0:n, c, :], pT_ps[0:n, c, :]))
                link.sync()
                dve.sem_inc(pt_set, 1)
                link(copy(pg[:, 1:1 + NC_S], s_ps[0:GT, 256:256 + NC_S]))
                part = lambda k: pg[:, k:k + 4 * (NSLC - 1)].rearrange("p (j f) -> p j f", f=4)[:, :, 0]
                link(tt(imp[:], part(0), part(4), ALU.add))
                link(dve.scalar_tensor_tensor(imp[:], imp[:], 0.5, part(1), ALU.mult, ALU.add))
                link(tt(imp[:], imp[:], part(2), ALU.add))
                link(tt(imp[:], imp[:], part(3), ALU.add))
                if not first(b):
                    dve.wait_ge(pv_done, 2 * b)
                link(dve.memset(score[:], 1e9))
                link(copy(score[:, 1:NSLC - 2], imp[:, 1:NSLC - 2]))
                for _ in range(TOPK // 8):
                    link(dve.max(top[:], score[:]))
                    link(dve.match_replace(score[:], top[:], score[:], -1.0))
                link(dve.tensor_scalar(score[:], score[:], 0.0, None, ALU.is_lt))
                dve.sem_inc(sel_set, 1)

            def gate(b):
                dve.wait_ge(pv_done, 2 * b + 1)
                for gg in range(NKV):
                    rows = slice(gg * MR // 2, (gg + 1) * MR // 2)
                    link.put(dve.tensor_scalar(row(osum[rows, ds(b, 1), :]), o_ps[rows, gg * DH:(gg + 1) * DH],
                                               row(g_rows[rows, ds(b, 1), 0:1]), None, ALU.mult))
                link.sync()
                dve.sem_inc(o_set, 1)
                dve.wait_ge(pv_done, 2 * b + 2)
                link(dve.tensor_scalar(row(sel_bias[:, ds(b, 1), :]), s_ps[0:MR, 0:NSLC], -NEG, NEG, ALU.mult, ALU.add))
                dve.sem_inc(sel_used, 1)

            def step(b):
                take(dve, copy, t_dve, b, 0)
                if not first(b):
                    gelu_inner(b - 1, 1)
                    gelu_out(b - 1, 1)
                    softmax(b - 1)
                take(dve, copy, t_dve, b, 1)
                gelu_inner(b, 0)
                gelu_out(b, 0)
                if not first(b):
                    select(b - 1)
                    gate(b - 1)
                link.restart()

            sequences(dve, step)
            gelu_inner(PR, 1)
            gelu_out(PR, 1)


KCH = 2 * CS * KVW // 512
CH_B = KCH + 1
PAST_T, WIN_T = PAST // P, WIN // P
NEW_S = PAST
WIN_0 = NEW_S + TS
NEW_W = WIN_0 + WIN
SCOLS = NEW_W + TS
PG = 5


def phase_sampled(nc, d, r):
    with ExitStack() as ctx:
        sb = lambda name, shape, dt=F32: ctx.enter_context(nc.sbuf_tensor("a_" + name, shape, dt))
        pb = lambda name, shape: ctx.enter_context(nc.psum_tensor("a_" + name + "_ps", shape, F32))
        sem = ctx.enter_context(Semaphores(nc, "a_"))
        ident, qkT, qbd, g_rows, osum, sel_bias, oT = (r[n] for n in ("ident", "qkT", "qbd", "g_rows", "osum", "sel_bias", "oTs"))
        rows_of, pages, in_page = (sb(n, s, I32) for n, s in (("rows_of", [P, 2 * NB]), ("pages", [P, 2 * NB]), ("in_page", [P, 1])))
        row_now = sb("row_now", [P, 4], I32)
        kx = [sb(f"kx{i}", [P, CS * KVW]) for i in range(2)]
        vx = [sb(f"vx{i}", [P, CS * KVW]) for i in range(2)]
        kwx = sb("kwx", [P, WIN_T, KVW])
        vwx = sb("vwx", [P, WIN_T, KVW])
        vn = sb("vn", [P, NB, 2, KVW])
        win_mask = sb("win_mask", [MR, WIN])
        new_mask = sb("new_mask", [MR, TS])
        kT = [sb(f"kT{k}", [P, 512]) for k in range(2)]
        qs = sb("qs", [P, MR])
        s_all = sb("s_all", [MR, SCOLS])
        prob = sb("prob", [MR, SCOLS])
        pT = sb("pT", [P, PAST_T + WIN_T, MR])
        pTn = sb("pTn", [P, 2, MR])
        stat = sb("stat", [MR, 8])
        odup = sb("odup", [MR, NB, 2, DH])
        t_ps = [pb(f"t{k}", [P, 512]) for k in range(2)]
        s_ps = [pb(f"s{k}", [MR, 512]) for k in range(2)]
        p_ps = [pb(f"p{k}", [P, 8, MR]) for k in range(2)]
        new_ps = pb("new", [MR, 2, TS])
        o_ps = pb("o", [MR, 2, KVW])

        pt_ld, m_ld, kw_ld, vw_ld, rows_set, row_set = (sem(n) for n in ("pt_ld", "m_ld", "kw_ld", "vw_ld", "rows_set", "row_set"))
        k_ld, v_ld = [sem("k_ld0"), sem("k_ld1")], [sem("v_ld0"), sem("v_ld1")]
        t_done, qk_done, s_added, new_done, new_added = (sem(n) for n in ("t_done", "qk_done", "s_added", "new_done", "new_added"))
        kt_set = [sem("kt_set0"), sem("kt_set1")]
        q_set, max_set, exp_done, pt_done, pv_done, o_set = (sem(n) for n in ("q_set", "max_set", "exp_done", "pt_done", "pv_done", "o_set"))
        pt_set = [sem("pt_set0"), sem("pt_set1")]
        zeroed = sem("zeroed")
        dup_set, oT_done, oT_set, ch_v, ch_p = (sem(n) for n in ("dup_set", "oT_done", "oT_set", "ch_v", "ch_p"))
        block = ctx.enter_context(nc.Block())
        first = lambda b: isinstance(b, int) and b == 0
        end = lambda b: isinstance(b, int) and b == NB

        def sequences(eng, step):
            step(0)
            with eng.Fori(1, NB) as b:
                step(b)
            step(NB)

        def uses(b, c):
            return (4 if c % 2 else 5) * b + c // 2

        def before(b, c):
            return CH_B * b + (c - 1 if c >= 2 else -c)

        def p_uses(b, u):
            return (2 if u % 2 else 3) * b + u // 2

        @block.sync
        def _(sp):
            sp.dma_start(win_mask[:], d["win_mask"]).then_inc(m_ld, 16)
            sp.dma_start(new_mask[:], d["new_mask"]).then_inc(m_ld, 16)
            sp.wait_ge(zeroed, 1)
            sp.dma_start(vn[0:TS], d["v_new"].rearrange("(b t) (c w) -> t b c w", t=TS, c=2)).then_inc(m_ld, 16)

            def load(name, dst, b, s):
                src = d[name].rearrange("z b (p r) h c -> (z b) p (r h c)", r=WIN_T)
                at = src[b] if isinstance(b, int) else src[ds(b, 1)].rearrange("b p n -> (b p) n")
                sp.dma_start(dst[:].rearrange("p r w -> p (r w)"), at).then_inc(s, 16)

            load("state_k_win", kwx, 0, kw_ld)
            load("state_v_win", vwx, 0, vw_ld)
            with sp.Fori(1, NB) as b:
                sp.wait_ge(t_done, CH_B * b)
                load("state_k_win", kwx, b, kw_ld)
                sp.wait_ge(pv_done, PG * b)
                load("state_v_win", vwx, b, vw_ld)

        @block.gpsimd
        def _(pool):
            link = Chain(pool, ch_p)
            for q in range(PAGE // CS):
                pool.dma_start(pages[q::PAGE // CS, :], bass.AP(d["page_table"].tensor, 0, [(1, P * CS // PAGE), (P * CS // PAGE, 2 * NB)]),
                               allow_slow_non_contiguous=True).then_inc(pt_ld, 16)
            pool.dma_start(in_page[:], d["in_page"]).then_inc(pt_ld, 16)
            pool.wait_ge(pt_ld, 16 * (PAGE // CS + 1))
            link(pool.tensor_scalar(rows_of[:], pages[:], PAGE // CS, None, ALU.mult))
            link(pool.tensor_tensor(rows_of[:], rows_of[:], in_page[:].to_broadcast([P, 2 * NB]), ALU.add))
            link.restart()

            def gather(b):
                for s in range(4):
                    if not first(b):
                        if s < 2:
                            pool.wait_ge(t_done, CH_B * (b - 1) + KCH // 2 * (s + 1))
                        else:
                            pool.wait_ge(pv_done, PG * (b - 1) + 2 * (s - 1))
                    pool.nop(nofuse=True)
                    link(pool.tensor_copy(row_now[:, s:s + 1], rows_of[:, ds(2 * b + s % 2, 1)]))
                    link.restart()
                    table = d["cache_k_slc" if s < 2 else "cache_v_slc"].rearrange("z n (q r) h c -> (z n q) (r h c)", r=CS)
                    pool.indirect_dma_start((kx if s < 2 else vx)[s % 2][:], None, table,
                                            bass.IndirectOffsetOnAxis(ap=row_now[:, s:s + 1], axis=0)
                                            ).then_inc((k_ld if s < 2 else v_ld)[s % 2], 16)

            gather(0)
            with pool.Fori(1, NB) as b:
                gather(b)

        @block.tensor
        def _(pe):
            def transposes(b, c):
                if c < KCH:
                    i = c // (KCH // 2)
                    if c % (KCH // 2) == 0:
                        pe.wait_ge(k_ld[i], 16 * b + 16)
                    src = [kx[i][:, (4 * c + l) % CS * KVW:((4 * c + l) % CS + 1) * KVW] for l in range(4)]
                else:
                    pe.wait_ge(kw_ld, 16 * b + 16)
                    src = [kwx[:, l, :] for l in range(4)]
                if not (first(b) and c < 2):
                    pe.wait_ge(kt_set[c % 2], uses(b, c))
                for l in range(4):
                    ins = pe.transpose(t_ps[c % 2][:, l * P:(l + 1) * P], src[l], ident[:])
                ins.then_inc(t_done, 1)

            def scores(b, c):
                pe.wait_ge(kt_set[c % 2], uses(b, c) + 1)
                if c == 0:
                    pe.wait_ge(q_set, b + 1)
                if not (first(b) and c < 2):
                    pe.wait_ge(s_added, before(b, c))
                pe.matmul(s_ps[c % 2][:], qs[:], kT[c % 2][:], start=True, stop=True).then_inc(qk_done, 1)

            def new_scores(b):
                if not first(b):
                    pe.wait_ge(new_added, b)
                for n in range(2):
                    ins = pe.matmul(new_ps[:, n, :], qs[:], row(qkT[:, NG + n:NG + n + 1, ds(SEQ + TS * b, TS)]), start=True, stop=True)
                ins.then_inc(new_done, 1)

            def prob_transposes(b, u):
                if u == 0:
                    pe.wait_ge(exp_done, b + 1)
                if not (first(b) and u < 2):
                    pe.wait_ge(pt_set[u % 2], p_uses(b, u))
                pe.nop(nofuse=True)
                if u < 4:
                    for n in range(8):
                        at = (8 * u + n) * P
                        ins = pe.transpose(p_ps[u % 2][:, n, :], prob[:, at:at + P], ident[0:MR, 0:MR])
                else:
                    for n in range(WIN_T):
                        pe.transpose(p_ps[0][:, n, :], prob[:, WIN_0 + n * P:WIN_0 + (n + 1) * P], ident[0:MR, 0:MR])
                    for n, at in enumerate((NEW_S, NEW_W)):
                        ins = pe.transpose(p_ps[0][0:TS, WIN_T + n, :], prob[:, at:at + TS], ident[0:MR, 0:MR])
                ins.then_inc(pt_done, 1)

            def values(b, u):
                pe.wait_ge(pt_set[u % 2], p_uses(b, u) + 1)
                if u == 0 and not first(b):
                    pe.wait_ge(o_set, b)
                if u < 4:
                    if u % 2 == 0:
                        pe.wait_ge(v_ld[u // 2], 16 * b + 16)
                    for n in range(8):
                        t = 8 * u + n
                        ins = pe.matmul(o_ps[:, 0, :], pT[:, t, :], vx[u // 2][:, t % CS * KVW:(t % CS + 1) * KVW],
                                        start=(t == 0), stop=False)
                else:
                    pe.matmul(o_ps[:, 0, :], pTn[:, 0, :], row(vn[:, ds(b, 1), 0, :]), start=False, stop=True)
                    pe.wait_ge(vw_ld, 16 * b + 16)
                    for n in range(WIN_T):
                        pe.matmul(o_ps[:, 1, :], pT[:, PAST_T + n, :], vwx[:, n, :], start=(n == 0), stop=False)
                    ins = pe.matmul(o_ps[:, 1, :], pTn[:, 1, :], row(vn[:, ds(b, 1), 1, :]), start=False, stop=True)
                ins.then_inc(pv_done, 1)

            pe.wait_ge(m_ld, 48)

            def step(b):
                if not end(b):
                    transposes(b, 0)
                    transposes(b, 1)
                for c in range(CH_B):
                    if not end(b):
                        scores(b, c)
                        if c + 2 < CH_B:
                            transposes(b, c + 2)
                    if not first(b):
                        if 1 <= c <= PG:
                            prob_transposes(b - 1, c - 1)
                        if 2 <= c <= PG + 1:
                            values(b - 1, c - 2)
                if not end(b):
                    new_scores(b)

            sequences(pe, step)
            pe.wait_ge(dup_set, 1)
            for b in range(NB):
                ins = pe.transpose(t_ps[0][:, b * MR:(b + 1) * MR], odup[:, b, :, :].rearrange("p k c -> p (k c)"), ident[0:MR, 0:MR])
            ins.then_inc(oT_done, 1)

        def take_keys(eng, copy, b, c):
            eng.wait_ge(t_done, CH_B * b + c + 1)
            if not (first(b) and c < 2):
                eng.wait_ge(qk_done, before(b, c))
            copy(kT[c % 2][:], t_ps[c % 2][:]).then_inc(kt_set[c % 2], 1)

        def take_probs(eng, copy, b, u):
            eng.wait_ge(pt_done, PG * b + u + 1)
            if u == (1 if eng is nc.scalar else 0) and not first(b):
                eng.wait_ge(pv_done, PG * b)
            if u < 4:
                ins = copy(pT[:, 8 * u:8 * u + 8, :], p_ps[u % 2][:])
            else:
                copy(pT[:, PAST_T:PAST_T + WIN_T, :], p_ps[0][:, 0:WIN_T, :])
                ins = copy(pTn[0:TS], p_ps[0][0:TS, WIN_T:WIN_T + 2, :])
            ins.then_inc(pt_set[u % 2], 1)

        @block.scalar
        def _(act):
            copy = lambda out, in_: act.activation(out, in_, ACT.Copy)

            def step(b):
                if not end(b):
                    take_keys(act, copy, b, 1)
                for c in range(CH_B):
                    if not end(b) and c + 2 < CH_B and c % 2:
                        take_keys(act, copy, b, c + 2)
                    if not first(b) and c in (2, 4):
                        take_probs(act, copy, b - 1, c - 1)
                if not end(b):
                    act.wait_ge(max_set, b + 1)
                    if not first(b):
                        act.wait_ge(pt_done, PG * b)
                    act.activation(prob[:, 0:WIN_0], s_all[:, 0:WIN_0], ACT.Exp, bias=stat[:, 0:1], accum_out=stat[:, 2:3])
                    act.activation(prob[:, WIN_0:SCOLS], s_all[:, WIN_0:SCOLS], ACT.Exp, bias=stat[:, 1:2],
                                   accum_out=stat[:, 3:4]).then_inc(exp_done, 1)

            sequences(act, step)

        @block.vector
        def _(dve):
            link = Chain(dve, ch_v)
            copy = dve.tensor_copy
            tt = dve.tensor_tensor
            dve.memset(vn[:], 0.0).then_inc(zeroed, 1)
            link.put(dve.memset(pTn[:], 0.0))
            link(copy(qs[:], qbd[:, 0, :]))
            dve.sem_inc(q_set, 1)
            dve.wait_ge(m_ld, 48)
            link.restart()

            def add(b, c):
                dve.wait_ge(qk_done, CH_B * b + c + 1)
                if c == 0 and not first(b):
                    dve.wait_ge(exp_done, b)
                if c < KCH:
                    i = c // (KCH // 2)
                    split = lambda ap: ap.rearrange("p (l n f) -> p l n f", l=4, f=4)
                    bias = sel_bias[:, ds(b, 1), 32 * i:32 * i + 32].unsqueeze(3).to_broadcast([MR, 4, 32, 4])
                    link(tt(split(s_all[:, 512 * c:512 * c + 512]), split(s_ps[c % 2][:]), bias, ALU.add))
                else:
                    link(tt(s_all[:, WIN_0:NEW_W], s_ps[0][:], win_mask[:], ALU.add))
                dve.sem_inc(s_added, 1)

            def out(b):
                dve.wait_ge(pv_done, PG * b + PG)
                link(dve.tensor_scalar(stat[:, 4:6], stat[:, 2:4], 1e-30, None, ALU.max))
                link(dve.reciprocal(stat[:, 4:6], stat[:, 4:6]))
                link(tt(stat[:, 6:8], stat[:, 4:6], row(g_rows[:, ds(b, 1), 1:3]), ALU.mult))
                for n in range(2):
                    for g in range(NKV):
                        rows = slice(g * MR // 2, (g + 1) * MR // 2)
                        at = row(osum[rows, ds(b, 1), :])
                        link.put(dve.scalar_tensor_tensor(at, o_ps[rows, n, g * DH:(g + 1) * DH], stat[rows, 6 + n:7 + n], at,
                                                          ALU.mult, ALU.add))
                    link.sync()
                dve.sem_inc(o_set, 1)

            def step(b):
                if not end(b):
                    take_keys(dve, copy, b, 0)
                for c in range(CH_B):
                    if not end(b):
                        add(b, c)
                        if c + 2 < CH_B and c % 2 == 0:
                            take_keys(dve, copy, b, c + 2)
                    if not first(b) and c in (1, 3, 5):
                        take_probs(dve, copy, b - 1, c - 1)
                if not first(b):
                    out(b - 1)
                if not end(b):
                    dve.wait_ge(new_done, b + 1)
                    for n, at in enumerate((NEW_S, NEW_W)):
                        link.put(tt(s_all[:, at:at + TS], new_ps[:, n, :], new_mask[:], ALU.add))
                    link.sync()
                    dve.sem_inc(new_added, 1)
                    if not (isinstance(b, int) and b == NB - 1):
                        link(copy(qs[:], row(qbd[:, ds(b + 1, 1), :])))
                        dve.sem_inc(q_set, 1)
                    link.put(dve.tensor_reduce(stat[:, 0:1], s_all[:, 0:WIN_0], X, ALU.max, negate=True))
                    link(dve.tensor_reduce(stat[:, 1:2], s_all[:, WIN_0:SCOLS], X, ALU.max, negate=True))
                    dve.sem_inc(max_set, 1)
                link.restart()

            sequences(dve, step)
            for k in range(2):
                link.put(copy(odup[:, :, k, :], osum[:]))
            link.sync()
            dve.sem_inc(dup_set, 1)
            dve.wait_ge(oT_done, 1)
            for g in range(NKV):
                rows = slice(g * DH, (g + 1) * DH)
                src = t_ps[0][rows, :].rearrange("p (b g j t) -> p g b j t", b=NB, g=NKV, j=NG)[:, g]
                copy(oT[rows, :, :].rearrange("p j (b t) -> p b j t", t=TS), src).then_inc(oT_set, 1)


WT = WIN // P
CMP, SLC, WIND = range(3)


def prompt_units():
    units = [(i, g, br, [0] if br == CMP else list(range(0 if br == SLC else max(0, i - WT), i + 1)))
             for i in range(TT) for g in range(NKV) for br in (CMP, SLC, WIND)]
    groups, n = [], 0
    for unit in units:
        k = -(-len(unit[3]) // 4)
        groups.append(range(n, n + k))
        n += k
    assert len(units) % 2 == 0 and n % 2 == 0
    return units, groups, n


def score_plan(units, banks, ahead):
    held, at, before = [None] * banks, [], []
    here = 0
    for u, (_, _, br, tiles) in enumerate(units):
        n = 1 if br == CMP or len(tiles) <= 4 else 2
        if here + n > banks:
            here = 0
        before.append(max((w for w in held[here:here + n] if w is not None), default=None))
        at.append(here)
        held[here:here + n] = [u] * n
        here += n
    starts, v = [[] for _ in range(len(units) + 1)], 0
    for step in range(-1, len(units)):
        while v < len(units) and v <= step + ahead and (before[v] is None or before[v] <= step):
            starts[step + 1].append(v)
            v += 1
        assert v == len(units) or v > step + 1
    return at, before, starts


def phase_prompt(nc, d, r):
    assert SEQ // 64 <= TOPK
    units, groups, NGR = prompt_units()
    U, UT = len(units), len(units) // TT
    BANKS, AHEAD = 5, 3
    s_at, s_before, starts = score_plan(units, BANKS, AHEAD)
    with ExitStack() as ctx:
        sb = lambda name, shape: ctx.enter_context(nc.sbuf_tensor("pr_" + name, shape, F32))
        pb = lambda name, shape: ctx.enter_context(nc.psum_tensor("pr_" + name + "_ps", shape, F32))
        sem = ctx.enter_context(Semaphores(nc, "pr_"))
        ident, qkT, v_nat, gates, kc_p, vc_p, oT, oTs = (r[n] for n in ("ident", "qkT", "v_nat", "gates", "kc_p", "vc_p", "oT", "oTs"))
        causal = sb("causal", [P, P])
        behind_win = sb("behind_win", [P, P])
        cmp_mask = sb("cmp_mask", [P, TT, NC_P])
        any_cmp = sb("any_cmp", [P, 1])
        qz = [sb(f"qz{g}", [P, SEQ]) for g in range(NKV)]
        prob = [sb(f"prob{k}", [P, SEQ]) for k in range(AHEAD)]
        pT = [sb(f"pT{k}", [P, TT, P]) for k in range(2)]
        o_j = sb("o_j", [P, TT, P])
        nmax = sb("nmax", [P, U])
        sums = sb("sums", [P, U])
        coef = sb("coef", [P, NKV, 3])
        parts = sb("parts", [P, NKV, 3, DH])
        s_ps = pb("s", [P, BANKS * 512])
        pt_ps = [pb(f"pt{k}", [P, 4, P]) for k in range(2)]
        o_ps = pb("o", [P, NKV, 3, DH])

        m_ld, zeroed, q_set, s_done, max_set, exp_done, pt_done = (
            sem(n) for n in ("m_ld", "zeroed", "q_set", "s_done", "max_set", "exp_done", "pt_done"))
        pt_set = [sem("pt_set0"), sem("pt_set1")]
        pv_done, o_taken, oj_set, oT_done, oT_set, ch_v, oTs_set = (sem(n) for n in ("pv_done", "o_taken", "oj_set", "oT_done", "oT_set", "ch_v", "oTs_set"))
        block = ctx.enter_context(nc.Block())
        scores_of = lambda u: s_ps[:, 512 * s_at[u]:512 * s_at[u] + (NC_P if units[u][2] == CMP else len(units[u][3]) * P)]

        def head_pairs(eng, step):
            step(0)
            with eng.Fori(1, NG) as j:
                step(j)

        first = lambda j: isinstance(j, int)

        @block.sync
        def _(sp):
            for dst, name in ((causal, "causal"), (behind_win, "behind_win"), (any_cmp, "any_cmp")):
                sp.dma_start(dst[:], d[name]).then_inc(m_ld, 16)
            sp.dma_start(cmp_mask[:], d["cmp_mask"]).then_inc(m_ld, 16)

        @block.gpsimd
        def _(pool):
            pool.tensor_copy(oT[:, :, SEQ:TOK], oTs[:]).then_inc(oTs_set, 1)
            pool.wait_ge(oTs_set, 1)
            for g in range(NKV):
                pool.memset(qz[g][(1 - g) * DH:(2 - g) * DH, :], 0.0).then_inc(zeroed, 1)
                pool.wait_ge(zeroed, g + 1)

            def step(j):
                if not first(j):
                    pool.wait_ge(s_done, U * j)
                for g in range(NKV):
                    rows = slice(g * DH, (g + 1) * DH)
                    pool.tensor_copy(qz[g][rows, :], row(qkT[rows, ds(j, 1), 0:SEQ])).then_inc(q_set, 1)
                    pool.wait_ge(q_set, NKV * j + g + 1)

            head_pairs(pool, step)

        @block.tensor
        def _(pe):
            pe.wait_ge(zeroed, NKV)

            def step(j):
                def score(u):
                    i, g, br, tiles = units[u]
                    if s_before[u] is not None:
                        pe.wait_ge(exp_done, U * j + s_before[u] + 1)
                    s = scores_of(u)
                    q = qz[g][:, i * P:(i + 1) * P]
                    if br == CMP:
                        ins = pe.matmul(s, q, kc_p[:], start=True, stop=True)
                    else:
                        k0, n = tiles[0] * P, len(tiles) * P
                        for at in range(0, n, 512):
                            w = min(512, n - at)
                            ins = pe.matmul(s[:, at:at + w], q, qkT[:, NG + br - 1, k0 + at:k0 + at + w],
                                            start=True, stop=True)
                    ins.then_inc(s_done, 1)

                def transpose(u):
                    i, g, br, tiles = units[u]
                    pe.wait_ge(exp_done, U * j + u + 1)
                    for k, n in enumerate(groups[u]):
                        if not (first(j) and n < 2):
                            pe.wait_ge(pt_set[n % 2], NGR // 2 * j + n // 2)
                        pe.nop(nofuse=True)
                        if br == CMP:
                            ins = pe.transpose(pt_ps[n % 2][0:NC_P, 0, :], prob[u % AHEAD][:, 0:NC_P], ident[:])
                        else:
                            for m in range(4 * k, min(4 * k + 4, len(tiles))):
                                ins = pe.transpose(pt_ps[n % 2][:, m % 4, :], prob[u % AHEAD][:, m * P:(m + 1) * P], ident[:])
                        ins.then_inc(pt_done, 1)

                def values(u):
                    i, g, br, tiles = units[u]
                    for n in groups[u]:
                        pe.wait_ge(pt_set[n % 2], NGR // 2 * j + n // 2 + 1)
                    if u % UT == 0 and not (first(j) and u == 0):
                        pe.wait_ge(o_taken, TT * j + i)
                    cols = slice(g * DH, (g + 1) * DH)
                    if br == CMP:
                        ins = pe.matmul(o_ps[:, g, br, :], pT[u % 2][0:NC_P, 0, :], vc_p[:, cols], start=True, stop=True)
                    else:
                        for m, t in enumerate(tiles):
                            ins = pe.matmul(o_ps[:, g, br, :], pT[u % 2][:, m, :], v_nat[:, t, br, cols],
                                            start=(m == 0), stop=(m == len(tiles) - 1))
                    ins.then_inc(pv_done, 1)

                pe.wait_ge(q_set, NKV * j + NKV)
                for v in starts[0]:
                    score(v)
                for u in range(U):
                    transpose(u)
                    for v in starts[u + 1]:
                        score(v)
                    if u:
                        values(u - 1)
                values(U - 1)
                pe.wait_ge(oj_set, TT * j + TT)
                for i in range(TT):
                    ins = pe.transpose(s_ps[:, i * P:(i + 1) * P], o_j[:, i, :], ident[:])
                ins.then_inc(oT_done, 1)
                pe.wait_ge(oT_set, j + 1)

            head_pairs(pe, step)

        def take(eng, copy, j, u, parity):
            i, g, br, tiles = units[u]
            for k, n in enumerate(groups[u]):
                if n % 2 != parity:
                    continue
                eng.wait_ge(pt_done, NGR * j + n + 1)
                if not (first(j) and u < 2):
                    eng.wait_ge(pv_done, U * j + u - 1)
                if br == CMP:
                    ins = copy(pT[u % 2][0:NC_P, 0, :], pt_ps[n % 2][0:NC_P, 0, :])
                else:
                    w = min(4, len(tiles) - 4 * k)
                    ins = copy(pT[u % 2][:, 4 * k:4 * k + w, :], pt_ps[n % 2][:, 0:w, :])
                ins.then_inc(pt_set[n % 2], 1)

        @block.scalar
        def _(act):
            copy = lambda out, in_: act.activation(out, in_, ACT.Copy)

            def step(j):
                def exponentials(u):
                    s = scores_of(u)
                    act.wait_ge(max_set, U * j + u + 1)
                    if u >= AHEAD:
                        act.wait_ge(pt_done, NGR * j + groups[u - AHEAD][-1] + 1)
                    act.activation(prob[u % AHEAD][:, 0:s.shape[1]], s, ACT.Exp, bias=nmax[:, u:u + 1],
                                   accum_out=sums[:, u:u + 1]).then_inc(exp_done, 1)

                for v in starts[0]:
                    exponentials(v)
                for u in range(U):
                    take(act, copy, j, u, 1)
                    for v in starts[u + 1]:
                        exponentials(v)
                act.wait_ge(oT_done, j + 1)
                act.activation(row(oT[:, ds(j, 1), 0:SEQ]), s_ps[:, 0:SEQ], ACT.Copy).then_inc(oT_set, 1)

            head_pairs(act, step)

        @block.vector
        def _(dve):
            link = Chain(dve, ch_v)
            copy = dve.tensor_copy
            dve.wait_ge(m_ld, 64)

            def step(j):
                def maximum(u):
                    i, g, br, tiles = units[u]
                    s = scores_of(u)
                    n = s.shape[1]
                    dve.wait_ge(s_done, U * j + u + 1)
                    if br == CMP:
                        link(dve.tensor_tensor(s[:, 0:n], s[:, 0:n], cmp_mask[:, i, :], ALU.add))
                    else:
                        link.put(dve.tensor_tensor(s[:, n - P:n], s[:, n - P:n], causal[:], ALU.add))
                        if br == WIND and i >= WT:
                            link.put(dve.tensor_tensor(s[:, 0:P], s[:, 0:P], behind_win[:], ALU.add))
                        link.sync()
                    dve.tensor_reduce(nmax[:, u:u + 1], s[:, 0:n], X, ALU.max, negate=True).then_inc(max_set, 1)

                def coefficients(i):
                    dve.wait_ge(exp_done, U * j + UT * i + UT)
                    at = sums[:, UT * i:UT * i + UT].rearrange("p (g b) -> p g b", g=NKV)
                    gate = row(gates[:, i:i + 1, :]).rearrange("p (g n) -> p g n", g=NKV)[:, :, ds(3 * j, 3)]
                    link(dve.tensor_scalar(coef[:], at, 1e-30, None, ALU.max))
                    link(dve.reciprocal(coef[:], coef[:]))
                    link(dve.tensor_tensor(coef[:], coef[:], gate, ALU.mult))
                    if i == 0:
                        link(dve.tensor_scalar(coef[:, :, CMP], coef[:, :, CMP], any_cmp[:], None, ALU.mult))

                def output(i):
                    dve.wait_ge(pv_done, U * j + UT * i + UT)
                    link(dve.tensor_tensor(parts[:], o_ps[:], coef[:].unsqueeze(3).to_broadcast([P, NKV, 3, DH]), ALU.mult))
                    dve.sem_inc(o_taken, 1)
                    at = o_j[:, i, :].rearrange("p (g c) -> p g c", g=NKV)
                    link(dve.tensor_tensor(at, parts[:, :, 0, :], parts[:, :, 1, :], ALU.add))
                    link(dve.tensor_tensor(at, at, parts[:, :, 2, :], ALU.add))
                    dve.sem_inc(oj_set, 1)

                if not first(j):
                    dve.wait_ge(oT_done, j)
                for v in starts[0]:
                    maximum(v)
                for u in range(U):
                    take(dve, copy, j, u, 0)
                    for v in starts[u + 1]:
                        maximum(v)
                    if u % UT == 0 and u:
                        output(u // UT - 1)
                    if u % UT == UT - 1:
                        coefficients(u // UT)
                output(TT - 1)
                link.restart()

            head_pairs(dve, step)


def phase_merge(nc, d, r, mergedT):
    parts = (("g1", "hT", DT), ("g2", "hT", DT), ("s5", "yT", FT), ("nsa", "oT", NG))
    with ExitStack() as ctx:
        sb = lambda name, shape: ctx.enter_context(nc.sbuf_tensor("m_" + name, shape, F32))
        sem = ctx.enter_context(Semaphores(nc, "m_"))
        w = [[sb(f"w_{name}{k}", [P, kt, P]) for name, _, kt in parts] for k in range(2)]
        tanh = [sb(f"tanh{k}", [P, 2, 384]) for k in range(2)]
        ps = [ctx.enter_context(nc.psum_tensor(f"m_ps{k}", [P, 4, 512], F32)) for k in range(2)]
        w_ld = [sem("w_ld0"), sem("w_ld1")]
        multiplied, tanhed, merged, ch_v = sem("multiplied"), sem("tanhed"), sem("merged"), sem("ch_v")
        block = ctx.enter_context(nc.Block())
        NC = len(CHUNKS)

        def turns(eng, body):
            for n in range(2 * NC):
                body(0, n // NC, n % NC, n)
            with eng.Fori(1, DT // 2) as i:
                for n in range(2 * NC):
                    body(i, n // NC, n % NC, n)

        first = lambda i: isinstance(i, int)

        @block.sync
        def _(sp):
            def load(i, k):
                ft = 2 * i + k
                rows = lambda name: d[name].rearrange("z k n -> (z k) n")
                for g in range(2):
                    at = OFF_MIX + D * g
                    sp.dma_start(w[k][g][:], rows("w_in")[:, ds(at + ft * P, P)].rearrange("(c p) n -> p c n", p=P)).then_inc(w_ld[k], 16)
                sp.dma_start(w[k][2][:], rows("s5_w_up")[:, ds(ft * P, P)].rearrange("(c p) n -> p c n", p=P)).then_inc(w_ld[k], 16)
                for g in range(NKV):
                    sp.dma_start(w[k][3][g * DH:(g + 1) * DH, :, :],
                                 rows("nsa_w_up")[g * NG * DH:(g + 1) * NG * DH, ds(ft * P, P)].rearrange("(j q) n -> q j n", q=DH)
                                 ).then_inc(w_ld[k], 16)

            load(0, 0)
            load(0, 1)
            with sp.Fori(1, DT // 2) as i:
                for k in range(2):
                    sp.wait_ge(multiplied, 2 * NC * i + NC * k - NC)
                    load(i, k)

        @block.tensor
        def _(pe):
            def body(i, k, c, n):
                if c == 0:
                    pe.wait_ge(w_ld[k], 80 * i + 80)
                if not (first(i) and n < 2):
                    pe.wait_ge(merged, 2 * NC * i + n - 1)
                at, m = CHUNKS[c]
                for q, (_, src, kt) in enumerate(parts):
                    for t in range(kt):
                        ins = pe.matmul(ps[n % 2][:, q, 0:m], w[k][q][:, t, :], r[src][:, t, at:at + m],
                                        start=(t == 0), stop=(t == kt - 1))
                ins.then_inc(multiplied, 1)

            turns(pe, body)

        @block.scalar
        def _(act):
            def body(i, k, c, n):
                act.wait_ge(multiplied, 2 * NC * i + n + 1)
                if not (first(i) and n < 2):
                    act.wait_ge(merged, 2 * NC * i + n - 1)
                m = CHUNKS[c][1]
                act.activation(tanh[n % 2][:, :, 0:m], ps[n % 2][:, 0:2, 0:m], ACT.Tanh, scale=0.5).then_inc(tanhed, 1)

            turns(act, body)

        @block.vector
        def _(dve):
            link = Chain(dve, ch_v)

            def body(i, k, c, n):
                at, m = CHUNKS[c]
                dve.wait_ge(tanhed, 2 * NC * i + n + 1)
                t = tanh[n % 2]
                for q in range(2):
                    link.put(dve.scalar_tensor_tensor(t[:, q, 0:m], t[:, q, 0:m], 1.0, ps[n % 2][:, 2 + q, 0:m], ALU.add, ALU.mult))
                link.sync()
                link(dve.scalar_tensor_tensor(row(mergedT[:, ds(2 * i + k, 1), at:at + m]), t[:, 0, 0:m], 0.5, t[:, 1, 0:m],
                                              ALU.mult, ALU.add))
                link.restart()
                dve.sem_inc(merged, 1)

            turns(dve, body)


def phase_out(nc, d, r, mergedT, h2T):
    with ExitStack() as ctx:
        sb = lambda name, shape: ctx.enter_context(nc.sbuf_tensor("o_" + name, shape, F32))
        sem = ctx.enter_context(Semaphores(nc, "o_"))
        ident = r["ident"]
        w = sb("w", [P, DT, D])
        ffnw = sb("ffnw", [P, DT])
        xt = [sb(f"x{k}", [P, D]) for k in range(2)]
        x1 = [sb(f"x1{k}", [P, D]) for k in range(2)]
        xn = [sb(f"xn{k}", [P, D]) for k in range(2)]
        junk = sb("junk", [P, D])
        mt = [sb(f"mt{k}", [P, DT, P]) for k in range(2)]
        ssum, rms, rstd = sb("ssum", [P, 2]), sb("rms", [P, 2]), sb("rstd", [P, 2])
        eps = sb("eps", [P, 1])
        z_ps = [ctx.enter_context(nc.psum_tensor(f"o_z{k}", [P, 2, 512], F32)) for k in range(2)]
        xT_ps = ctx.enter_context(nc.psum_tensor("o_xT", [P, DT, P], F32))
        w_ld = [sem(f"w_ld{c}") for c in range(DT)]
        x_ld = [sem("x_ld0"), sem("x_ld1")]
        (c_ld, mt_set, z_done, x1_set, squared, rooted, xn_set, xT_done, h2_set, eps_set, ch_v) = (
            sem(n) for n in ("c_ld", "mt_set", "z_done", "x1_set", "squared", "rooted", "xn_set", "xT_done", "h2_set", "eps_set", "ch_v"))
        x1_stored = [sem("x1_stored0"), sem("x1_stored1")]
        block = ctx.enter_context(nc.Block())
        x_p = d["x_prompt"].rearrange("a (t p) n -> (a t) p n", p=P)
        x1_d = d["x1"].rearrange("(t p) n -> t p n", p=P)
        tile = lambda ap, t: ap[t] if isinstance(t, int) else ap[ds(t, 1)].rearrange("t p n -> (t p) n")

        @block.sync
        def _(sp):
            def load(t, k):
                if behind(t, 2):
                    sp.wait_ge(x1_set, t - 1)
                if isinstance(t, int) and t == TT:
                    sp.dma_start(xt[k][0:NS, :], d["x_sample"].rearrange("b t n -> (b t) n")).then_inc(x_ld[k], 16)
                else:
                    sp.dma_start(xt[k][:], tile(x_p, t)).then_inc(x_ld[k], 16)
                if isinstance(t, int) and t == 0:
                    wo = d["w_out"].rearrange("z (c p) n -> p (z c) n", p=P)
                    for c in range(DT):
                        sp.dma_start(w[:, c, :], wo[:, c, :]).then_inc(w_ld[c], 16)

            token_tiles(sp, load)

        @block.gpsimd
        def _(pool):
            def body(t, k):
                if behind(t, 2):
                    pool.wait_ge(z_done, t - 1)
                pool.tensor_copy(mt[k][:], mergedT[:, :, ds(t * P, P)]).then_inc(mt_set, 1)
                if behind(t, 1):
                    store(t - 1, 1 - k)

            def store(t, k):
                pool.wait_ge(x1_set, t + 1)
                pool.dma_start(tile(x1_d, t), x1[k][:]).then_inc(x1_stored[k], 16)

            token_tiles(pool, body)
            store(TT, 0)
            pool.wait_ge(x1_stored[0], 16 * (TT // 2 + 1))
            pool.wait_ge(x1_stored[1], 16 * (TT // 2))

        @block.tensor
        def _(pe):
            def transposes(t, k):
                pe.wait_ge(xn_set, t + 1)
                if behind(t, 1):
                    pe.wait_ge(h2_set, t)
                for c in range(DT):
                    ins = pe.transpose(xT_ps[:, c, :], xn[k][:, c * P:(c + 1) * P], ident[:])
                ins.then_inc(xT_done, 1)

            def body(t, k):
                pe.wait_ge(mt_set, t + 1)
                if behind(t, 2):
                    pe.wait_ge(x1_set, t - 1)
                for c in range(DT):
                    if isinstance(t, int) and t == 0:
                        pe.wait_ge(w_ld[c], 16)
                    for b in range(2):
                        ins = pe.matmul(z_ps[k][:, b, :], mt[k][:, c, :], w[:, c, b * 512:(b + 1) * 512],
                                        start=(c == 0), stop=(c == DT - 1))
                ins.then_inc(z_done, 1)
                if behind(t, 1):
                    transposes(t - 1, 1 - k)

            token_tiles(pe, body)
            transposes(TT, 0)

        @block.scalar
        def _(act):
            act.dma_start(ffnw[:], d["norm_ffn_w"].rearrange("z (c p) -> p (z c)", p=P), allow_slow_non_contiguous=True).then_inc(c_ld, 16)
            act.wait_ge(eps_set, 1)

            def body(t, k):
                act.wait_ge(x1_set, t + 1)
                act.activation(junk[:], x1[k][:], ACT.Square, accum_out=ssum[:, k:k + 1]).then_inc(squared, 1)
                act.wait_ge(squared, t + 1)
                act.activation(rms[:, k:k + 1], ssum[:, k:k + 1], ACT.Sqrt, bias=eps[:], scale=1.0 / D).then_inc(rooted, 1)

            token_tiles(act, body)

        @block.vector
        def _(dve):
            link = Chain(dve, ch_v)
            dve.memset(eps[:], EPS).then_inc(eps_set, 1)
            dve.wait_ge(c_ld, 16)

            def weigh(t, k):
                dve.wait_ge(xT_done, t + 1)
                dve.tensor_tensor(h2T[:, :, ds(t * P, P)], xT_ps[:], ffnw[:].unsqueeze(2).to_broadcast([P, DT, P]),
                                  ALU.mult).then_inc(h2_set, 1)

            def body(t, k):
                dve.wait_ge(z_done, t + 1)
                turn = t // 2 if isinstance(t, int) else None
                dve.wait_ge(x_ld[k], 8 * (t - k) + 16)
                if behind(t, 2):
                    dve.wait_ge(x1_stored[k], 8 * (t - k))
                link(dve.scalar_tensor_tensor(x1[k][:], z_ps[k][:].rearrange("p b n -> p (b n)"), 0.5, xt[k][:], ALU.mult, ALU.add))
                dve.sem_inc(x1_set, 1)
                dve.wait_ge(rooted, t + 1)
                link(dve.reciprocal(rstd[:, k:k + 1], rms[:, k:k + 1]))
                if behind(t, 2):
                    dve.wait_ge(xT_done, t - 1)
                link(dve.tensor_scalar(xn[k][:], x1[k][:], rstd[:, k:k + 1], None, ALU.mult))
                link.restart()
                dve.sem_inc(xn_set, 1)
                if behind(t, 1):
                    weigh(t - 1, 1 - k)

            token_tiles(dve, body)
            weigh(TT, 0)


KF = DFF // P


def phase_ffn2(nc, d, r, aT):
    with ExitStack() as ctx:
        sb = lambda name, shape: ctx.enter_context(nc.sbuf_tensor("f_" + name, shape, F32))
        sem = ctx.enter_context(Semaphores(nc, "f_"))
        ident = r["ident"]
        w = [sb(f"w{k}", [P, KF, P]) for k in range(2)]
        yT = r["hT"][:, 0, :]
        x1s = [r["hT"][:, 1 + k, :].rearrange("p (t n) -> p t n", n=P) for k in range(2)]
        ps = [ctx.enter_context(nc.psum_tensor(f"f_ps{c}", [P, 512], F32)) for c in range(3)]
        back = ctx.enter_context(nc.psum_tensor("f_back", [P, 12, P], F32))
        w_ld = [[sem(f"w_ld{k}{h}") for h in range(2)] for k in range(2)]
        x_ld, stored = [sem("x_ld0"), sem("x_ld1")], [sem("st0"), sem("st1")]
        multiplied, taken, backed, y_set, zeroed = (sem(n) for n in ("multiplied", "taken", "backed", "y_set", "zeroed"))
        block = ctx.enter_context(nc.Block())
        x1_d = d["x1"].rearrange("(t p) n -> p t n", p=P)
        H = KF // 2

        def turns(eng, body):
            body(0, 0)
            body(0, 1)
            with eng.Fori(1, DT // 2) as i:
                for k in range(2):
                    body(i, k)

        first = lambda i: isinstance(i, int)

        @block.sync
        def _(sp):
            def load(i, k):
                cols = ds((2 * i + k) * P, P)
                if not first(i):
                    sp.wait_ge(multiplied, 2 * i + k - 1)
                for h in range(2):
                    sp.dma_start(w[k][:, h * H:(h + 1) * H, :],
                                 d["w_ffn2"][0, h * H * P:(h + 1) * H * P, cols].rearrange("(c p) n -> p c n", p=P)).then_inc(w_ld[k][h], 16)

            turns(sp, load)

        @block.gpsimd
        def _(pool):
            def load(i, k):
                if not first(i):
                    pool.wait_ge(stored[k], 32 * i)
                pool.dma_start(x1s[k], x1_d[:, :, ds((2 * i + k) * P, P)]).then_inc(x_ld[k], 16)

            def store(i, k):
                pool.wait_ge(y_set, 2 * i + k + 1)
                pool.nop(nofuse=True)
                cols = ds((2 * i + k) * P, P)
                pool.dma_start(d["y_prompt"].rearrange("a (t p) n -> p (a t) n", p=P)[:, :, cols], x1s[k][:, 0:TT, :]).then_inc(stored[k], 16)
                pool.dma_start(d["y_sample"].rearrange("b t n -> (b t) n")[:, cols], x1s[k][0:NS, TT, :]).then_inc(stored[k], 16)

            load(0, 0)
            load(0, 1)
            store(0, 0)
            with pool.Fori(1, DT // 2) as i:
                load(i, 0)
                store(i - 1, 1)
                load(i, 1)
                store(i, 0)
            store(DT // 2 - 1, 1)
            for k in range(2):
                pool.wait_ge(stored[k], 32 * (DT // 2))

        @block.tensor
        def _(pe):
            def back_to_rows(n):
                pe.wait_ge(taken, n + 1)
                if not (isinstance(n, int) and n == 0):
                    pe.wait_ge(y_set, n)
                for t in range(NT):
                    ins = pe.transpose(back[:, t, :], yT[:, t * P:(t + 1) * P], ident[:])
                ins.then_inc(backed, 1)

            def body(i, k):
                n = 2 * i + k
                if not (first(i) and k == 0):
                    pe.wait_ge(taken, n)
                for h in range(2):
                    pe.wait_ge(w_ld[k][h], 16 * i + 16)
                    for c in range(h * H, (h + 1) * H):
                        for b, (at, m) in enumerate(CHUNKS):
                            ins = pe.matmul(ps[b][:, 0:m], w[k][:, c, :], aT[:, c, at:at + m], start=(c == 0), stop=(c == KF - 1))
                ins.then_inc(multiplied, 1)
                back_to_rows(n)

            pe.wait_ge(zeroed, 1)
            turns(pe, body)

        @block.scalar
        def _(act):
            def body(i, k):
                n = 2 * i + k
                act.wait_ge(multiplied, n + 1)
                if not (first(i) and k == 0):
                    act.wait_ge(backed, n)
                for b, (at, m) in enumerate(CHUNKS):
                    ins = act.activation(yT[:, at:at + m], ps[b][:, 0:m], ACT.Copy)
                ins.then_inc(taken, 1)

            turns(act, body)

        @block.vector
        def _(dve):
            dve.memset(yT[:, TOK:TPAD], 0.0).then_inc(zeroed, 1)

            def body(i, k):
                dve.wait_ge(backed, 2 * i + k + 1)
                dve.wait_ge(x_ld[k], 16 * i + 16)
                dve.tensor_tensor(x1s[k], x1s[k], back[:, 0:NT, :], ALU.add).then_inc(y_set, 1)

            turns(dve, body)


def constants():
    half = DH // 2
    inv = np.float32(10000.0) ** (-np.arange(half, dtype=np.float32) / np.float32(half))
    pos = np.zeros(TPAD, np.float32)
    pos[:SEQ] = np.arange(SEQ)
    pos[SEQ:TOK] = PAST + np.arange(NS) % TS
    ang = pos[:, None] * inv[None, :].astype(np.float32)
    rope = np.stack([np.cos(ang.astype(np.float64)), np.sin(ang.astype(np.float64))], 1).astype(np.float32)
    out = {"rope": rope, "identity": np.eye(P, dtype=np.float32)}
    gsum = np.zeros((NKV, NG, TS, NKV, TS), np.float32)
    for g in range(NKV):
        for t in range(TS):
            gsum[g, :, t, g, t] = 1.0
    gsum = gsum.reshape(MR, GT)
    t = np.arange(MR) % TS
    key = 4 * np.arange(P)[None, :] + np.arange(WIN_T)[:, None]
    win_mask = np.where(key.reshape(1, WIN) <= t[:, None], NEG, 0.0).astype(np.float32)
    new_mask = np.where(np.arange(TS)[None, :] > t[:, None], NEG, 0.0).astype(np.float32)
    q, k = np.arange(P)[:, None], np.arange(P)[None, :]
    mask = lambda hidden: np.where(hidden, NEG, 0.0).astype(np.float32)
    ends = CS * np.arange(NC_P) + CL - 1
    out.update(causal=mask(k > q), behind_win=mask(k <= q),
               cmp_mask=mask(ends[None, None, :] > (P * np.arange(TT)[None, :] + q)[:, :, None]),
               any_cmp=(q >= CL - 1).astype(np.float32))
    out.update(win_mask=win_mask, new_mask=new_mask)
    out.update(gsum=gsum, gspread=np.ascontiguousarray(gsum.T), in_page=(np.arange(P, dtype=np.int32) % (PAGE // CS))[:, None])
    return out


SCRATCH = {"x1": (TPAD, D), "v_new": (NS, 2 * KVW), "g_new": (NS, 3 * NH)}


def build(nc, d):
    ap = lambda name, dims: bass.AP(d[name].tensor, 0, dims)
    d["normw_q"] = ap("q_norm_w", [(0, P), (0, NH), (1, DH)])
    d["normw_k"] = ap("k_norm_w", [(0, P), (DH, 3), (1, DH)])
    columns = lambda name: lambda j: d[name][0, :, ds(256 * j, 256)].rearrange("(c p) n -> p c n", p=P)
    tokens = lambda t, ft, at, n: row(t[:, ds(ft, 1), at:at + n])
    with ExitStack() as whole:
        ident = whole.enter_context(nc.sbuf_tensor("ident", [P, P], F32))
        hT = whole.enter_context(nc.sbuf_tensor("hT", [P, DT, TPAD], F32))
        with ExitStack() as mixers:
            sb = lambda name, shape, stack=mixers: stack.enter_context(nc.sbuf_tensor(name, shape, F32))
            yT = sb("yT", [P, FT, TPAD])
            n_qk, n_v = (NG + 2) * TPAD, NT * 3 * KVW
            kept = sb("kept", [P, n_qk + n_v])
            assert DT * TPAD <= n_qk + n_v
            mergedT = kept[:, 0:DT * TPAD].rearrange("p (c n) -> p c n", c=DT)
            r = {"ident": ident, "hT": hT, "uT": yT, "yT": yT,
                 "qkT": kept[:, 0:n_qk].rearrange("p (c n) -> p c n", n=TPAD),
                 "v_nat": kept[:, n_qk:].rearrange("p (t c w) -> p t c w", c=3, w=KVW),
                 "gates": sb("gates", [P, NT, 3 * NH]), "oTs": sb("oTs", [P, NG, NS]),
                 "kc_p": sb("kc_p", [P, NC_P]), "vc_p": sb("vc_p", [NC_P, KVW])}
            phase_project(nc, d, r)
            phase_gemm(nc, "u", columns("w_in"), 1, DT, hT,
                       lambda act, ft, c, at, n, ps: act.activation(tokens(yT, ft, at, n), ps, ACT.Copy))
            phase_s5(nc, d, r)
            phase_gelu(nc, yT)
            with ExitStack() as sampled:
                r["qbd"] = sb("qbd", [P, NB + 1, MR], sampled)
                r["g_rows"] = sb("g_rows", [MR, NB, 3], sampled)
                r["osum"] = sb("osum", [MR, NB, DH], sampled)
                r["sel_bias"] = sb("sel_bias", [MR, NB, NSLC], sampled)
                phase_compress(nc, d, r)
                phase_sampled(nc, d, r)
            r["oT"] = sb("oT", [P, NG, TPAD])
            phase_prompt(nc, d, r)
            yT2 = sb("yT2", [P, FT, TPAD])
            phase_gemm(nc, "glu", columns("s5_w_glu"), 1, FT, yT,
                       lambda act, ft, c, at, n, ps: act.activation(tokens(yT2, ft, at, n), ps, ACT.Tanh, scale=0.5),
                       lambda dve, ft, c, at, n, link: link(dve.scalar_tensor_tensor(
                           tokens(yT2, ft, at, n), tokens(yT2, ft, at, n), 1.0, tokens(yT, ft, at, n), ALU.add, ALU.mult)))
            r["yT"] = yT2
            phase_merge(nc, d, r, mergedT)
            phase_out(nc, d, r, mergedT, hT)
        aT = whole.enter_context(nc.sbuf_tensor("aT", [P, KF, TOK], F32))
        phase_gemm(nc, "ffn", columns("w_ffn1"), DFF // 512, DT, hT,
                   lambda act, ft, c, at, n, ps: act.activation(tokens(aT, ft, at, n), ps, ACT.Relu),
                   lambda dve, ft, c, at, n, link: link(dve.tensor_tensor(
                       tokens(aT, ft, at, n), tokens(aT, ft, at, n), tokens(aT, ft, at, n), ALU.mult)))
        phase_ffn2(nc, d, r, aT)


_INS = ["x_prompt", "x_sample", "cache_k_cmp", "cache_v_cmp", "cache_k_slc", "cache_v_slc", "state_k_win", "state_v_win",
        "state_s5_re", "state_s5_im", "page_table", "norm_mix_w", "w_in", "s5_lam_re", "s5_lam_im", "s5_log_dt",
        "s5_b_re", "s5_b_im", "s5_c_re", "s5_c_im", "s5_d", "s5_w_glu", "s5_w_up", "q_norm_w", "k_norm_w", "cmp_pe_k",
        "cmp_wk1", "cmp_wk2", "cmp_pe_v", "cmp_wv1", "cmp_wv2", "nsa_w_up", "w_out", "norm_ffn_w", "w_ffn1", "w_ffn2"]
_KV_P, _KV_S = (1, 1, SEQ, NKV, DH), (1, NB, TS, NKV, DH)
_OUTS = [("y_prompt", (1, SEQ, D)), ("y_sample", (NB, TS, D)), ("k_cmp_p", _KV_P), ("k_cmp_s", _KV_S),
         ("v_cmp_p", _KV_P), ("v_cmp_s", _KV_S), ("k_slc_p", _KV_P), ("k_slc_s", _KV_S), ("v_slc_p", _KV_P),
         ("v_slc_s", _KV_S), ("k_win_p", (1, 1, WIN, NKV, DH)), ("k_win_s", (1, NB, WIN, NKV, DH)),
         ("v_win_p", (1, 1, WIN, NKV, DH)), ("v_win_s", (1, NB, WIN, NKV, DH)), ("s5_re_p", (1, 1, S5G, S5P)),
         ("s5_re_s", (1, NB, S5G, S5P)), ("s5_im_p", (1, 1, S5G, S5P)), ("s5_im_s", (1, NB, S5G, S5P))]


def kernel(**inputs):
    import concourse.bacc as bacc
    from concourse.bass_utils import run_bass_kernel_spmd

    nc = bacc.Bacc("TRN2", target_bir_lowering=False, num_devices=1)
    arrays, d = {}, {}
    given = {name: inputs[name] for name in _INS}
    for name, a in {**given, **constants()}.items():
        a = np.ascontiguousarray(a)
        arrays["in_" + name] = a
        d[name] = nc.dram_tensor("in_" + name, a.shape, mybir.dt.from_np(a.dtype), kind="ExternalInput").ap()
    for name, shape in _OUTS:
        d[name] = nc.dram_tensor("out_" + name, shape, F32, kind="ExternalOutput").ap()
    for name, shape in SCRATCH.items():
        d[name] = nc.dram_tensor("scratch_" + name, shape, F32, kind="Internal").ap()
    build(nc, d)
    result = run_bass_kernel_spmd(nc, [arrays], core_ids=[0])
    return tuple(result.results[0]["out_" + name] for name, _ in _OUTS)
```

```python
from contextlib import ExitStack

import numpy as np
import concourse.bass as bass
from concourse import mybir

F32 = mybir.dt.float32
I32 = mybir.dt.int32
ALU = mybir.AluOpType
ACT = mybir.ActivationFunctionType
X = mybir.AxisListType.X
XY = mybir.AxisListType.XY
ds = bass.ds

P = 128
D = 1024
SEQ = 1024
NB, TS = 8, 8
NS = NB * TS
PAST, PAGE = 4096, 128
PAGES = PAST // PAGE
S5W, S5G, S5H, S5P = 512, 32, 16, 64
DH, NH, NKV, NG = 64, 8, 2, 4
KVW = NKV * DH
CL, CS, CH = 32, 16, 128
NSLC, TOPK = 65, 16
WIN = 512
DFF = 4096
EPS = 1e-6
NEG = -1e30
SCALE = DH ** -0.5
DT = D // P
TT = SEQ // P
NT = TT + 1
TOK = SEQ + NS
TPAD = NT * P
OFF_Q = S5W
N_QKV = NH * DH + 6 * KVW + 3 * NH
OFF_MIX = OFF_Q + N_QKV
HN = NH + 6
C_TANH = 0.7978845608028654
C_CUBE = 0.044715


class Chain:

    def __init__(self, eng, sem):
        self.eng, self.sem, self.n = eng, sem, 0

    def put(self, ins):
        ins.then_inc(self.sem, 1)
        self.n += 1

    def sync(self):
        self.eng.wait_ge(self.sem, self.n)

    def after(self, n):
        self.eng.wait_ge(self.sem, n)

    def __call__(self, ins):
        self.put(ins)
        self.sync()

    def restart(self):
        self.eng.sem_clear(self.sem)
        self.n = 0


class Semaphores:

    def __init__(self, nc, prefix):
        self.nc, self.prefix, self.held, self.stack = nc, prefix, [], ExitStack()

    def __enter__(self):
        return self

    def __call__(self, name):
        self.held.append(self.stack.enter_context(self.nc.semaphore(self.prefix + name)))
        return self.held[-1]

    def __exit__(self, *failure):
        if failure[0] is None:
            with self.nc.Block() as block:
                @block.sync
                def _(sp):
                    for s in self.held:
                        sp.sem_clear(s)
        self.stack.close()


def row(ap):
    return ap.rearrange("p a n -> p (a n)")


def token_tiles(eng, body):
    body(0, 0)
    body(1, 1)
    with eng.Fori(1, TT // 2) as i:
        for k in range(2):
            body(2 * i + k, k)
    body(TT, 0)


def behind(t, n):
    return not isinstance(t, int) or t >= n


def phase_project(nc, d, r):
    with ExitStack() as ctx:
        sb = lambda name, shape: ctx.enter_context(nc.sbuf_tensor(name, shape, F32))
        pb = lambda name, shape: ctx.enter_context(nc.psum_tensor(name, shape, F32))
        sem = ctx.enter_context(Semaphores(nc, "p_"))
        w_qkv = sb("w_qkv", [P, DT, N_QKV])
        mixw = sb("mixw", [P, DT])
        normw = sb("normw", [P, HN, DH])
        rope = sb("rope", [P, NT, 2, DH // 2])
        xt = [sb(f"xt{k}", [P, D]) for k in range(2)]
        xn = [sb(f"xn{k}", [P, D]) for k in range(2)]
        sq_junk = sb("sq_junk", [P, D])
        ssum = sb("ssum", [P, 2])
        rstd = sb("rstd", [P, 2])
        hs = [sb(f"hs{k}", [P, DT, P]) for k in range(2)]
        qk = [sb(f"qk{k}", [P, HN, DH]) for k in range(2)]
        roped = [sb(f"roped{k}", [P, HN, DH]) for k in range(2)]
        tmp = sb("tmp", [P, HN, DH])
        tmp2 = sb("tmp2", [P, HN, DH])
        hsum = sb("hsum", [P, HN])
        hrms = sb("hrms", [P, HN])
        rms = sb("rms", [P, 2])
        eps = sb("eps", [P, 1])
        k_nat = sb("k_nat", [P, NT, 3, KVW])
        xT_ps = pb("xT_ps", [P, DT, P])
        z_ps = pb("z_ps", [P, 3, 512])
        qT_ps = pb("qT_ps", [P, 8, P])

        w_ld = [sem(f"w_ld{c}") for c in range(DT)]
        c_ld = [sem(f"c_ld{c}") for c in range(6)]
        x_ld = [sem("x_ld0"), sem("x_ld1")]
        squared, xn_ready, xT_done, hs_ready = sem("squared"), sem("xn_ready"), sem("xT_done"), sem("hs_ready")
        hT_copied, z_done, z_evac = sem("hT_copied"), sem("z_done"), sem("z_evac")
        rope_done, k_copied, qT_done, qT_evac = sem("rope_done"), sem("k_copied"), sem("qT_done"), sem("qT_evac")
        x_rms, head_sums, head_rms, eps_set = sem("x_rms"), sem("head_sums"), sem("head_rms"), sem("eps_set")
        tanh_done, gates_ready = sem("tanh_done"), sem("gates_ready")
        ch_v, stored, copied = sem("ch_v"), sem("stored"), sem("copied")
        block = ctx.enter_context(nc.Block())
        hT, qkT, v_nat, gates, ident = r["hT"], r["qkT"], r["v_nat"], r["gates"], r["ident"]

        @block.sync
        def _(sp):
            x_p = d["x_prompt"].rearrange("a (t p) n -> (a t) p n", p=P)
            sp.dma_start(xt[0][:], x_p[0]).then_inc(x_ld[0], 16)
            sp.dma_start(xt[1][:], x_p[1]).then_inc(x_ld[1], 16)
            w = d["w_in"][0, :, OFF_Q:OFF_MIX].rearrange("(c p) n -> p c n", p=P)
            for c in range(DT):
                sp.dma_start(w_qkv[:, c, :], w[:, c, :]).then_inc(w_ld[c], 16)
            with sp.Fori(0, TT // 2 - 1) as i:
                for k in range(2):
                    sp.wait_ge(xn_ready, 2 * i + k + 1)
                    sp.dma_start(xt[k][:], x_p[ds(2 * i + k + 2, 1)].rearrange("t p n -> (t p) n")).then_inc(x_ld[k], 16)
            sp.wait_ge(xn_ready, TT - 1)
            sp.dma_start(xt[0][0:NS, :], d["x_sample"].rearrange("b t n -> (b t) n")).then_inc(x_ld[0], 16)
            sp.wait_ge(z_evac, 3 * NT)
            sp.wait_ge(k_copied, NT)
            n = 0
            flat = lambda name: d[name].rearrange("z a t h c -> (z a t) (h c)")
            for src, c, names in ((k_nat, 0, "k_cmp"), (v_nat, 0, "v_cmp"), (k_nat, 1, "k_slc"), (v_nat, 1, "v_slc")):
                sp.dma_start(flat(names + "_p").rearrange("(t p) c -> p t c", p=P), src[:, 0:TT, c, :]).then_inc(stored, 16)
                sp.dma_start(flat(names + "_s"), src[0:NS, TT, c, :]).then_inc(stored, 16)
                n += 2
            for src, names in ((k_nat, "k_win"), (v_nat, "v_win")):
                sp.dma_start(flat(names + "_p").rearrange("(t p) c -> p t c", p=P),
                             src[:, TT - WIN // P:TT, 2, :]).then_inc(stored, 16)
                new = d[names + "_s"].rearrange("z b w h c -> (z b) w (h c)")
                for b in range(NB):
                    sp.dma_start(new[b, WIN - TS:WIN, :], src[TS * b:TS * b + TS, TT, 2, :]).then_inc(stored, 16)
                    n += 1
                n += 1
            sp.dma_start(d["v_new"].rearrange("n (c w) -> n c w", c=2), v_nat[0:NS, TT, 1:3, :]).then_inc(stored, 16)
            sp.wait_ge(gates_ready, 1)
            sp.dma_start(d["g_new"], gates[0:NS, TT, :]).then_inc(stored, 16)
            sp.wait_ge(stored, 16 * (n + 2))

        @block.scalar
        def _(act):
            act.dma_start(mixw[:], d["norm_mix_w"].rearrange("z (c p) -> p (z c)", p=P),
                          allow_slow_non_contiguous=True).then_inc(c_ld[0], 16)
            act.dma_start(normw[:, 0:NH, :], d["normw_q"]).then_inc(c_ld[1], 16)
            for h in range(NKV):
                act.dma_start(normw[:, NH:HN, :].rearrange("p (b h) c -> p b h c", h=NKV)[:, :, h, :],
                              d["normw_k"]).then_inc(c_ld[4 + h], 16)
            act.dma_start(rope[:], d["rope"].rearrange("(t p) c f -> p t c f", p=P)).then_inc(c_ld[3], 16)
            act.dma_start(ident[:], d["identity"]).then_inc(c_ld[2], 16)
            for n, (state, out) in enumerate((("state_k_win", "k_win_s"), ("state_v_win", "v_win_s"))):
                keep = lambda ap, at: ap.rearrange("z b w h c -> (z b) w (h c)")[:, at:at + WIN - TS, :]
                act.dma_start(keep(d[out], 0), keep(d[state], TS)).then_inc(copied, 16)

            def evac(t, k):
                act.wait_ge(z_done, 3 * t + 1)
                if behind(t, 2):
                    act.wait_ge(rope_done, t - 1)
                pair = lambda ap: ap.rearrange("p (c w) -> p c w", w=KVW)
                act.activation(qk[k][:, 0:NH, :].rearrange("p (j g) c -> p g j c", g=NKV),
                               z_ps[:, 0, :].rearrange("p (g j c) -> p g j c", g=NKV, c=DH), ACT.Copy).then_inc(z_evac, 1)
                act.wait_ge(z_done, 3 * t + 2)
                kv = z_ps[:, 1, :].rearrange("p (b c w) -> p b c w", b=2, c=2)
                act.activation(qk[k][:, NH:NH + 4, :].rearrange("p (b h) c -> p b (h c)", b=2), kv[:, :, 0, :], ACT.Copy)
                v_at = v_nat[:, ds(t, 1), :, :].rearrange("p t c w -> p (t c) w")
                act.activation(v_at[:, 0:2, :], kv[:, :, 1, :], ACT.Copy).then_inc(z_evac, 1)
                act.wait_ge(z_done, 3 * t + 3)
                act.activation(qk[k][:, NH + 4:HN, :].rearrange("p h c -> p (h c)"), z_ps[:, 2, 0:KVW], ACT.Copy)
                act.activation(v_at[:, 2, :], z_ps[:, 2, KVW:2 * KVW], ACT.Copy)
                act.activation(row(gates[:, ds(t, 1), :]), z_ps[:, 2, 2 * KVW:2 * KVW + 3 * NH],
                               ACT.Copy).then_inc(z_evac, 1)

            def head_root(t):
                act.wait_ge(head_sums, t + 1)
                act.activation(hrms[:], hsum[:], ACT.Sqrt, bias=eps[:], scale=1.0 / DH).then_inc(head_rms, 1)

            def evac_qT(t, k):
                act.wait_ge(qT_done, t + 1)
                act.activation(qkT[:, 0:NG, ds(t * P, P)], qT_ps[:, 0:NG, :], ACT.Copy, scale=SCALE)
                act.activation(qkT[:, NG:NG + 2, ds(t * P, P)], qT_ps[:, NG:NG + 2, :], ACT.Copy).then_inc(qT_evac, 1)

            def square(t, k, turn):
                act.wait_ge(x_ld[k], 16 * turn + 16)
                if behind(t, 2):
                    act.wait_ge(xn_ready, t - 1)
                act.activation(sq_junk[:], xt[k][:], ACT.Square, accum_out=ssum[:, k:k + 1]).then_inc(squared, 1)
                act.wait_ge(squared, t + 1)
                act.activation(rms[:, k:k + 1], ssum[:, k:k + 1], ACT.Sqrt, bias=eps[:], scale=1.0 / D).then_inc(x_rms, 1)

            act.wait_ge(eps_set, 1)
            square(0, 0, 0)
            square(1, 1, 0)

            def body(t, k, turn):
                if not isinstance(t, int) or t + 2 < NT:
                    square(t + 2, k, turn + 1)
                if behind(t, 1):
                    head_root(t - 1)
                evac(t, k)
                if behind(t, 2):
                    evac_qT(t - 2, k)

            body(0, 0, 0)
            body(1, 1, 0)
            with act.Fori(1, TT // 2 - 1) as i:
                for k in range(2):
                    body(2 * i + k, k, i)
            for t in range(TT - 2, NT):
                body(t, t % 2, t // 2)
            head_root(TT)
            evac_qT(TT - 1, 1)
            evac_qT(TT, 0)
            act.wait_ge(z_evac, 3 * NT)
            act.activation(gates[:], gates[:], ACT.Tanh, scale=0.5).then_inc(tanh_done, 1)
            act.wait_ge(copied, 32)

        @block.vector
        def _(dve):
            link = Chain(dve, ch_v)
            dve.memset(eps[:], EPS).then_inc(eps_set, 1)
            for c in (0, 1, 3, 4, 5):
                dve.wait_ge(c_ld[c], 16)

            def normalise(t, k):
                dve.wait_ge(x_rms, t + 1)
                link(dve.reciprocal(rstd[:, k:k + 1], rms[:, k:k + 1]))
                if behind(t, 2):
                    dve.wait_ge(xT_done, t - 1)
                dve.tensor_scalar(xn[k][:], xt[k][:], rstd[:, k:k + 1], None, ALU.mult).then_inc(xn_ready, 1)

            def weigh(t, k):
                dve.wait_ge(xT_done, t + 1)
                if behind(t, 2):
                    dve.wait_ge(z_done, 3 * t - 3)
                    dve.wait_ge(hT_copied, t - 1)
                dve.tensor_tensor(hs[k][:], xT_ps[:], mixw[:].unsqueeze(2).to_broadcast([P, DT, P]),
                                  ALU.mult).then_inc(hs_ready, 1)

            def rotate(t, k):
                dve.wait_ge(z_evac, 3 * t + 3)
                q = qk[k]
                link(dve.tensor_tensor(tmp[:], q[:], q[:], ALU.mult))
                link(dve.tensor_reduce(hsum[:], tmp[:], X, ALU.add))
                dve.sem_inc(head_sums, 1)
                dve.wait_ge(head_rms, t + 1)
                link(dve.reciprocal(hsum[:], hrms[:]))
                link(dve.tensor_tensor(tmp[:], q[:], hsum[:].unsqueeze(2).to_broadcast([P, HN, DH]), ALU.mult))
                link(dve.tensor_tensor(tmp2[:], tmp[:], normw[:], ALU.mult))
                half = DH // 2
                cos = rope[:, ds(t, 1), 0, :].to_broadcast([P, HN, half])
                sin = rope[:, ds(t, 1), 1, :].to_broadcast([P, HN, half])
                link.put(dve.tensor_tensor(q[:, :, 0:half], tmp2[:, :, 0:half], cos, ALU.mult))
                link.put(dve.tensor_tensor(tmp[:, :, 0:half], tmp2[:, :, half:DH], sin, ALU.mult))
                link.put(dve.tensor_tensor(q[:, :, half:DH], tmp2[:, :, half:DH], cos, ALU.mult))
                link(dve.tensor_tensor(tmp[:, :, half:DH], tmp2[:, :, 0:half], sin, ALU.mult))
                if behind(t, 2):
                    dve.wait_ge(qT_done, t - 1)
                    dve.wait_ge(k_copied, t - 1)
                link.put(dve.tensor_tensor(roped[k][:, :, 0:half], q[:, :, 0:half], tmp[:, :, 0:half], ALU.subtract))
                link(dve.tensor_tensor(roped[k][:, :, half:DH], q[:, :, half:DH], tmp[:, :, half:DH], ALU.add))
                link.restart()
                dve.sem_inc(rope_done, 1)

            normalise(0, 0)
            weigh(0, 0)
            normalise(1, 1)

            def body(t, k):
                if not isinstance(t, int) or t + 1 < NT:
                    weigh(t + 1, 1 - k)
                if not isinstance(t, int) or t + 2 < NT:
                    normalise(t + 2, k)
                if behind(t, 1):
                    rotate(t - 1, 1 - k)

            body(0, 0)
            body(1, 1)
            with dve.Fori(1, TT // 2 - 1) as i:
                for k in range(2):
                    body(2 * i + k, k)
            for t in range(TT - 2, NT):
                body(t, t % 2)
            rotate(TT, 0)
            dve.wait_ge(tanh_done, 1)
            dve.tensor_scalar(gates[:], gates[:], 0.5, 0.5, ALU.mult, ALU.add).then_inc(gates_ready, 1)

        @block.gpsimd
        def _(pool):
            def body(t, k):
                pool.wait_ge(hs_ready, t + 1)
                pool.tensor_copy(hT[:, :, ds(t * P, P)], hs[k][:]).then_inc(hT_copied, 1)
                pool.wait_ge(rope_done, t + 1)
                pool.tensor_copy(k_nat[:, ds(t, 1), :, :].rearrange("p t c w -> p (t c w)"),
                                 roped[k][:, NH:HN, :].rearrange("p h c -> p (h c)")).then_inc(k_copied, 1)

            token_tiles(pool, body)

        @block.tensor
        def _(pe):
            def transpose_x(t, k):
                pe.wait_ge(xn_ready, t + 1)
                if behind(t, 1):
                    pe.wait_ge(hs_ready, t)
                for c in range(DT):
                    ins = pe.transpose(xT_ps[:, c, :], xn[k][:, c * P:(c + 1) * P], ident[:])
                ins.then_inc(xT_done, 1)

            def project(t, k):
                pe.wait_ge(hs_ready, t + 1)
                parts = ((0, 512), (512, 512), (1024, N_QKV - 1024))
                multiply = lambda b, c: pe.matmul(z_ps[:, b, 0:parts[b][1]], hs[k][:, c, :],
                                                  w_qkv[:, c, parts[b][0]:sum(parts[b])], start=(c == 0), stop=(c == DT - 1))
                if not behind(t, 1):
                    for c in range(DT):
                        pe.wait_ge(w_ld[c], 16)
                        for b in range(3):
                            ins = multiply(b, c)
                            if c == DT - 1:
                                ins.then_inc(z_done, 1)
                    return
                for b in range(3):
                    pe.wait_ge(z_evac, 3 * t - 2 + b)
                    for c in range(DT):
                        ins = multiply(b, c)
                    ins.then_inc(z_done, 1)

            def transpose_qk(t, k):
                pe.wait_ge(rope_done, t + 1)
                if behind(t, 1):
                    pe.wait_ge(qT_evac, t)
                for j in range(NG):
                    pe.transpose(qT_ps[:, j, :], roped[k][:, 2 * j:2 * j + 2, :].rearrange("p h c -> p (h c)"), ident[:])
                for j in range(2):
                    ins = pe.transpose(qT_ps[:, NG + j, :],
                                       roped[k][:, NH + 2 + 2 * j:NH + 4 + 2 * j, :].rearrange("p h c -> p (h c)"), ident[:])
                ins.then_inc(qT_done, 1)

            pe.wait_ge(c_ld[2], 16)
            transpose_x(0, 0)

            def body(t, k):
                if not isinstance(t, int) or t + 1 < NT:
                    transpose_x(t + 1, 1 - k)
                project(t, k)
                if behind(t, 2):
                    transpose_qk(t - 2, k)

            token_tiles(pe, body)
            transpose_qk(TT - 1, 1)
            transpose_qk(TT, 0)


CHUNKS = [(0, 384), (384, 384), (768, 320)]
assert sum(n for _, n in CHUNKS) == TOK


def phase_gemm(nc, name, weights, n_pairs, kt, src, act_step, dve_step=None):
    with ExitStack() as ctx:
        sem = ctx.enter_context(Semaphores(nc, name))
        w = [ctx.enter_context(nc.sbuf_tensor(f"{name}_w{k}", [P, kt, 256], F32)) for k in range(2)]
        ps = [ctx.enter_context(nc.psum_tensor(f"{name}_ps{f}", [P, 3, 512], F32)) for f in range(2)]
        w_ld = [sem("w_ld0"), sem("w_ld1")]
        multiplied, taken, finished, ch_v = sem("multiplied"), sem("taken"), sem("finished"), sem("ch_v")
        block = ctx.enter_context(nc.Block())

        @block.sync
        def _(sp):
            for k in range(2):
                sp.dma_start(w[k][:], weights(k)).then_inc(w_ld[k], 16)
            if n_pairs > 1:
                with sp.Fori(0, n_pairs - 1) as i:
                    for k in range(2):
                        sp.wait_ge(multiplied, 4 * i + 2 * k + 2)
                        sp.dma_start(w[k][:], weights(2 * i + k + 2)).then_inc(w_ld[k], 16)

        def turns(eng, body):
            for k in range(2):
                for f in range(2):
                    body(0, k, f, k == 0)
            if n_pairs > 1:
                with eng.Fori(1, n_pairs) as i:
                    for k in range(2):
                        for f in range(2):
                            body(i, k, f, False)

        @block.tensor
        def _(pe):
            def body(i, k, f, first):
                if f == 0:
                    pe.wait_ge(w_ld[k], 16 * i + 16)
                if not first:
                    pe.wait_ge(taken, 4 * i + 2 * k + f - 1)
                for c in range(kt):
                    for b, (at, n) in enumerate(CHUNKS):
                        ins = pe.matmul(ps[f][:, b, 0:n], w[k][:, c, f * P:(f + 1) * P], src[:, c, at:at + n],
                                        start=(c == 0), stop=(c == kt - 1))
                ins.then_inc(multiplied, 1)

            turns(pe, body)

        @block.scalar
        def _(act):
            def body(i, k, f, first):
                act.wait_ge(multiplied, 4 * i + 2 * k + f + 1)
                ft = 4 * i + 2 * k + f
                for c, (at, n) in enumerate(CHUNKS):
                    ins = act_step(act, ft, c, at, n, ps[f][:, c, 0:n])
                ins.then_inc(taken, 1)

            turns(act, body)

        if dve_step is not None:
            @block.vector
            def _(dve):
                link = Chain(dve, ch_v)

                def body(i, k, f, first):
                    dve.wait_ge(taken, 4 * i + 2 * k + f + 1)
                    for c, (at, n) in enumerate(CHUNKS):
                        dve_step(dve, 4 * i + 2 * k + f, c, at, n, link)
                    link.restart()

                turns(dve, body)


ST = S5G * S5P // P
FT = S5W // P
SJ = ST // FT
LB = 256
ROUND = 12582912.0
TWO_PI_HI, TWO_PI_LO = 6.28125, 0.0019353071795864769
NEARLY_PI = 3.1415925


def phase_s5(nc, d, r):
    with ExitStack() as ctx:
        sb = lambda name, shape: ctx.enter_context(nc.sbuf_tensor("s5_" + name, shape, F32))
        pb = lambda name, shape: ctx.enter_context(nc.psum_tensor("s5_" + name, shape, F32))
        sem = ctx.enter_context(Semaphores(nc, "s5_"))
        uT, yT, ident, hT = r["uT"], r["yT"], r["ident"], r["hT"]
        ldt = sb("ldt", [ST, 2])
        dt = sb("dt", [ST, 2])
        prm = sb("prm", [P, 5, ST])
        bz = sb("bz", [P, 2, P])
        bbT = sb("bbT", [P, 2, ST, P])
        cz = sb("cz", [P, 2, ST, 2, S5H])
        rot = sb("rot", [P, 2, ST, LB])
        dvec = sb("dvec", [P, FT])
        snat = sb("snat", [P, 2, P])
        state = sb("state", [P, 2, NB, ST])
        bbs = sb("bbs", [P, 2, SJ, P])
        czs = sb("czs", [P, 3, SJ, 2 * S5H])
        pms = sb("pms", [P, 5, SJ])
        m_row = sb("m_row", [P, LB])
        m9 = sb("m9", [P, NB, TS + 1])
        ones9 = sb("ones9", [P, NB, TS + 1])
        t4 = sb("t4", [P, 4, 2, LB])
        yin = sb("yin", [P, 2, 2, 2, LB])
        yout = sb("yout", [P, 2, 2, 2, LB])
        xs = sb("xs", [P, 2, 4, 2, LB])
        flatten = lambda t, dims: t[:].rearrange(dims)
        bnat = flatten(yin, "p k q b n -> p (k q b n)")[:, 0:2 * ST * S5H].rearrange("p (c t h) -> p c t h", c=2, h=S5H)
        bt = flatten(yout, "p k q b n -> p (k q b n)")[:, 0:1024].rearrange("p (c t h) -> p c t h", c=4, h=S5H)
        cnat = flatten(t4, "p q b n -> p (q b n)")[:, 0:2 * FT * P].rearrange("p (c f k q) -> p c f k q", c=2, f=FT, k=2)
        rt = flatten(xs, "p c q b n -> p (c q b n)")[:, 0:ST * P].rearrange("p (t n) -> p t n", t=ST)
        small = flatten(xs, "p c q b n -> p (c q b n)")[0:ST, ST * P:2 * ST * P].rearrange("t (n q) -> t n q", q=P)
        lam, ab, pk = small[:, 0:2, :], small[:, 2:4, :], small[:, 4:9, :]
        th, ldm, turns, cosarg, den, s1, s2 = (small[:, n, :] for n in range(9, 16))
        e4 = sb("e4", [P, 2])
        carry = sb("carry", [P, 2])
        in9 = sb("in9", [P, 2, NB, TS + 1])
        out9 = sb("out9", [P, 2, NB, TS + 1])
        q4 = sb("q4", [P, 4, NB, TS])
        x9 = sb("x9", [P, 2, NB, TS])
        r4 = sb("r4", [P, 4, NB, TS])
        fin_p = sb("fin_p", [P, 2, ST])
        fin_s = sb("fin_s", [P, 2, NB, ST])
        fo_p = sb("fo_p", [ST, 2, P])
        fo_s = sb("fo_s", [P, 2, P])
        bu = [pb(f"bu{k}", [P, 2, 512]) for k in range(2)]
        bus = pb("bus", [P, 2, NS])
        y_ps = pb("y_ps", [P, 3, 512])

        w_u = bbT[:].rearrange("p c s n -> p (c s n)").rearrange("p (k c n) -> p k c n", k=2, c=DT)
        u_ps = [[bu[0][:, 0, :], bu[0][:, 1, :], bu[1][:, 0, :]], [bu[1][:, 1, :], y_ps[:, 1, :], y_ps[:, 2, :]]]
        assert 2 * DT * 256 == 2 * ST * P and FT == 4
        wu_ld, u_done, u_taken = [sem("wu_ld0"), sem("wu_ld1")], sem("u_done"), sem("u_taken")

        ld = [sem(f"ld{n}") for n in range(11)]
        a_dt, a_th, a_mag, a_sin = sem("a_dt"), sem("a_th"), sem("a_mag"), sem("a_sin")
        pk_set, pkT, prm_set, bz_set, bzT, bbT_set = (sem(n) for n in ("pk_set", "pkT", "prm_set", "bz_set", "bzT", "bbT_set"))
        cT, cz_set, sT, s_set = sem("cT"), sem("cz_set"), sem("sT"), sem("s_set")
        staged, bu_done, bu_used, bus_done, bus_used = (sem(n) for n in ("staged", "bu_done", "bu_used", "bus_done", "bus_used"))
        x_ready, x_used, x9_ready, y_done, y_used = (sem(n) for n in ("x_ready", "x_used", "x9_ready", "y_done", "y_used"))
        fin_set, finT, fo_set, stored, ch_v = (sem(n) for n in ("fin_set", "finT", "fo_set", "stored", "ch_v"))
        scanned, scanned9, ch_g = sem("scanned"), sem("scanned9"), sem("ch_g")
        block = ctx.enter_context(nc.Block())

        @block.sync
        def _(sp):
            tile = lambda ap: ap.rearrange("z (t g) q -> (z t) (g q)", g=2)
            sp.dma_start(lam[:, 0, :], tile(d["s5_lam_re"])).then_inc(ld[0], 16)
            sp.dma_start(lam[:, 1, :], tile(d["s5_lam_im"])).then_inc(ld[1], 16)
            sp.dma_start(ldt[:], d["s5_log_dt"].rearrange("z (t g) -> (z t) g", g=2)).then_inc(ld[2], 16)
            for k in range(2):
                sp.dma_start(w_u[:, k], d["w_in"][0, :, 256 * k:256 * k + 256].rearrange("(c p) n -> p c n", p=P)).then_inc(wu_ld[k], 16)
            for n, name in enumerate(("s5_b_re", "s5_b_im")):
                sp.dma_start(bnat[:, n, :, :], bass.AP(d[name].tensor, 0, [(S5H, P), (P * S5H, ST), (1, S5H)])).then_inc(ld[3 + n], 16)
            for n, name in enumerate(("s5_c_re", "s5_c_im")):
                c = d[name].rearrange("z g h q -> (z g h) q").rearrange("(f p) q -> p f q", p=P)
                for k in range(2):
                    sp.dma_start(cnat[:, n, :, k, :], c).then_inc(ld[5 + n], 16)
            sp.dma_start(dvec[:], d["s5_d"].rearrange("z (f p) -> p (z f)", p=P), allow_slow_non_contiguous=True).then_inc(ld[7], 16)
            for n, name in enumerate(("state_s5_re", "state_s5_im")):
                sp.dma_start(snat[:, n, :], d[name].rearrange("z b (t g) q -> (z b t) (g q)", g=2)).then_inc(ld[8 + n], 16)
            sp.wait_ge(fo_set, 4)
            for n, name in enumerate(("s5_re", "s5_im")):
                sp.dma_start(d[name + "_p"].rearrange("z b (t g) q -> (z b t) (g q)", g=2), fo_p[:, n, :]).then_inc(stored, 16)
                sp.dma_start(d[name + "_s"].rearrange("z b (t g) q -> (z b t) (g q)", g=2), fo_s[:, n, :]).then_inc(stored, 16)
            sp.wait_ge(stored, 64)

        @block.scalar
        def _(act):
            act.wait_ge(ld[2], 16)
            act.activation(dt[:], ldt[:], ACT.Exp).then_inc(a_dt, 1)
            act.wait_ge(a_th, 1)
            act.activation(pk[:, 0, :], ldm[:], ACT.Exp).then_inc(a_mag, 1)
            act.wait_ge(a_th, 2)
            act.activation(pk[:, 1, :], cosarg[:], ACT.Sin).then_inc(a_sin, 1)
            act.activation(pk[:, 2, :], th[:], ACT.Sin).then_inc(a_sin, 1)
            for f in range(FT):
                act.wait_ge(u_done, f + 1)
                for c, (at, n) in enumerate(CHUNKS):
                    ins = act.activation(uT[:, f, at:at + n], u_ps[f % 2][c][:, 0:n], ACT.Copy)
                ins.then_inc(u_taken, 1)
            for s in range(ST):
                act.wait_ge(bzT, s + 1)
                act.activation(bbT[:, :, s, :], bu[s % 2][:, :, 0:P], ACT.Copy).then_inc(bbT_set, 1)
            act.wait_ge(sT, 1)
            act.activation(state[:].rearrange("p c b t -> p c (b t)"), y_ps[:, 0, 0:2 * P].rearrange("p (c n) -> p c n", c=2),
                           ACT.Copy).then_inc(s_set, 1)
            act.wait_ge(bbT_set, ST)
            act.wait_ge(cz_set, 4)
            act.wait_ge(prm_set, 1)

            def stage(i, first):
                if not first:
                    act.wait_ge(y_done, i)
                    act.wait_ge(y_used, i)
                act.activation(bbs[:], bbT[:, :, ds(SJ * i, SJ), :], ACT.Copy)
                act.activation(czs[:, 0:2], cz[:, :, ds(SJ * i, SJ), :, :].rearrange("p c j g h -> p c j (g h)"), ACT.Copy)
                act.activation(czs[:, 2], cz[:, 0, ds(SJ * i, SJ), :, :].rearrange("p j g h -> p j (g h)"), ACT.Copy, scale=-1.0)
                act.activation(pms[:], prm[:, :, ds(SJ * i, SJ)], ACT.Copy).then_inc(staged, 1)

            stage(0, True)
            with act.Fori(1, FT) as i:
                stage(i, False)

        @block.vector
        def _(dve):
            link = Chain(dve, ch_v)
            tt = dve.tensor_tensor
            for n in range(3):
                dve.wait_ge(ld[n], 16)
            dve.wait_ge(a_dt, 1)
            half = lambda ap: ap.rearrange("t (g q) -> t g q", g=2)
            dtb = dt[:].unsqueeze(2).to_broadcast([ST, 2, S5P])
            lr, li = lam[:, 0, :], lam[:, 1, :]
            link(tt(half(ldm[:]), half(lr), dtb, ALU.mult))
            dve.sem_inc(a_th, 1)
            link(tt(half(th[:]), half(li), dtb, ALU.mult))
            link(dve.tensor_scalar(turns[:], th[:], float(1 / (2 * np.pi)), ROUND, ALU.mult, ALU.add))
            link(dve.tensor_scalar(turns[:], turns[:], -ROUND, None, ALU.add))
            link(dve.scalar_tensor_tensor(th[:], turns[:], -TWO_PI_HI, th[:], ALU.mult, ALU.add))
            link(dve.scalar_tensor_tensor(th[:], turns[:], -TWO_PI_LO, th[:], ALU.mult, ALU.add))
            link(dve.tensor_scalar(th[:], th[:], NEARLY_PI, -NEARLY_PI, ALU.min, ALU.max))
            link(dve.scalar_tensor_tensor(cosarg[:], th[:], -1.0, th[:], ALU.mult, ALU.max))
            link(dve.tensor_scalar(cosarg[:], cosarg[:], -1.0, float(np.pi / 2), ALU.mult, ALU.add))
            dve.sem_inc(a_th, 1)
            dve.wait_ge(a_mag, 1)
            dve.wait_ge(a_sin, 2)
            link(tt(ab[:, 0, :], pk[:, 0, :], pk[:, 1, :], ALU.mult))
            link(tt(ab[:, 1, :], pk[:, 0, :], pk[:, 2, :], ALU.mult))
            link(tt(s1[:], lr, lr, ALU.mult))
            link(tt(s2[:], li, li, ALU.mult))
            link(tt(den[:], s1[:], s2[:], ALU.add))
            link(dve.reciprocal(den[:], den[:]))
            link(dve.tensor_scalar(ab[:, 0, :], ab[:, 0, :], -1.0, None, ALU.add))
            link(tt(s1[:], ab[:, 0, :], lr, ALU.mult))
            link(tt(s2[:], ab[:, 1, :], li, ALU.mult))
            link(tt(s1[:], s1[:], s2[:], ALU.add))
            link(tt(pk[:, 3, :], s1[:], den[:], ALU.mult))
            link(tt(s1[:], ab[:, 1, :], lr, ALU.mult))
            link(tt(s2[:], ab[:, 0, :], li, ALU.mult))
            link(tt(s1[:], s1[:], s2[:], ALU.subtract))
            link(tt(pk[:, 4, :], s1[:], den[:], ALU.mult))
            dve.sem_inc(pk_set, 1)
            dve.wait_ge(pkT, 1)
            link(dve.tensor_copy(prm[:], y_ps[:, 0, 0:5 * ST].rearrange("p (c t) -> p c t", c=5)))
            dve.sem_inc(prm_set, 1)
            dve.wait_ge(ld[3], 16)
            dve.wait_ge(ld[4], 16)
            fb = lambda n: prm[:, 3 + n, :].unsqueeze(2).to_broadcast([P, ST, S5H])
            link.put(tt(bt[:, 0], bnat[:, 0], fb(0), ALU.mult))
            link.put(tt(bt[:, 1], bnat[:, 1], fb(1), ALU.mult))
            link.put(tt(bt[:, 2], bnat[:, 1], fb(0), ALU.mult))
            link(tt(bt[:, 3], bnat[:, 0], fb(1), ALU.mult))
            link.put(tt(bt[:, 0], bt[:, 0], bt[:, 1], ALU.subtract))
            link(tt(bt[:, 2], bt[:, 2], bt[:, 3], ALU.add))
            link(dve.tensor_copy(rot[:, 0, :, 0:1], prm[:, 1, :].unsqueeze(2)))
            link(dve.tensor_copy(rot[:, 1, :, 0:1], prm[:, 2, :].unsqueeze(2)))
            n = 1
            while n < LB:
                co, si = rot[:, 0, :, 0:n], rot[:, 1, :, 0:n]
                cn = rot[:, 0, :, n - 1:n].to_broadcast([P, ST, n])
                sn = rot[:, 1, :, n - 1:n].to_broadcast([P, ST, n])
                link.put(tt(rot[:, 0, :, n:2 * n], co, cn, ALU.mult))
                link(tt(rt[:, :, 0:n], si, sn, ALU.mult))
                link(tt(rot[:, 0, :, n:2 * n], rot[:, 0, :, n:2 * n], rt[:, :, 0:n], ALU.subtract))
                link.put(tt(rot[:, 1, :, n:2 * n], si, cn, ALU.mult))
                link(tt(rt[:, :, 0:n], co, sn, ALU.mult))
                link(tt(rot[:, 1, :, n:2 * n], rot[:, 1, :, n:2 * n], rt[:, :, 0:n], ALU.add))
                n *= 2
            for s in range(ST):
                if s:
                    dve.wait_ge(bzT, s)
                link(dve.memset(bz[:], 0.0))
                at = s % SJ * 2 * S5H
                for g in range(2):
                    link.put(dve.tensor_copy(bz[g * S5P:(g + 1) * S5P, :, at + g * S5H:at + (g + 1) * S5H],
                                             bt[g * S5P:(g + 1) * S5P, 0:4:2, s, :]))
                link.sync()
                dve.sem_inc(bz_set, 1)
            link(dve.memset(cz[:], 0.0))
            dve.wait_ge(cT, 1)
            for n in range(2):
                for g in range(2):
                    rows = slice(g * S5P, (g + 1) * S5P)
                    src = bu[n][rows, 0, :].rearrange("p (s g h) -> p s g h", g=2, h=S5H)[:, :, g, :]
                    dve.tensor_scalar(cz[rows, n, :, g, :], src, 1.0 - 2.0 * n, None, ALU.mult).then_inc(cz_set, 1)
            link(dve.memset(ones9[:], 1.0))
            link(dve.memset(ones9[:, :, 0:1], 0.0))
            dve.wait_ge(ld[7], 16)
            dve.wait_ge(s_set, 1)
            link.restart()

            with dve.Fori(0, FT) as i:
                dve.wait_ge(staged, i + 1)
                for j in range(SJ):
                    s = SJ * i + j
                    m = pms[:, 0, j:j + 1]
                    table = lambda c, n, reps: rot[:, c, ds(s, 1), 0:n].to_broadcast([P, reps, n])
                    link.put(dve.tensor_scalar(m_row[:], rot[:, 0, ds(s, 1), :].rearrange("p a n -> p (a n)"), 0.0, m, ALU.mult, ALU.add))
                    link.put(dve.memset(carry[:], 0.0))
                    end = [row(rot[:, c, ds(s, 1), LB - 1:LB]) for c in range(2)]
                    b = bus[:].rearrange("p c (b t) -> p c b t", t=TS)
                    flat = lambda ap: ap.rearrange("p b t -> p (b t)")

                    def products(c, half):
                        part = lambda n: bu[c][:, n, :].rearrange("p (b n) -> p b n", n=LB)
                        if half == 0:
                            dve.wait_ge(bu_done, 8 * i + 2 * j + c + 1)
                            link.put(tt(t4[:, 0], part(0), table(0, LB, 2), ALU.mult))
                            link.put(tt(t4[:, 1], part(1), table(1, LB, 2), ALU.mult))
                        else:
                            link.put(tt(t4[:, 2], part(1), table(0, LB, 2), ALU.mult))
                            link.put(tt(t4[:, 3], part(0), table(1, LB, 2), ALU.mult))

                    def sums(c):
                        link.put(tt(yin[:, c, 0], t4[:, 0], t4[:, 1], ALU.add))
                        link.put(tt(yin[:, c, 1], t4[:, 2], t4[:, 3], ALU.subtract))

                    def scans(c, blk):
                        for q in range(2):
                            link.put(dve.tensor_tensor_scan(yout[:, c, q, blk, :], m_row[:], yin[:, c, q, blk, :],
                                                            carry[:, q:q + 1], ALU.mult, ALU.add))

                    def seam(c, blk, first):
                        ye = [yout[:, c, q, blk, LB - 1:LB] for q in range(2)]
                        if first:
                            link.put(tt(e4[:, 0:1], ye[1], end[1], ALU.mult))
                            link.put(tt(e4[:, 1:2], ye[1], end[0], ALU.mult))
                        else:
                            link.put(dve.scalar_tensor_tensor(carry[:, 0:1], ye[0], end[0], e4[:, 0:1], ALU.mult, ALU.subtract))
                            link.put(dve.scalar_tensor_tensor(carry[:, 1:2], ye[0], end[1], e4[:, 1:2], ALU.mult, ALU.add))

                    products(0, 0)
                    products(0, 1)
                    link.put(dve.tensor_scalar(m9[:], ones9[:], m, None, ALU.mult))
                    link.put(dve.tensor_copy(in9[:, :, :, 0:1], state[:, :, :, ds(s, 1)]))
                    link.after(link.n - 2)
                    dve.sem_inc(bu_used, 1)
                    sums(0)
                    if j:
                        dve.wait_ge(x_ready, 8 * i + 2 * j - 1)
                    link.sync()
                    scans(0, 0)
                    products(1, 0)
                    link.after(link.n - 2)
                    seam(0, 0, True)
                    products(1, 1)
                    link.after(link.n - 2)
                    seam(0, 0, False)
                    link.after(link.n - 2)
                    dve.sem_inc(bu_used, 1)
                    sums(1)
                    link.after(link.n - 2)
                    scans(0, 1)
                    dve.wait_ge(bus_done, s + 1)
                    for n, (part, t) in enumerate(((0, 0), (1, 1), (1, 0), (0, 1))):
                        link.put(tt(q4[:, n], b[:, part], table(t, TS, NB), ALU.mult))
                    link.after(link.n - 4)
                    dve.sem_inc(scanned, 1)
                    seam(0, 1, True)
                    link.after(link.n - 2)
                    dve.sem_inc(bus_used, 1)
                    link.put(tt(in9[:, 0, :, 1:TS + 1], q4[:, 0], q4[:, 1], ALU.add))
                    link.put(tt(in9[:, 1, :, 1:TS + 1], q4[:, 2], q4[:, 3], ALU.subtract))
                    link.after(link.n - 2)
                    seam(0, 1, False)
                    if j:
                        dve.wait_ge(x_ready, 8 * i + 2 * j)
                        dve.wait_ge(x9_ready, s)
                    link.after(link.n - 2)
                    for q in range(2):
                        link.put(dve.tensor_tensor_scan(flat(out9[:, q]), flat(m9[:]), flat(in9[:, q]), 0.0, ALU.mult, ALU.add))
                    link.after(link.n - 2)
                    scans(1, 0)
                    link.after(link.n - 2)
                    dve.sem_inc(scanned9, 1)
                    link.sync()
                    seam(1, 0, True)
                    link.sync()
                    seam(1, 0, False)
                    link.sync()
                    scans(1, 1)
                    link.sync()
                    dve.sem_inc(scanned, 1)
                    seam(1, 1, True)
                    link.sync()
                    seam(1, 1, False)
                    link.sync()
                    link(dve.tensor_copy(fin_p[:, :, ds(s, 1)], carry[:].unsqueeze(2)))
                dve.wait_ge(y_done, i + 1)
                for at, n, c in ((0, 512, 0), (512, 512, 1), (SEQ, NS, 2)):
                    link.put(dve.scalar_tensor_tensor(row(yT[:, ds(i, 1), at:at + n]), row(uT[:, ds(i, 1), at:at + n]),
                                                      row(dvec[:, ds(i, 1)].unsqueeze(2)), y_ps[:, c, 0:n], ALU.mult, ALU.add))
                link.sync()
                link.restart()
                dve.sem_inc(y_used, 1)
            dve.sem_inc(fin_set, 1)
            dve.wait_ge(finT, 1)
            for n in range(2):
                dve.tensor_copy(fo_p[:, n, :], y_ps[0:ST, 0, n * P:(n + 1) * P]).then_inc(fo_set, 1)
                dve.tensor_copy(fo_s[:, n, :], y_ps[:, 1, n * P:(n + 1) * P]).then_inc(fo_set, 1)

        @block.gpsimd
        def _(pool):
            link = Chain(pool, ch_g)
            tt = pool.tensor_tensor
            with pool.Fori(0, FT) as i:
                for j in range(SJ):
                    s = SJ * i + j
                    table = lambda c, n, reps: rot[:, c, ds(s, 1), 0:n].to_broadcast([P, reps, n])
                    def products(c):
                        turn = 8 * i + 2 * j + c
                        pool.wait_ge(scanned, turn + 1)
                        if j:
                            pool.wait_ge(x_used, turn - 1)
                        pool.nop(nofuse=True)
                        for n, (part, t) in enumerate(((0, 0), (1, 1), (0, 1), (1, 0))):
                            ins = tt(xs[:, c, n], yout[:, c, part], table(t, LB, 2), ALU.mult)
                        ins.then_inc(x_ready, 1)

                    products(0)
                    pool.wait_ge(scanned9, s + 1)
                    pool.wait_ge(x_used, 8 * i + 2 * j + 1)
                    pool.nop(nofuse=True)
                    for n, (part, t) in enumerate(((0, 0), (1, 1), (0, 1), (1, 0))):
                        link.put(tt(r4[:, n], out9[:, part, :, 1:TS + 1], table(t, TS, NB), ALU.mult))
                    link.sync()
                    link.put(tt(x9[:, 0], r4[:, 0], r4[:, 1], ALU.subtract))
                    link(tt(x9[:, 1], r4[:, 2], r4[:, 3], ALU.add))
                    link(pool.tensor_copy(fin_s[:, :, :, ds(s, 1)], x9[:, :, :, TS - 1:TS]))
                    pool.sem_inc(x9_ready, 1)
                    products(1)
                link.restart()

        @block.tensor
        def _(pe):
            for f in range(FT):
                if f == 1:
                    pe.wait_ge(pk_set, 1)
                    for n in range(5):
                        ins = pe.transpose(y_ps[:, 0, n * ST:(n + 1) * ST], pk[:, n, :], ident[0:ST, 0:ST])
                    ins.then_inc(pkT, 1)
                if f % 2 == 0:
                    pe.wait_ge(wu_ld[f // 2], 16)
                if f > 1:
                    pe.wait_ge(u_taken, f - 1)
                for c in range(DT):
                    for b, (at, n) in enumerate(CHUNKS):
                        ins = pe.matmul(u_ps[f % 2][b][:, 0:n], w_u[:, f // 2, c, f % 2 * P:(f % 2 + 1) * P],
                                        hT[:, c, at:at + n], start=(c == 0), stop=(c == DT - 1))
                ins.then_inc(u_done, 1)
            pe.wait_ge(u_taken, FT)
            for s in range(ST):
                pe.wait_ge(bz_set, s + 1)
                if s > 1:
                    pe.wait_ge(bbT_set, s - 1)
                for n in range(2):
                    ins = pe.transpose(bu[s % 2][:, n, 0:P], bz[:, n, :], ident[:])
                ins.then_inc(bzT, 1)
            for n in range(2):
                pe.wait_ge(ld[5 + n], 32)
                pe.wait_ge(bbT_set, ST)
                for f in range(FT):
                    ins = pe.transpose(bu[n][:, 0, f * P:(f + 1) * P], cnat[:, n, f, :, :].rearrange("p k q -> p (k q)"), ident[:])
            ins.then_inc(cT, 1)
            pe.wait_ge(prm_set, 1)
            for n in range(2):
                pe.wait_ge(ld[8 + n], 16)
                ins = pe.transpose(y_ps[:, 0, n * P:(n + 1) * P], snat[:, n, :], ident[:])
            ins.then_inc(sT, 1)
            pe.wait_ge(s_set, 1)
            pe.wait_ge(cz_set, 4)

            def feature_tile(i, first):
                pe.wait_ge(staged, i + 1)

                def inputs(j, c):
                    if c < 2:
                        if not (first and j == 0):
                            pe.wait_ge(bu_used, 8 * i + 2 * j + c - 1)
                        for n in range(2):
                            ins = pe.matmul(bu[c][:, n, :], bbs[:, n, j, :], row(uT[:, ds(i, 1), c * 512:(c + 1) * 512]),
                                            start=True, stop=True)
                        ins.then_inc(bu_done, 1)
                    else:
                        if not (first and j == 0):
                            pe.wait_ge(bus_used, SJ * i + j)
                        for n in range(2):
                            ins = pe.matmul(bus[:, n, :], bbs[:, n, j, :], row(uT[:, ds(i, 1), SEQ:TOK]), start=True, stop=True)
                        ins.then_inc(bus_done, 1)

                for c in range(3):
                    inputs(0, c)
                for j in range(SJ):
                    if j + 1 < SJ:
                        inputs(j + 1, 0)
                    rows = slice(32 * j, 32 * j + 32)
                    for c in range(3):
                        if c < 2:
                            pe.wait_ge(x_ready, 8 * i + 2 * j + c + 1)
                        else:
                            pe.wait_ge(x9_ready, SJ * i + j + 1)
                        if not first and j == 0 and c == 0:
                            pe.wait_ge(y_used, i)
                        n = 512 if c < 2 else NS
                        if c < 2:
                            terms = [(q, xs[:, c, k, :, :].rearrange("p b n -> p (b n)")) for k, q in enumerate((0, 2, 1, 1))]
                        else:
                            terms = [(q, x9[:, q, :, :].rearrange("p b t -> p (b t)")) for q in range(2)]
                        for k, (q, x) in enumerate(terms):
                            ins = pe.matmul(y_ps[rows, c, 0:n], czs[:, q, j, :], x, start=(k == 0), stop=(k == len(terms) - 1))
                        if c < 2:
                            ins.then_inc(x_used, 1)
                        elif j == SJ - 1:
                            ins.then_inc(y_done, 1)
                        if c == 0 and j + 1 < SJ:
                            inputs(j + 1, 1)
                            inputs(j + 1, 2)

            feature_tile(0, True)
            with pe.Fori(1, FT) as i:
                feature_tile(i, False)
            pe.wait_ge(fin_set, 1)
            for n in range(2):
                pe.transpose(y_ps[0:ST, 0, n * P:(n + 1) * P], fin_p[:, n, :], ident[:])
                ins = pe.transpose(y_ps[:, 1, n * P:(n + 1) * P], fin_s[:, n, :, :].rearrange("p b t -> p (b t)"), ident[:])
            ins.then_inc(finT, 1)


class Gelu:

    def __init__(self, nc, sem, yT, free_at):
        self.yT = yT
        self.sq = nc.alloc_sbuf_tensor_at("ge_sq", [P, FT, TOK], F32, offset=free_at)
        self.squared, self.inner, self.tanhed, self.done, self.half = (sem(n) for n in ("ge_sq", "ge_in", "ge_th", "ge_out", "ge_half"))

    def scalar(self, act):
        sq, yT = self.sq, self.yT
        for f in range(FT):
            act.activation(sq[:, f, :], yT[:, f, 0:TOK], ACT.Square).then_inc(self.squared, 1)
        for f in range(FT):
            act.wait_ge(self.inner, f + 1)
            act.activation(sq[:, f, :], sq[:, f, :], ACT.Tanh, scale=C_TANH).then_inc(self.tanhed, 1)
        for f in range(FT):
            act.wait_ge(self.done, f + 1)
            act.activation(yT[:, f, 0:TOK], yT[:, f, 0:TOK], ACT.Copy, scale=0.5).then_inc(self.half, 1)

    def vector(self, dve, link):
        sq, yT = self.sq, self.yT
        for f in range(FT):
            dve.wait_ge(self.squared, f + 1)
            link(dve.tensor_scalar(sq[:, f, :], sq[:, f, :], C_CUBE, 1.0, ALU.mult, ALU.add))
            dve.tensor_tensor(sq[:, f, :], sq[:, f, :], yT[:, f, 0:TOK], ALU.mult).then_inc(self.inner, 1)
        for f in range(FT):
            dve.wait_ge(self.tanhed, f + 1)
            dve.scalar_tensor_tensor(yT[:, f, 0:TOK], sq[:, f, :], 1.0, yT[:, f, 0:TOK], ALU.add, ALU.mult).then_inc(self.done, 1)


LP = CL // 2
NC_S = (PAST + TS - CL) // CS + 1
NC_P = (SEQ - CL) // CS + 1
NCP = 2 * P
GT = NKV * TS
MR = NH * TS


def phase_compress(nc, d, r):
    with ExitStack() as ctx:
        sb = lambda name, shape, dt=F32: ctx.enter_context(nc.sbuf_tensor("c_" + name, shape, dt))
        pb = lambda name, shape: ctx.enter_context(nc.psum_tensor("c_" + name + "_ps", shape, F32))
        sem = ctx.enter_context(Semaphores(nc, "c_"))
        ident, qkT, qbd, g_rows, osum, sel_bias = (r[n] for n in ("ident", "qkT", "qbd", "g_rows", "osum", "sel_bias"))
        w1 = sb("w1", [P, 2, LP, CH])
        w2 = sb("w2", [P, 2, DH])
        pe_nat = sb("pe_nat", [LP, 2, P])
        peT = sb("peT", [P, 2, LP])
        hbias = sb("hbias", [P, 2])
        pages = sb("pages", [P, 2 * NB], I32)
        in_page = sb("in_page", [P, 1], I32)
        rows_of = sb("rows_of", [P, 2 * NB], I32)
        row_now = sb("row_now", [P, 4], I32)
        gsum = sb("gsum", [MR, GT])
        gspread = sb("gspread", [GT, MR])
        x = [sb(f"x{s}", [P, CS * KVW]) for s in range(4)]
        xT = [sb(f"xT{v}", [P, CS // 2, 2, NCP]) for v in range(2)]
        xb = [sb(f"xb{v}", [P, 2, NC_S]) for v in range(2)]
        sq = [sb(f"sq{v}", [P, 2, NC_S]) for v in range(2)]
        g = [sb(f"g{v}", [P, 2, NC_S]) for v in range(2)]
        kc = sb("kc", [P, NC_S])
        vc = sb("vc", [P, 2, KVW])
        qs = sb("qs", [P, MR])
        prob = sb("prob", [MR, NC_S])
        stat = sb("stat", [MR, 4])
        pT = sb("pT", [P, 2, MR])
        pg = sb("pg", [GT, 4 * NSLC + 1])
        imp = sb("imp", [GT, NSLC - 1])
        score = sb("score", [GT, NSLC])
        top = sb("top", [GT, 8])
        t_ps = [pb(f"t{k}", [P, 4, P]) for k in range(2)]
        h_ps = [pb(f"h{v}", [P, 512]) for v in range(2)]
        w2_ps = pb("w2", [P, 512])
        s_ps = pb("s", [P, 512])
        pT_ps = pb("pT", [P, 2, MR])
        o_ps = pb("o", [MR, P])

        w_ld, k_ld, pt_ld, g_ld = sem("w_ld"), sem("k_ld"), sem("pt_ld"), sem("g_ld")
        x_ld = [sem(f"x_ld{s}") for s in range(4)]
        peT_done, peT_set, hb_done, hb_set = (sem(n) for n in ("peT_done", "peT_set", "hb_done", "hb_set"))
        rows_set, row_set, ch_p, ch_v, zeroed = (sem(n) for n in ("rows_set", "row_set", "ch_p", "ch_v", "zeroed"))
        x_used, t_done, t_dve, t_act = (sem(n) for n in ("x_used", "t_done", "t_dve", "t_act"))
        h_done, h_read, inner, tanhed, g_rdy = (sem(n) for n in ("h_done", "h_read", "inner", "tanhed", "g_rdy"))
        kc_done, vc_done, kc_set, vc_set = (sem(n) for n in ("kc_done", "vc_done", "kc_set", "vc_set"))
        q_set, s_done, max_set, exp_done, p_set = (sem(n) for n in ("q_set", "s_done", "max_set", "exp_done", "p_set"))
        pt_done, pt_set, sel_set, pv_done, o_set = (sem(n) for n in ("pt_done", "pt_set", "sel_set", "pv_done", "o_set"))
        sel_used, prompt_ld = sem("sel_used"), [sem("prompt_ld0"), sem("prompt_ld1")]
        block = ctx.enter_context(nc.Block())
        PR = NB

        first = lambda b: isinstance(b, int) and b == 0
        later = lambda b: not isinstance(b, int) or b >= 2
        prompt = lambda b: isinstance(b, int) and b == PR

        def sequences(eng, step):
            step(0)
            step(1)
            with eng.Fori(2, NB - 1) as b:
                step(b)
            step(NB - 1)
            step(PR)

        def after(b, v):
            return (b, 1) if v == 0 else None if prompt(b) else (b + 1, 0)

        def n_fills(b):
            return 4 if prompt(b) else 8

        def fills(b, v):
            return 16 * b + (4 if prompt(b) else 8) * v

        def half_fills(b, v):
            return 8 * b + (2 if prompt(b) else 4) * v

        @block.sync
        def _(sp):
            for n, (a, b) in enumerate((("cmp_wk1", "cmp_wk2"), ("cmp_wv1", "cmp_wv2"))):
                sp.dma_start(w1[:, n, :, :], bass.AP(d[a].tensor, 0, [(CH, P), (P * CH, LP), (1, CH)])).then_inc(w_ld, 16)
                sp.dma_start(w2[:, n, :], d[b].rearrange("z f c -> (z f) c")).then_inc(w_ld, 16)
            sp.dma_start(pe_nat[:, 0, :], d["cmp_pe_k"].rearrange("z (c l) q -> (z c) (l q)", l=2)).then_inc(k_ld, 16)
            sp.dma_start(pe_nat[:, 1, :], d["cmp_pe_v"].rearrange("z (c l) q -> (z c) (l q)", l=2)).then_inc(k_ld, 16)
            sp.dma_start(gsum[:], d["gsum"]).then_inc(k_ld, 16)
            sp.dma_start(gspread[:], d["gspread"]).then_inc(k_ld, 16)
            for h in range(NH):
                sp.dma_start(g_rows[h * TS:(h + 1) * TS, :, :],
                             d["g_new"].rearrange("(b t) (h c) -> t b h c", t=TS, h=NH)[:, :, h, :]).then_inc(g_ld, 16)
            for v, name in ((0, "k_cmp_p"), (1, "v_cmp_p")):
                sp.wait_ge(x_used, 4 * NB - 3 + 2 * v)
                sp.dma_start(x[2 * v][0:SEQ // CS, :],
                             d[name].rearrange("z a (n r) h c -> (z a n) (r h c)", r=CS)).then_inc(prompt_ld[v], 16)

        @block.gpsimd
        def _(pool):
            link = Chain(pool, ch_p)
            for q in range(PAGE // CS):
                pool.dma_start(pages[q::PAGE // CS, :], bass.AP(d["page_table"].tensor, 0, [(1, P * CS // PAGE), (P * CS // PAGE, 2 * NB)]),
                               allow_slow_non_contiguous=True).then_inc(pt_ld, 16)
            pool.dma_start(in_page[:], d["in_page"]).then_inc(pt_ld, 16)
            pool.wait_ge(pt_ld, 16 * (PAGE // CS + 1))
            link(pool.tensor_scalar(rows_of[:], pages[:], PAGE // CS, None, ALU.mult))
            link(pool.tensor_tensor(rows_of[:], rows_of[:], in_page[:].to_broadcast([P, 2 * NB]), ALU.add))
            link.restart()

            def gather(b):
                for s in range(4):
                    if not first(b):
                        pool.wait_ge(x_used, 4 * b + s - 3)
                    pool.nop(nofuse=True)
                    link(pool.tensor_copy(row_now[:, s:s + 1], rows_of[:, ds(2 * b + s % 2, 1)]))
                    link.restart()
                    table = d["cache_k_cmp" if s < 2 else "cache_v_cmp"].rearrange("z n (q r) h c -> (z n q) (r h c)", r=CS)
                    pool.indirect_dma_start(x[s][:], None, table, bass.IndirectOffsetOnAxis(ap=row_now[:, s:s + 1], axis=0)
                                            ).then_inc(x_ld[s], 16)

            gather(0)
            with pool.Fori(1, NB) as b:
                gather(b)

        @block.tensor
        def _(pe):
            pe.wait_ge(k_ld, 64)
            pe.wait_ge(w_ld, 64)
            for v in range(2):
                ins = pe.transpose(t_ps[0][:, v, 0:LP], pe_nat[:, v, :], ident[0:LP, 0:LP])
            ins.then_inc(peT_done, 1)
            pe.wait_ge(peT_set, 1)
            for v in range(2):
                for c in range(LP):
                    ins = pe.matmul(w2_ps[:, v:v + 1], w1[:, v, c, :], peT[:, v, c:c + 1], start=(c == 0), stop=(c == LP - 1))
            ins.then_inc(hb_done, 1)
            pe.wait_ge(hb_set, 1)

            def fill(b, v, n):
                i, q = divmod(n, 4)
                rows = SEQ // CS if prompt(b) else P
                if q == 0:
                    if prompt(b):
                        pe.wait_ge(prompt_ld[v], 16)
                    else:
                        pe.wait_ge(x_ld[2 * v + i], 16 * b + 16)
                if not (first(b) and v == 0 and i == 0 and q < 2):
                    pe.wait_ge(t_act if q % 2 else t_dve, half_fills(b, v) + 2 * i + q // 2)
                pe.nop(nofuse=True)
                for l in range(4):
                    at = (4 * q + l) * KVW
                    ins = pe.transpose(t_ps[q % 2][:, l, 0:rows], x[2 * v + i][0:rows, at:at + KVW], ident[0:rows, 0:rows])
                ins.then_inc(t_done, 1)
                if q == 3:
                    pe.wait_ge(t_done, fills(b, v) + 4 * i + 4)
                    pe.sem_inc(x_used, 1)

            def hidden(b, v):
                n = half_fills(b, v) + (2 if prompt(b) else 4)
                pe.wait_ge(t_dve, n)
                pe.wait_ge(t_act, n)
                if not first(b):
                    pe.wait_ge(h_read, 2 * b + v - 1)
                m = NC_P if prompt(b) else NC_S
                out = h_ps[v][:, 0:2 * m].rearrange("p (h n) -> p h n", h=2)
                for c in range(LP):
                    ins = pe.matmul(out, w1[:, v, c, :], xT[v][:, c % (LP // 2), :, c // (LP // 2):c // (LP // 2) + m],
                                    start=(c == 0), stop=(c == LP - 1))
                    if c == LP - 1:
                        ins.then_inc(h_done, 1)
                    if c % 2 and after(b, v) is not None and c // 2 < n_fills(after(b, v)[0]):
                        fill(*after(b, v), c // 2)
                    if v == 1 and c == LP // 2 and not first(b):
                        grouped(b - 1)

            def keys(b):
                m = NC_P if prompt(b) else NC_S
                pe.wait_ge(g_rdy, 2 * b + 1)
                if not first(b):
                    pe.wait_ge(vc_set, b)
                for h in range(NKV):
                    ins = pe.matmul(w2_ps[h * DH:(h + 1) * DH, 0:m], w2[:, 0, :], g[0][:, h, 0:m], start=True, stop=True)
                ins.then_inc(kc_done, 1)

            def values(b):
                m = NC_P if prompt(b) else NC_S
                pe.wait_ge(g_rdy, 2 * b + 2)
                pe.wait_ge(kc_set, b + 1)
                for c in range(1 if prompt(b) else 2):
                    n = min(P, m - c * P)
                    for h in range(NKV):
                        at = 256 + c * KVW + h * DH
                        ins = pe.matmul(w2_ps[0:n, at:at + DH], g[1][:, h, c * P:c * P + n], w2[:, 1, :], start=True, stop=True)
                ins.then_inc(vc_done, 1)

            def scores(b):
                pe.wait_ge(kc_set, b + 1)
                pe.wait_ge(q_set, b + 1)
                if not first(b):
                    pe.wait_ge(sel_used, b)
                pe.matmul(s_ps[0:MR, 0:NC_S], qs[:], kc[:], start=True, stop=True).then_inc(s_done, 1)

            def grouped(b):
                pe.wait_ge(p_set, b + 1)
                if not first(b):
                    pe.wait_ge(pt_set, b)
                pe.nop(nofuse=True)
                pe.matmul(s_ps[0:GT, 256:256 + NC_S], gsum[:], prob[:], start=True, stop=True)
                for c in range(2):
                    n = min(P, NC_S - c * P)
                    ins = pe.transpose(pT_ps[0:n, c, :], prob[:, c * P:c * P + n], ident[0:MR, 0:MR])
                ins.then_inc(pt_done, 1)

            def attend(b):
                pe.wait_ge(pt_set, b + 1)
                pe.wait_ge(vc_set, b + 1)
                if not first(b):
                    pe.wait_ge(o_set, b)
                for c in range(2):
                    n = min(P, NC_S - c * P)
                    ins = pe.matmul(o_ps[:], pT[0:n, c, :], vc[0:n, c, :], start=(c == 0), stop=(c == 1))
                ins.then_inc(pv_done, 1)
                pe.wait_ge(sel_set, b + 1)
                pe.matmul(s_ps[0:MR, 0:NSLC], gspread[:], score[:], start=True, stop=True).then_inc(pv_done, 1)

            def step(b):
                hidden(b, 0)
                if later(b):
                    attend(b - 2)
                if not first(b):
                    values(b - 1)
                    scores(b - 1)
                hidden(b, 1)
                keys(b)

            for n in range(n_fills(0)):
                fill(0, 0, n)
            sequences(pe, step)
            attend(NB - 1)
            values(PR)

        def take(eng, copy, done, b, v, i):
            rows = SEQ // CS if prompt(b) else P
            if 4 * i < n_fills(b):
                if i == 0 and not first(b):
                    eng.wait_ge(h_done, 2 * b + v - 1)
                for q in range(1 if done is t_act else 0, 4, 2):
                    eng.wait_ge(t_done, fills(b, v) + 4 * i + q + 1)
                    src = t_ps[q % 2][:].rearrange("p (c l) n -> p c l n", l=2)
                    for h in range(NKV):
                        for l in range(2):
                            ins = copy(xT[v][l * DH:(l + 1) * DH, 2 * q:2 * q + 2, h, i * P:i * P + rows],
                                       src[h * DH:(h + 1) * DH, :, l, 0:rows])
                    ins.then_inc(done, 1)

        @block.scalar
        def _(act):
            copy = lambda out, in_: act.activation(out, in_, ACT.Copy)
            act.wait_ge(peT_done, 1)
            act.activation(peT[:], t_ps[0][:, 0:2, 0:LP], ACT.Copy).then_inc(peT_set, 1)
            act.wait_ge(hb_done, 1)
            act.activation(hbias[:], w2_ps[:, 0:2], ACT.Copy).then_inc(hb_set, 1)
            act.wait_ge(hb_set, 1)

            def gelu_in(b, v):
                m = NC_P if prompt(b) else NC_S
                act.wait_ge(h_done, 2 * b + v + 1)
                if not first(b):
                    act.wait_ge(g_rdy, 2 * b + v - 1)
                out = h_ps[v][:, 0:2 * m].rearrange("p (h n) -> p h n", h=2)
                act.activation(xb[v][:, :, 0:m], out, ACT.Identity, bias=hbias[:, v:v + 1])
                act.activation(sq[v][:, :, 0:m], out, ACT.Square, bias=hbias[:, v:v + 1]).then_inc(h_read, 1)

            def gelu_tanh(b, v):
                m = NC_P if prompt(b) else NC_S
                act.wait_ge(inner, 2 * b + v + 1)
                act.activation(sq[v][:, :, 0:m], sq[v][:, :, 0:m], ACT.Tanh, scale=C_TANH).then_inc(tanhed, 1)

            def take_values(b):
                act.wait_ge(vc_done, b + 1)
                if prompt(b):
                    act.activation(r["vc_p"][:], w2_ps[0:NC_P, 256:256 + KVW], ACT.Copy, scale=0.5).then_inc(vc_set, 1)
                    return
                if not first(b):
                    act.wait_ge(o_set, b)
                for c in range(2):
                    n = min(P, NC_S - c * P)
                    ins = act.activation(vc[0:n, c, :], w2_ps[0:n, 256 + c * KVW:256 + (c + 1) * KVW], ACT.Copy, scale=0.5)
                ins.then_inc(vc_set, 1)

            def exponentials(b):
                act.wait_ge(max_set, b + 1)
                if not first(b):
                    act.wait_ge(pt_done, b)
                act.activation(prob[:], s_ps[0:MR, 0:NC_S], ACT.Exp, bias=stat[:, 0:1],
                               accum_out=stat[:, 1:2]).then_inc(exp_done, 1)

            def take_keys(b):
                act.wait_ge(kc_done, b + 1)
                if prompt(b):
                    act.activation(r["kc_p"][:], w2_ps[:, 0:NC_P], ACT.Copy, scale=0.5).then_inc(kc_set, 1)
                    return
                if not first(b):
                    act.wait_ge(s_done, b)
                act.activation(kc[:], w2_ps[:, 0:NC_S], ACT.Copy, scale=0.5).then_inc(kc_set, 1)

            def step(b):
                take(act, copy, t_act, b, 1, 0)
                if not first(b):
                    gelu_tanh(b - 1, 1)
                take(act, copy, t_act, b, 1, 1)
                gelu_in(b, 0)
                if not first(b):
                    take_values(b - 1)
                    exponentials(b - 1)
                if not prompt(b):
                    take(act, copy, t_act, b + 1, 0, 0)
                gelu_tanh(b, 0)
                if not prompt(b):
                    take(act, copy, t_act, b + 1, 0, 1)
                gelu_in(b, 1)
                take_keys(b)

            for i in range(2):
                take(act, copy, t_act, 0, 0, i)
            sequences(act, step)
            gelu_tanh(PR, 1)
            take_values(PR)

        @block.vector
        def _(dve):
            link = Chain(dve, ch_v)
            copy = dve.tensor_copy
            tt = dve.tensor_tensor
            link(dve.memset(qbd[:], 0.0))
            for j in range(NG):
                for gg in range(NKV):
                    rows = slice(gg * DH, (gg + 1) * DH)
                    at = (gg * NG + j) * TS
                    link.put(copy(qbd[rows, 0:NB, at:at + TS], qkT[rows, j, SEQ:TOK].rearrange("p (b t) -> p b t", t=TS)))
            link.sync()
            link.put(dve.memset(pg[:], 0.0))
            link(copy(qs[:], qbd[:, 0, :]))
            dve.sem_inc(q_set, 1)
            dve.wait_ge(g_ld, 16 * NH)
            link.restart()

            def gelu_inner(b, v):
                m = NC_P if prompt(b) else NC_S
                dve.wait_ge(h_read, 2 * b + v + 1)
                s, xx = sq[v][:, :, 0:m], xb[v][:, :, 0:m]
                link(dve.tensor_scalar(s, s, C_CUBE, 1.0, ALU.mult, ALU.add))
                link(tt(s, s, xx, ALU.mult))
                dve.sem_inc(inner, 1)

            def gelu_out(b, v):
                m = NC_P if prompt(b) else NC_S
                dve.wait_ge(tanhed, 2 * b + v + 1)
                if not first(b):
                    dve.wait_ge(vc_done if v else kc_done, b)
                s, xx = sq[v][:, :, 0:m], xb[v][:, :, 0:m]
                dve.scalar_tensor_tensor(g[v][:, :, 0:m], s, 1.0, xx, ALU.add, ALU.mult).then_inc(g_rdy, 1)

            def softmax(b):
                dve.wait_ge(s_done, b + 1)
                link.put(copy(qs[:], row(qbd[:, ds(b + 1, 1), :])))
                link(dve.tensor_reduce(stat[:, 0:1], s_ps[0:MR, 0:NC_S], X, ALU.max, negate=True))
                dve.sem_inc(max_set, 1)
                dve.sem_inc(q_set, 1)
                dve.wait_ge(exp_done, b + 1)
                link(dve.tensor_scalar(stat[:, 2:3], stat[:, 1:2], 1e-30, None, ALU.max))
                link(dve.reciprocal(stat[:, 2:3], stat[:, 2:3]))
                link(dve.tensor_scalar(prob[:], prob[:], stat[:, 2:3], None, ALU.mult))
                dve.sem_inc(p_set, 1)

            def select(b):
                dve.wait_ge(pt_done, b + 1)
                for c in range(2):
                    n = min(P, NC_S - c * P)
                    link.put(copy(pT[0:n, c, :], pT_ps[0:n, c, :]))
                link.sync()
                dve.sem_inc(pt_set, 1)
                link(copy(pg[:, 1:1 + NC_S], s_ps[0:GT, 256:256 + NC_S]))
                part = lambda k: pg[:, k:k + 4 * (NSLC - 1)].rearrange("p (j f) -> p j f", f=4)[:, :, 0]
                link(tt(imp[:], part(0), part(4), ALU.add))
                link(dve.scalar_tensor_tensor(imp[:], imp[:], 0.5, part(1), ALU.mult, ALU.add))
                link(tt(imp[:], imp[:], part(2), ALU.add))
                link(tt(imp[:], imp[:], part(3), ALU.add))
                if not first(b):
                    dve.wait_ge(pv_done, 2 * b)
                link(dve.memset(score[:], 1e9))
                link(copy(score[:, 1:NSLC - 2], imp[:, 1:NSLC - 2]))
                for _ in range(TOPK // 8):
                    link(dve.max(top[:], score[:]))
                    link(dve.match_replace(score[:], top[:], score[:], -1.0))
                link(dve.tensor_scalar(score[:], score[:], 0.0, None, ALU.is_lt))
                dve.sem_inc(sel_set, 1)

            def gate(b):
                dve.wait_ge(pv_done, 2 * b + 1)
                for gg in range(NKV):
                    rows = slice(gg * MR // 2, (gg + 1) * MR // 2)
                    link.put(dve.tensor_scalar(row(osum[rows, ds(b, 1), :]), o_ps[rows, gg * DH:(gg + 1) * DH],
                                               row(g_rows[rows, ds(b, 1), 0:1]), None, ALU.mult))
                link.sync()
                dve.sem_inc(o_set, 1)
                dve.wait_ge(pv_done, 2 * b + 2)
                link(dve.tensor_scalar(row(sel_bias[:, ds(b, 1), :]), s_ps[0:MR, 0:NSLC], -NEG, NEG, ALU.mult, ALU.add))
                dve.sem_inc(sel_used, 1)

            def step(b):
                if not first(b):
                    gelu_inner(b - 1, 1)
                take(dve, copy, t_dve, b, 1, 0)
                if not first(b):
                    gelu_out(b - 1, 1)
                take(dve, copy, t_dve, b, 1, 1)
                if later(b):
                    gate(b - 2)
                gelu_inner(b, 0)
                if not first(b):
                    softmax(b - 1)
                if not prompt(b):
                    take(dve, copy, t_dve, b + 1, 0, 0)
                gelu_out(b, 0)
                if not prompt(b):
                    take(dve, copy, t_dve, b + 1, 0, 1)
                if not first(b):
                    select(b - 1)
                link.restart()

            for i in range(2):
                take(dve, copy, t_dve, 0, 0, i)
            sequences(dve, step)
            gate(NB - 1)
            gelu_inner(PR, 1)
            gelu_out(PR, 1)


KCH = 2 * CS * KVW // 512
CH_B = KCH + 1
PAST_T, WIN_T = PAST // P, WIN // P
NEW_S = PAST
WIN_0 = NEW_S + TS
NEW_W = WIN_0 + WIN
SCOLS = NEW_W + TS
PG = 5


def phase_sampled(nc, d, r):
    with ExitStack() as ctx:
        sb = lambda name, shape, dt=F32: ctx.enter_context(nc.sbuf_tensor("a_" + name, shape, dt))
        pb = lambda name, shape: ctx.enter_context(nc.psum_tensor("a_" + name + "_ps", shape, F32))
        sem = ctx.enter_context(Semaphores(nc, "a_"))
        ident, qkT, qbd, g_rows, osum, sel_bias, oT = (r[n] for n in ("ident", "qkT", "qbd", "g_rows", "osum", "sel_bias", "oTs"))
        rows_of, pages, in_page = (sb(n, s, I32) for n, s in (("rows_of", [P, 2 * NB]), ("pages", [P, 2 * NB]), ("in_page", [P, 1])))
        row_now = sb("row_now", [P, 4], I32)
        kx = [sb(f"kx{i}", [P, CS * KVW]) for i in range(2)]
        vx = [sb(f"vx{i}", [P, CS * KVW]) for i in range(2)]
        kwx = sb("kwx", [P, WIN_T, KVW])
        vwx = sb("vwx", [P, WIN_T, KVW])
        vn = sb("vn", [P, NB, 2, KVW])
        win_mask = sb("win_mask", [MR, WIN])
        new_mask = sb("new_mask", [MR, TS])
        kT = [sb(f"kT{k}", [P, 512]) for k in range(2)]
        qs = sb("qs", [P, MR])
        s_all = sb("s_all", [MR, SCOLS])
        prob_at = nc.sbuf_base
        prob = sb("prob", [MR, SCOLS])
        pT = sb("pT", [P, PAST_T + WIN_T, MR])
        pTn = sb("pTn", [P, 2, MR])
        stat = sb("stat", [MR, 8])
        odup = sb("odup", [MR, NB, 2, DH])
        t_ps = [pb(f"t{k}", [P, 512]) for k in range(2)]
        s_ps = [pb(f"s{k}", [MR, 512]) for k in range(2)]
        p_ps = [pb(f"p{k}", [P, 8, MR]) for k in range(2)]
        new_ps = pb("new", [MR, 2, TS])
        o_ps = pb("o", [MR, 2, KVW])

        pt_ld, m_ld, kw_ld, vw_ld, rows_set, row_set = (sem(n) for n in ("pt_ld", "m_ld", "kw_ld", "vw_ld", "rows_set", "row_set"))
        k_ld, v_ld = [sem("k_ld0"), sem("k_ld1")], [sem("v_ld0"), sem("v_ld1")]
        t_done, qk_done, s_added, new_done, new_added = (sem(n) for n in ("t_done", "qk_done", "s_added", "new_done", "new_added"))
        kt_set = [sem("kt_set0"), sem("kt_set1")]
        q_set, max_set, exp_done, pt_done, pv_done, o_set = (sem(n) for n in ("q_set", "max_set", "exp_done", "pt_done", "pv_done", "o_set"))
        pt_set = [sem("pt_set0"), sem("pt_set1")]
        zeroed = sem("zeroed")
        assert FT * TOK <= SCOLS
        gelu = Gelu(nc, sem, r["yT"], prob_at)
        dup_set, oT_done, oT_set, ch_v, ch_p = (sem(n) for n in ("dup_set", "oT_done", "oT_set", "ch_v", "ch_p"))
        block = ctx.enter_context(nc.Block())
        first = lambda b: isinstance(b, int) and b == 0
        end = lambda b: isinstance(b, int) and b == NB

        def sequences(eng, step):
            step(0)
            with eng.Fori(1, NB) as b:
                step(b)
            step(NB)

        def uses(b, c):
            return (4 if c % 2 else 5) * b + c // 2

        def before(b, c):
            return CH_B * b + (c - 1 if c >= 2 else -c)

        def p_uses(b, u):
            return (2 if u % 2 else 3) * b + u // 2

        @block.sync
        def _(sp):
            sp.dma_start(win_mask[:], d["win_mask"]).then_inc(m_ld, 16)
            sp.dma_start(new_mask[:], d["new_mask"]).then_inc(m_ld, 16)
            sp.wait_ge(zeroed, 1)
            sp.dma_start(vn[0:TS], d["v_new"].rearrange("(b t) (c w) -> t b c w", t=TS, c=2)).then_inc(m_ld, 16)

            def load(name, dst, b, s):
                src = d[name].rearrange("z b (p r) h c -> (z b) p (r h c)", r=WIN_T)
                at = src[b] if isinstance(b, int) else src[ds(b, 1)].rearrange("b p n -> (b p) n")
                sp.dma_start(dst[:].rearrange("p r w -> p (r w)"), at).then_inc(s, 16)

            load("state_k_win", kwx, 0, kw_ld)
            load("state_v_win", vwx, 0, vw_ld)
            with sp.Fori(1, NB) as b:
                sp.wait_ge(t_done, CH_B * b)
                load("state_k_win", kwx, b, kw_ld)
                sp.wait_ge(pv_done, PG * b)
                load("state_v_win", vwx, b, vw_ld)

        @block.gpsimd
        def _(pool):
            link = Chain(pool, ch_p)
            for q in range(PAGE // CS):
                pool.dma_start(pages[q::PAGE // CS, :], bass.AP(d["page_table"].tensor, 0, [(1, P * CS // PAGE), (P * CS // PAGE, 2 * NB)]),
                               allow_slow_non_contiguous=True).then_inc(pt_ld, 16)
            pool.dma_start(in_page[:], d["in_page"]).then_inc(pt_ld, 16)
            pool.wait_ge(pt_ld, 16 * (PAGE // CS + 1))
            link(pool.tensor_scalar(rows_of[:], pages[:], PAGE // CS, None, ALU.mult))
            link(pool.tensor_tensor(rows_of[:], rows_of[:], in_page[:].to_broadcast([P, 2 * NB]), ALU.add))
            link.restart()

            def gather(b):
                for s in range(4):
                    if not first(b):
                        if s < 2:
                            pool.wait_ge(t_done, CH_B * (b - 1) + KCH // 2 * (s + 1))
                        else:
                            pool.wait_ge(pv_done, PG * (b - 1) + 2 * (s - 1))
                    pool.nop(nofuse=True)
                    link(pool.tensor_copy(row_now[:, s:s + 1], rows_of[:, ds(2 * b + s % 2, 1)]))
                    link.restart()
                    table = d["cache_k_slc" if s < 2 else "cache_v_slc"].rearrange("z n (q r) h c -> (z n q) (r h c)", r=CS)
                    pool.indirect_dma_start((kx if s < 2 else vx)[s % 2][:], None, table,
                                            bass.IndirectOffsetOnAxis(ap=row_now[:, s:s + 1], axis=0)
                                            ).then_inc((k_ld if s < 2 else v_ld)[s % 2], 16)

            gather(0)
            with pool.Fori(1, NB) as b:
                gather(b)

        @block.tensor
        def _(pe):
            def transposes(b, c):
                if c < KCH:
                    i = c // (KCH // 2)
                    if c % (KCH // 2) == 0:
                        pe.wait_ge(k_ld[i], 16 * b + 16)
                    src = [kx[i][:, (4 * c + l) % CS * KVW:((4 * c + l) % CS + 1) * KVW] for l in range(4)]
                else:
                    pe.wait_ge(kw_ld, 16 * b + 16)
                    src = [kwx[:, l, :] for l in range(4)]
                if not (first(b) and c < 2):
                    pe.wait_ge(kt_set[c % 2], uses(b, c))
                for l in range(4):
                    ins = pe.transpose(t_ps[c % 2][:, l * P:(l + 1) * P], src[l], ident[:])
                ins.then_inc(t_done, 1)

            def scores(b, c):
                pe.wait_ge(kt_set[c % 2], uses(b, c) + 1)
                if c == 0:
                    pe.wait_ge(q_set, b + 1)
                if not (first(b) and c < 2):
                    pe.wait_ge(s_added, before(b, c))
                pe.matmul(s_ps[c % 2][:], qs[:], kT[c % 2][:], start=True, stop=True).then_inc(qk_done, 1)

            def new_scores(b):
                if not first(b):
                    pe.wait_ge(new_added, b)
                for n in range(2):
                    ins = pe.matmul(new_ps[:, n, :], qs[:], row(qkT[:, NG + n:NG + n + 1, ds(SEQ + TS * b, TS)]), start=True, stop=True)
                ins.then_inc(new_done, 1)

            def prob_transposes(b, u):
                if u == 0:
                    pe.wait_ge(exp_done, b + 1)
                if not (first(b) and u < 2):
                    pe.wait_ge(pt_set[u % 2], p_uses(b, u))
                pe.nop(nofuse=True)
                if u < 4:
                    for n in range(8):
                        at = (8 * u + n) * P
                        ins = pe.transpose(p_ps[u % 2][:, n, :], prob[:, at:at + P], ident[0:MR, 0:MR])
                else:
                    for n in range(WIN_T):
                        pe.transpose(p_ps[0][:, n, :], prob[:, WIN_0 + n * P:WIN_0 + (n + 1) * P], ident[0:MR, 0:MR])
                    for n, at in enumerate((NEW_S, NEW_W)):
                        ins = pe.transpose(p_ps[0][0:TS, WIN_T + n, :], prob[:, at:at + TS], ident[0:MR, 0:MR])
                ins.then_inc(pt_done, 1)

            def values(b, u):
                pe.wait_ge(pt_set[u % 2], p_uses(b, u) + 1)
                if u == 0 and not first(b):
                    pe.wait_ge(o_set, b)
                if u < 4:
                    if u % 2 == 0:
                        pe.wait_ge(v_ld[u // 2], 16 * b + 16)
                    for n in range(8):
                        t = 8 * u + n
                        ins = pe.matmul(o_ps[:, 0, :], pT[:, t, :], vx[u // 2][:, t % CS * KVW:(t % CS + 1) * KVW],
                                        start=(t == 0), stop=False)
                else:
                    pe.matmul(o_ps[:, 0, :], pTn[:, 0, :], row(vn[:, ds(b, 1), 0, :]), start=False, stop=True)
                    pe.wait_ge(vw_ld, 16 * b + 16)
                    for n in range(WIN_T):
                        pe.matmul(o_ps[:, 1, :], pT[:, PAST_T + n, :], vwx[:, n, :], start=(n == 0), stop=False)
                    ins = pe.matmul(o_ps[:, 1, :], pTn[:, 1, :], row(vn[:, ds(b, 1), 1, :]), start=False, stop=True)
                ins.then_inc(pv_done, 1)

            pe.wait_ge(m_ld, 48)

            def step(b):
                if not end(b):
                    transposes(b, 0)
                    transposes(b, 1)
                for c in range(CH_B):
                    if not end(b):
                        scores(b, c)
                        if c + 2 < CH_B:
                            transposes(b, c + 2)
                    if not first(b):
                        if 1 <= c <= PG:
                            prob_transposes(b - 1, c - 1)
                        if 2 <= c <= PG + 1:
                            values(b - 1, c - 2)
                if not end(b):
                    new_scores(b)

            sequences(pe, step)
            pe.wait_ge(dup_set, 1)
            for b in range(NB):
                ins = pe.transpose(t_ps[0][:, b * MR:(b + 1) * MR], odup[:, b, :, :].rearrange("p k c -> p (k c)"), ident[0:MR, 0:MR])
            ins.then_inc(oT_done, 1)

        def take_keys(eng, copy, b, c):
            eng.wait_ge(t_done, CH_B * b + c + 1)
            if not (first(b) and c < 2):
                eng.wait_ge(qk_done, before(b, c))
            copy(kT[c % 2][:], t_ps[c % 2][:]).then_inc(kt_set[c % 2], 1)

        def take_probs(eng, copy, b, u):
            eng.wait_ge(pt_done, PG * b + u + 1)
            if u == (1 if eng is nc.scalar else 0) and not first(b):
                eng.wait_ge(pv_done, PG * b)
            if u < 4:
                ins = copy(pT[:, 8 * u:8 * u + 8, :], p_ps[u % 2][:])
            else:
                copy(pT[:, PAST_T:PAST_T + WIN_T, :], p_ps[0][:, 0:WIN_T, :])
                ins = copy(pTn[0:TS], p_ps[0][0:TS, WIN_T:WIN_T + 2, :])
            ins.then_inc(pt_set[u % 2], 1)

        @block.scalar
        def _(act):
            copy = lambda out, in_: act.activation(out, in_, ACT.Copy)
            gelu.scalar(act)

            def step(b):
                if not end(b):
                    take_keys(act, copy, b, 1)
                for c in range(CH_B):
                    if not end(b) and c + 2 < CH_B and c % 2:
                        take_keys(act, copy, b, c + 2)
                    if not first(b) and c in (2, 4):
                        take_probs(act, copy, b - 1, c - 1)
                if not end(b):
                    act.wait_ge(max_set, b + 1)
                    if not first(b):
                        act.wait_ge(pt_done, PG * b)
                    act.activation(prob[:, 0:WIN_0], s_all[:, 0:WIN_0], ACT.Exp, bias=stat[:, 0:1], accum_out=stat[:, 2:3])
                    act.activation(prob[:, WIN_0:SCOLS], s_all[:, WIN_0:SCOLS], ACT.Exp, bias=stat[:, 1:2],
                                   accum_out=stat[:, 3:4]).then_inc(exp_done, 1)

            sequences(act, step)

        @block.vector
        def _(dve):
            link = Chain(dve, ch_v)
            copy = dve.tensor_copy
            tt = dve.tensor_tensor
            dve.memset(vn[:], 0.0).then_inc(zeroed, 1)
            link.put(dve.memset(pTn[:], 0.0))
            link(copy(qs[:], qbd[:, 0, :]))
            dve.sem_inc(q_set, 1)
            gelu.vector(dve, link)
            dve.wait_ge(m_ld, 48)
            link.restart()

            def add(b, c):
                dve.wait_ge(qk_done, CH_B * b + c + 1)
                if c == 0 and not first(b):
                    dve.wait_ge(exp_done, b)
                if c < KCH:
                    i = c // (KCH // 2)
                    split = lambda ap: ap.rearrange("p (l n f) -> p l n f", l=4, f=4)
                    bias = sel_bias[:, ds(b, 1), 32 * i:32 * i + 32].unsqueeze(3).to_broadcast([MR, 4, 32, 4])
                    link(tt(split(s_all[:, 512 * c:512 * c + 512]), split(s_ps[c % 2][:]), bias, ALU.add))
                else:
                    link(tt(s_all[:, WIN_0:NEW_W], s_ps[0][:], win_mask[:], ALU.add))
                dve.sem_inc(s_added, 1)

            def out(b):
                dve.wait_ge(pv_done, PG * b + PG)
                link(dve.tensor_scalar(stat[:, 4:6], stat[:, 2:4], 1e-30, None, ALU.max))
                link(dve.reciprocal(stat[:, 4:6], stat[:, 4:6]))
                link(tt(stat[:, 6:8], stat[:, 4:6], row(g_rows[:, ds(b, 1), 1:3]), ALU.mult))
                for n in range(2):
                    for g in range(NKV):
                        rows = slice(g * MR // 2, (g + 1) * MR // 2)
                        at = row(osum[rows, ds(b, 1), :])
                        link.put(dve.scalar_tensor_tensor(at, o_ps[rows, n, g * DH:(g + 1) * DH], stat[rows, 6 + n:7 + n], at,
                                                          ALU.mult, ALU.add))
                    link.sync()
                dve.sem_inc(o_set, 1)

            def step(b):
                if not end(b):
                    take_keys(dve, copy, b, 0)
                for c in range(CH_B):
                    if not end(b):
                        add(b, c)
                        if c + 2 < CH_B and c % 2 == 0:
                            take_keys(dve, copy, b, c + 2)
                    if not first(b) and c in (1, 3, 5):
                        take_probs(dve, copy, b - 1, c - 1)
                if not first(b):
                    out(b - 1)
                if not end(b):
                    dve.wait_ge(new_done, b + 1)
                    for n, at in enumerate((NEW_S, NEW_W)):
                        link.put(tt(s_all[:, at:at + TS], new_ps[:, n, :], new_mask[:], ALU.add))
                    link.sync()
                    dve.sem_inc(new_added, 1)
                    if not (isinstance(b, int) and b == NB - 1):
                        link(copy(qs[:], row(qbd[:, ds(b + 1, 1), :])))
                        dve.sem_inc(q_set, 1)
                    link.put(dve.tensor_reduce(stat[:, 0:1], s_all[:, 0:WIN_0], X, ALU.max, negate=True))
                    link(dve.tensor_reduce(stat[:, 1:2], s_all[:, WIN_0:SCOLS], X, ALU.max, negate=True))
                    dve.sem_inc(max_set, 1)
                link.restart()

            sequences(dve, step)
            for k in range(2):
                link.put(copy(odup[:, :, k, :], osum[:]))
            link.sync()
            dve.sem_inc(dup_set, 1)
            dve.wait_ge(oT_done, 1)
            for g in range(NKV):
                rows = slice(g * DH, (g + 1) * DH)
                src = t_ps[0][rows, :].rearrange("p (b g j t) -> p g b j t", b=NB, g=NKV, j=NG)[:, g]
                copy(oT[rows, :, :].rearrange("p j (b t) -> p b j t", t=TS), src).then_inc(oT_set, 1)


WT = WIN // P
CMP, SLC, WIND = range(3)


def prompt_units():
    units = [(i, g, br, [0] if br == CMP else list(range(0 if br == SLC else max(0, i - WT), i + 1)))
             for i in range(TT) for g in range(NKV) for br in (CMP, SLC, WIND)]
    groups, n = [], 0
    for unit in units:
        k = -(-len(unit[3]) // 4)
        groups.append(range(n, n + k))
        n += k
    assert len(units) % 2 == 0 and n % 2 == 0
    return units, groups, n


def score_plan(units, banks, ahead):
    held, at, before = [None] * banks, [], []
    here = 0
    for u, (_, _, br, tiles) in enumerate(units):
        n = 1 if br == CMP or len(tiles) <= 4 else 2
        if here + n > banks:
            here = 0
        before.append(max((w for w in held[here:here + n] if w is not None), default=None))
        at.append(here)
        held[here:here + n] = [u] * n
        here += n
    starts, v = [[] for _ in range(len(units) + 1)], 0
    for step in range(-1, len(units)):
        while v < len(units) and v <= step + ahead and (before[v] is None or before[v] <= step):
            starts[step + 1].append(v)
            v += 1
        assert v == len(units) or v > step + 1
    return at, before, starts


def phase_prompt(nc, d, r):
    assert SEQ // 64 <= TOPK
    units, groups, NGR = prompt_units()
    U, UT = len(units), len(units) // TT
    BANKS, AHEAD = 5, 4
    s_at, s_before, starts = score_plan(units, BANKS, AHEAD)
    with ExitStack() as ctx:
        sb = lambda name, shape: ctx.enter_context(nc.sbuf_tensor("pr_" + name, shape, F32))
        pb = lambda name, shape: ctx.enter_context(nc.psum_tensor("pr_" + name + "_ps", shape, F32))
        sem = ctx.enter_context(Semaphores(nc, "pr_"))
        ident, qkT, v_nat, gates, kc_p, vc_p, oT, oTs = (r[n] for n in ("ident", "qkT", "v_nat", "gates", "kc_p", "vc_p", "oT", "oTs"))
        causal = sb("causal", [P, P])
        behind_win = sb("behind_win", [P, P])
        cmp_mask = sb("cmp_mask", [P, TT, NC_P])
        any_cmp = sb("any_cmp", [P, 1])
        qz = [sb(f"qz{g}", [P, SEQ]) for g in range(NKV)]
        prob = [sb(f"prob{k}", [P, SEQ]) for k in range(AHEAD)]
        pT = [sb(f"pT{k}", [P, TT, P]) for k in range(2)]
        o_j = sb("o_j", [P, TT, P])
        nmax = sb("nmax", [P, U])
        sums = sb("sums", [P, U])
        coef = sb("coef", [P, NKV, 3])
        parts = sb("parts", [P, NKV, 3, DH])
        s_ps = pb("s", [P, BANKS * 512])
        pt_ps = [pb(f"pt{k}", [P, 4, P]) for k in range(2)]
        o_ps = pb("o", [P, NKV, 3, DH])

        m_ld, zeroed, q_set, s_done, max_set, exp_done, pt_done = (
            sem(n) for n in ("m_ld", "zeroed", "q_set", "s_done", "max_set", "exp_done", "pt_done"))
        pt_set = [sem("pt_set0"), sem("pt_set1")]
        pv_done, o_taken, oj_set, oT_done, oT_set, ch_v, oTs_set = (sem(n) for n in ("pv_done", "o_taken", "oj_set", "oT_done", "oT_set", "ch_v", "oTs_set"))
        block = ctx.enter_context(nc.Block())
        scores_of = lambda u: s_ps[:, 512 * s_at[u]:512 * s_at[u] + (NC_P if units[u][2] == CMP else len(units[u][3]) * P)]

        def head_pairs(eng, step):
            step(0)
            with eng.Fori(1, NG) as j:
                step(j)

        first = lambda j: isinstance(j, int)

        @block.sync
        def _(sp):
            for dst, name in ((causal, "causal"), (behind_win, "behind_win"), (any_cmp, "any_cmp")):
                sp.dma_start(dst[:], d[name]).then_inc(m_ld, 16)
            sp.dma_start(cmp_mask[:], d["cmp_mask"]).then_inc(m_ld, 16)

        @block.gpsimd
        def _(pool):
            pool.tensor_copy(oT[:, :, SEQ:TOK], oTs[:]).then_inc(oTs_set, 1)
            pool.wait_ge(oTs_set, 1)
            for g in range(NKV):
                pool.memset(qz[g][(1 - g) * DH:(2 - g) * DH, :], 0.0).then_inc(zeroed, 1)
                pool.wait_ge(zeroed, g + 1)

            def step(j):
                if not first(j):
                    pool.wait_ge(s_done, U * j)
                for g in range(NKV):
                    rows = slice(g * DH, (g + 1) * DH)
                    pool.tensor_copy(qz[g][rows, :], row(qkT[rows, ds(j, 1), 0:SEQ])).then_inc(q_set, 1)
                    pool.wait_ge(q_set, NKV * j + g + 1)

            head_pairs(pool, step)

        @block.tensor
        def _(pe):
            pe.wait_ge(zeroed, NKV)

            def step(j):
                def score(u):
                    i, g, br, tiles = units[u]
                    if s_before[u] is not None:
                        pe.wait_ge(exp_done, U * j + s_before[u] + 1)
                    s = scores_of(u)
                    q = qz[g][:, i * P:(i + 1) * P]
                    if br == CMP:
                        ins = pe.matmul(s, q, kc_p[:], start=True, stop=True)
                    else:
                        k0, n = tiles[0] * P, len(tiles) * P
                        for at in range(0, n, 512):
                            w = min(512, n - at)
                            ins = pe.matmul(s[:, at:at + w], q, qkT[:, NG + br - 1, k0 + at:k0 + at + w],
                                            start=True, stop=True)
                    ins.then_inc(s_done, 1)

                def transpose(u):
                    i, g, br, tiles = units[u]
                    pe.wait_ge(exp_done, U * j + u + 1)
                    for k, n in enumerate(groups[u]):
                        if not (first(j) and n < 2):
                            pe.wait_ge(pt_set[n % 2], NGR // 2 * j + n // 2)
                        pe.nop(nofuse=True)
                        if br == CMP:
                            ins = pe.transpose(pt_ps[n % 2][0:NC_P, 0, :], prob[u % AHEAD][:, 0:NC_P], ident[:])
                        else:
                            for m in range(4 * k, min(4 * k + 4, len(tiles))):
                                ins = pe.transpose(pt_ps[n % 2][:, m % 4, :], prob[u % AHEAD][:, m * P:(m + 1) * P], ident[:])
                        ins.then_inc(pt_done, 1)

                def values(u):
                    i, g, br, tiles = units[u]
                    for n in groups[u]:
                        pe.wait_ge(pt_set[n % 2], NGR // 2 * j + n // 2 + 1)
                    if u % UT == 0 and not (first(j) and u == 0):
                        pe.wait_ge(o_taken, TT * j + i)
                    cols = slice(g * DH, (g + 1) * DH)
                    if br == CMP:
                        ins = pe.matmul(o_ps[:, g, br, :], pT[u % 2][0:NC_P, 0, :], vc_p[:, cols], start=True, stop=True)
                    else:
                        for m, t in enumerate(tiles):
                            ins = pe.matmul(o_ps[:, g, br, :], pT[u % 2][:, m, :], v_nat[:, t, br, cols],
                                            start=(m == 0), stop=(m == len(tiles) - 1))
                    ins.then_inc(pv_done, 1)

                pe.wait_ge(q_set, NKV * j + NKV)
                for v in starts[0]:
                    score(v)
                for u in range(U):
                    transpose(u)
                    for v in starts[u + 1]:
                        score(v)
                    if u:
                        values(u - 1)
                values(U - 1)
                pe.wait_ge(oj_set, TT * j + TT)
                for i in range(TT):
                    ins = pe.transpose(s_ps[:, i * P:(i + 1) * P], o_j[:, i, :], ident[:])
                ins.then_inc(oT_done, 1)
                pe.wait_ge(oT_set, j + 1)

            head_pairs(pe, step)

        def take(eng, copy, j, u, parity):
            i, g, br, tiles = units[u]
            for k, n in enumerate(groups[u]):
                if n % 2 != parity:
                    continue
                eng.wait_ge(pt_done, NGR * j + n + 1)
                if not (first(j) and u < 2):
                    eng.wait_ge(pv_done, U * j + u - 1)
                if br == CMP:
                    ins = copy(pT[u % 2][0:NC_P, 0, :], pt_ps[n % 2][0:NC_P, 0, :])
                else:
                    w = min(4, len(tiles) - 4 * k)
                    ins = copy(pT[u % 2][:, 4 * k:4 * k + w, :], pt_ps[n % 2][:, 0:w, :])
                ins.then_inc(pt_set[n % 2], 1)

        @block.scalar
        def _(act):
            copy = lambda out, in_: act.activation(out, in_, ACT.Copy)

            def step(j):
                def exponentials(u):
                    s = scores_of(u)
                    act.wait_ge(max_set, U * j + u + 1)
                    if u >= AHEAD:
                        act.wait_ge(pt_done, NGR * j + groups[u - AHEAD][-1] + 1)
                    act.activation(prob[u % AHEAD][:, 0:s.shape[1]], s, ACT.Exp, bias=nmax[:, u:u + 1],
                                   accum_out=sums[:, u:u + 1]).then_inc(exp_done, 1)

                for v in starts[0]:
                    exponentials(v)
                for u in range(U):
                    take(act, copy, j, u, 1)
                    for v in starts[u + 1]:
                        exponentials(v)
                act.wait_ge(oT_done, j + 1)
                act.activation(row(oT[:, ds(j, 1), 0:SEQ]), s_ps[:, 0:SEQ], ACT.Copy).then_inc(oT_set, 1)

            head_pairs(act, step)

        @block.vector
        def _(dve):
            link = Chain(dve, ch_v)
            copy = dve.tensor_copy
            dve.wait_ge(m_ld, 64)

            def step(j):
                def maximum(u):
                    i, g, br, tiles = units[u]
                    s = scores_of(u)
                    n = s.shape[1]
                    dve.wait_ge(s_done, U * j + u + 1)
                    if br == CMP:
                        link(dve.tensor_tensor(s[:, 0:n], s[:, 0:n], cmp_mask[:, i, :], ALU.add))
                    else:
                        link.put(dve.tensor_tensor(s[:, n - P:n], s[:, n - P:n], causal[:], ALU.add))
                        if br == WIND and i >= WT:
                            link.put(dve.tensor_tensor(s[:, 0:P], s[:, 0:P], behind_win[:], ALU.add))
                        link.sync()
                    dve.tensor_reduce(nmax[:, u:u + 1], s[:, 0:n], X, ALU.max, negate=True).then_inc(max_set, 1)

                def coefficients(i):
                    dve.wait_ge(exp_done, U * j + UT * i + UT)
                    at = sums[:, UT * i:UT * i + UT].rearrange("p (g b) -> p g b", g=NKV)
                    gate = row(gates[:, i:i + 1, :]).rearrange("p (g n) -> p g n", g=NKV)[:, :, ds(3 * j, 3)]
                    link(dve.tensor_scalar(coef[:], at, 1e-30, None, ALU.max))
                    link(dve.reciprocal(coef[:], coef[:]))
                    link(dve.tensor_tensor(coef[:], coef[:], gate, ALU.mult))
                    if i == 0:
                        link(dve.tensor_scalar(coef[:, :, CMP], coef[:, :, CMP], any_cmp[:], None, ALU.mult))

                def output(i):
                    dve.wait_ge(pv_done, U * j + UT * i + UT)
                    link(dve.tensor_tensor(parts[:], o_ps[:], coef[:].unsqueeze(3).to_broadcast([P, NKV, 3, DH]), ALU.mult))
                    dve.sem_inc(o_taken, 1)
                    at = o_j[:, i, :].rearrange("p (g c) -> p g c", g=NKV)
                    link(dve.tensor_tensor(at, parts[:, :, 0, :], parts[:, :, 1, :], ALU.add))
                    link(dve.tensor_tensor(at, at, parts[:, :, 2, :], ALU.add))
                    dve.sem_inc(oj_set, 1)

                if not first(j):
                    dve.wait_ge(oT_done, j)
                for v in starts[0]:
                    maximum(v)
                for u in range(U):
                    take(dve, copy, j, u, 0)
                    for v in starts[u + 1]:
                        maximum(v)
                    if u % UT == 0 and u:
                        output(u // UT - 1)
                    if u % UT == UT - 1:
                        coefficients(u // UT)
                output(TT - 1)
                link.restart()

            head_pairs(dve, step)


def phase_merge(nc, d, r, mergedT, hT_at, free_at):
    parts = (("g1", "hT", DT), ("g2", "hT", DT), ("s5", "yT", FT), ("nsa", "oT", NG))
    with ExitStack() as ctx:
        sb = lambda name, shape: ctx.enter_context(nc.sbuf_tensor("m_" + name, shape, F32))
        sem = ctx.enter_context(Semaphores(nc, "m_"))
        over = lambda name, shape, at: nc.alloc_sbuf_tensor_at("m_" + name, shape, F32R, offset=at)
        w, w_at = [[], []], [[], []]
        for k in range(2):
            for name, _, kt in parts:
                w_at[k].append(nc.sbuf_base)
                w[k].append(sb(f"w_{name}{k}", [P, kt, P]))
        w_split = [[[over(f"w_hi{k}{g}", [P, DT, P], free_at + (2 * k + g) * DT * P * 4),
                     over(f"w_lo{k}{g}", [P, DT, P], w_at[k][g])] for g in range(2)] for k in range(2)]
        h = [ctx.enter_context(nc.sbuf_tensor("m_h_hi", [P, DT, TOK], F32R)), over("h_lo", [P, DT, TPAD], hT_at)]
        hT = r["hT"]
        tanh = [sb(f"tanh{k}", [P, 2, 384]) for k in range(2)]
        ps = [ctx.enter_context(nc.psum_tensor(f"m_ps{k}", [P, 4, 512], F32)) for k in range(2)]
        w_ld = [sem("w_ld0"), sem("w_ld1")]
        multiplied, tanhed, merged, ch_v = sem("multiplied"), sem("tanhed"), sem("merged"), sem("ch_v")
        h_high, h_low, w_high, w_low = sem("h_high"), sem("h_low"), sem("w_high"), sem("w_low")
        block = ctx.enter_context(nc.Block())
        NC = len(CHUNKS)

        def turns(eng, body):
            for n in range(2 * NC):
                body(0, n // NC, n % NC, n)
            with eng.Fori(1, DT // 2 - 1) as i:
                for n in range(2 * NC):
                    body(i, n // NC, n % NC, n)
            for n in range(2 * NC):
                body(DT // 2 - 1, n // NC, n % NC, n)

        first = lambda i: isinstance(i, int) and i == 0

        def splits_next(i, k, c):
            return c == 0 and not (first(i) and k == 0) and not (isinstance(i, int) and 2 * i + k == DT - 1)

        @block.sync
        def _(sp):
            def load(i, k):
                ft = 2 * i + k
                rows = lambda name: d[name].rearrange("z k n -> (z k) n")
                for g in range(2):
                    at = OFF_MIX + D * g
                    sp.dma_start(w[k][g][:], rows("w_in")[:, ds(at + ft * P, P)].rearrange("(c p) n -> p c n", p=P)).then_inc(w_ld[k], 16)
                sp.dma_start(w[k][2][:], rows("s5_w_up")[:, ds(ft * P, P)].rearrange("(c p) n -> p c n", p=P)).then_inc(w_ld[k], 16)
                for g in range(NKV):
                    sp.dma_start(w[k][3][g * DH:(g + 1) * DH, :, :],
                                 rows("nsa_w_up")[g * NG * DH:(g + 1) * NG * DH, ds(ft * P, P)].rearrange("(j q) n -> q j n", q=DH)
                                 ).then_inc(w_ld[k], 16)

            load(0, 0)
            load(0, 1)
            with sp.Fori(1, DT // 2) as i:
                for k in range(2):
                    sp.wait_ge(multiplied, 2 * NC * i + NC * k - NC)
                    load(i, k)

        @block.tensor
        def _(pe):
            def body(i, k, c, n):
                if c == 0:
                    pe.wait_ge(w_ld[k], 80 * i + 80)
                    pe.wait_ge(w_low, 2 * i + k + 1)
                if not (first(i) and n < 2):
                    pe.wait_ge(merged, 2 * NC * i + n - 1)
                at, m = CHUNKS[c]
                for g in range(2):
                    for t in range(DT):
                        if first(i) and n == 0 and g == 0:
                            pe.wait_ge(h_low, t + 1)
                        for e, (wp, hp) in enumerate(TERMS):
                            pe.matmul(ps[n % 2][:, g, 0:m], w_split[k][g][wp][:, t, :], h[hp][:, t, at:at + m],
                                      start=(t == 0 and e == 0), stop=(t == DT - 1 and e == 2))
                for q, (_, src, kt) in list(enumerate(parts))[2:]:
                    for t in range(kt):
                        ins = pe.matmul(ps[n % 2][:, q, 0:m], w[k][q][:, t, :], r[src][:, t, at:at + m],
                                        start=(t == 0), stop=(t == kt - 1))
                ins.then_inc(multiplied, 1)

            turns(pe, body)

        @block.scalar
        def _(act):
            def high(i, k):
                act.wait_ge(w_ld[k], 80 * i + 80)
                for g in range(2):
                    ins = act.activation(w_split[k][g][0][:], w[k][g][:], ACT.Copy)
                ins.then_inc(w_high, 1)

            high(0, 0)
            for c in range(DT):
                act.activation(h[0][:, c, :], hT[:, c, 0:TOK], ACT.Copy).then_inc(h_high, 1)
            high(0, 1)

            def body(i, k, c, n):
                act.wait_ge(multiplied, 2 * NC * i + n + 1)
                if not (first(i) and n < 2):
                    act.wait_ge(merged, 2 * NC * i + n - 1)
                m = CHUNKS[c][1]
                act.activation(tanh[n % 2][:, :, 0:m], ps[n % 2][:, 0:2, 0:m], ACT.Tanh, scale=0.5).then_inc(tanhed, 1)
                if splits_next(i, k, c):
                    high(i + k, 1 - k)

            turns(act, body)

        @block.vector
        def _(dve):
            link = Chain(dve, ch_v)

            def low(i, k):
                dve.wait_ge(w_high, 2 * i + k + 1)
                for g in range(2):
                    ins = dve.tensor_tensor(w_split[k][g][1][:], w[k][g][:], w_split[k][g][0][:].bitcast(F32), ALU.subtract)
                    link.put(ins)
                link.sync()
                dve.sem_inc(w_low, 1)

            low(0, 0)
            for c in range(DT):
                dve.wait_ge(h_high, c + 1)
                dve.tensor_tensor(h[1][:, c, 0:TOK], hT[:, c, 0:TOK], h[0][:, c, :].bitcast(F32), ALU.subtract).then_inc(h_low, 1)
            low(0, 1)
            link.restart()

            def body(i, k, c, n):
                at, m = CHUNKS[c]
                dve.wait_ge(tanhed, 2 * NC * i + n + 1)
                t = tanh[n % 2]
                for q in range(2):
                    link.put(dve.scalar_tensor_tensor(t[:, q, 0:m], t[:, q, 0:m], 1.0, ps[n % 2][:, 2 + q, 0:m], ALU.add, ALU.mult))
                link.sync()
                link(dve.scalar_tensor_tensor(row(mergedT[:, ds(2 * i + k, 1), at:at + m]), t[:, 0, 0:m], 0.5, t[:, 1, 0:m],
                                              ALU.mult, ALU.add))
                dve.sem_inc(merged, 1)
                if splits_next(i, k, c):
                    low(i + k, 1 - k)
                link.restart()

            turns(dve, body)


def phase_out(nc, d, r, mergedT, h2T):
    with ExitStack() as ctx:
        sb = lambda name, shape: ctx.enter_context(nc.sbuf_tensor("o_" + name, shape, F32))
        sem = ctx.enter_context(Semaphores(nc, "o_"))
        ident = r["ident"]
        w = sb("w", [P, DT, D])
        ffnw = sb("ffnw", [P, DT])
        xt = [sb(f"x{k}", [P, D]) for k in range(2)]
        x1 = [sb(f"x1{k}", [P, D]) for k in range(2)]
        xn = [sb(f"xn{k}", [P, D]) for k in range(2)]
        junk = sb("junk", [P, D])
        mt = [sb(f"mt{k}", [P, DT, P]) for k in range(2)]
        ssum, rms, rstd = sb("ssum", [P, 2]), sb("rms", [P, 2]), sb("rstd", [P, 2])
        eps = sb("eps", [P, 1])
        z_ps = [ctx.enter_context(nc.psum_tensor(f"o_z{k}", [P, 2, 512], F32)) for k in range(2)]
        xT_ps = ctx.enter_context(nc.psum_tensor("o_xT", [P, DT, P], F32))
        w_ld = [sem(f"w_ld{c}") for c in range(DT)]
        x_ld = [sem("x_ld0"), sem("x_ld1")]
        (c_ld, mt_set, z_done, x1_set, squared, rooted, xn_set, xT_done, h2_set, eps_set, ch_v) = (
            sem(n) for n in ("c_ld", "mt_set", "z_done", "x1_set", "squared", "rooted", "xn_set", "xT_done", "h2_set", "eps_set", "ch_v"))
        x1_stored = [sem("x1_stored0"), sem("x1_stored1")]
        block = ctx.enter_context(nc.Block())
        x_p = d["x_prompt"].rearrange("a (t p) n -> (a t) p n", p=P)
        x1_d = d["x1"].rearrange("(t p) n -> t p n", p=P)
        tile = lambda ap, t: ap[t] if isinstance(t, int) else ap[ds(t, 1)].rearrange("t p n -> (t p) n")

        @block.sync
        def _(sp):
            def load(t, k):
                if behind(t, 2):
                    sp.wait_ge(x1_set, t - 1)
                if isinstance(t, int) and t == TT:
                    sp.dma_start(xt[k][0:NS, :], d["x_sample"].rearrange("b t n -> (b t) n")).then_inc(x_ld[k], 16)
                else:
                    sp.dma_start(xt[k][:], tile(x_p, t)).then_inc(x_ld[k], 16)
                if isinstance(t, int) and t == 0:
                    wo = d["w_out"].rearrange("z (c p) n -> p (z c) n", p=P)
                    for c in range(DT):
                        sp.dma_start(w[:, c, :], wo[:, c, :]).then_inc(w_ld[c], 16)

            token_tiles(sp, load)

        @block.gpsimd
        def _(pool):
            def body(t, k):
                if behind(t, 2):
                    pool.wait_ge(z_done, t - 1)
                pool.tensor_copy(mt[k][:], mergedT[:, :, ds(t * P, P)]).then_inc(mt_set, 1)
                if behind(t, 1):
                    store(t - 1, 1 - k)

            def store(t, k):
                pool.wait_ge(x1_set, t + 1)
                pool.dma_start(tile(x1_d, t), x1[k][:]).then_inc(x1_stored[k], 16)

            token_tiles(pool, body)
            store(TT, 0)
            pool.wait_ge(x1_stored[0], 16 * (TT // 2 + 1))
            pool.wait_ge(x1_stored[1], 16 * (TT // 2))

        @block.tensor
        def _(pe):
            def transposes(t, k):
                pe.wait_ge(xn_set, t + 1)
                if behind(t, 1):
                    pe.wait_ge(h2_set, t)
                for c in range(DT):
                    ins = pe.transpose(xT_ps[:, c, :], xn[k][:, c * P:(c + 1) * P], ident[:])
                ins.then_inc(xT_done, 1)

            def body(t, k):
                pe.wait_ge(mt_set, t + 1)
                if behind(t, 2):
                    pe.wait_ge(x1_set, t - 1)
                for c in range(DT):
                    if isinstance(t, int) and t == 0:
                        pe.wait_ge(w_ld[c], 16)
                    for b in range(2):
                        ins = pe.matmul(z_ps[k][:, b, :], mt[k][:, c, :], w[:, c, b * 512:(b + 1) * 512],
                                        start=(c == 0), stop=(c == DT - 1))
                ins.then_inc(z_done, 1)
                if behind(t, 1):
                    transposes(t - 1, 1 - k)

            token_tiles(pe, body)
            transposes(TT, 0)

        @block.scalar
        def _(act):
            act.dma_start(ffnw[:], d["norm_ffn_w"].rearrange("z (c p) -> p (z c)", p=P), allow_slow_non_contiguous=True).then_inc(c_ld, 16)
            act.wait_ge(eps_set, 1)

            def body(t, k):
                act.wait_ge(x1_set, t + 1)
                act.activation(junk[:], x1[k][:], ACT.Square, accum_out=ssum[:, k:k + 1]).then_inc(squared, 1)
                act.wait_ge(squared, t + 1)
                act.activation(rms[:, k:k + 1], ssum[:, k:k + 1], ACT.Sqrt, bias=eps[:], scale=1.0 / D).then_inc(rooted, 1)

            token_tiles(act, body)

        @block.vector
        def _(dve):
            link = Chain(dve, ch_v)
            dve.memset(eps[:], EPS).then_inc(eps_set, 1)
            dve.wait_ge(c_ld, 16)

            def weigh(t, k):
                dve.wait_ge(xT_done, t + 1)
                dve.tensor_tensor(h2T[:, :, ds(t * P, P)], xT_ps[:], ffnw[:].unsqueeze(2).to_broadcast([P, DT, P]),
                                  ALU.mult).then_inc(h2_set, 1)

            def body(t, k):
                dve.wait_ge(z_done, t + 1)
                turn = t // 2 if isinstance(t, int) else None
                dve.wait_ge(x_ld[k], 8 * (t - k) + 16)
                if behind(t, 2):
                    dve.wait_ge(x1_stored[k], 8 * (t - k))
                link(dve.scalar_tensor_tensor(x1[k][:], z_ps[k][:].rearrange("p b n -> p (b n)"), 0.5, xt[k][:], ALU.mult, ALU.add))
                dve.sem_inc(x1_set, 1)
                dve.wait_ge(rooted, t + 1)
                link(dve.reciprocal(rstd[:, k:k + 1], rms[:, k:k + 1]))
                if behind(t, 2):
                    dve.wait_ge(xT_done, t - 1)
                link(dve.tensor_scalar(xn[k][:], x1[k][:], rstd[:, k:k + 1], None, ALU.mult))
                link.restart()
                dve.sem_inc(xn_set, 1)
                if behind(t, 1):
                    weigh(t - 1, 1 - k)

            token_tiles(dve, body)
            weigh(TT, 0)


KF = DFF // P
F32R = mybir.dt.float32r
TERMS = ((0, 0), (0, 1), (1, 0))
HEAD = 4
ROW = TOK * 4
place = lambda n: n + HEAD if isinstance(n, int) and n < HEAD else n


def phase_ffn1(nc, d, hT, aT, hT_at, aT_at):
    with ExitStack() as ctx:
        sb = lambda name, shape, dt=F32R: ctx.enter_context(nc.sbuf_tensor("e_" + name, shape, dt))
        sem = ctx.enter_context(Semaphores(nc, "e_"))
        over = lambda name, shape, at: nc.alloc_sbuf_tensor_at("e_" + name, shape, F32R, offset=at)
        h = [sb("h_hi", [P, DT, TOK]), over("h_lo", [P, DT, TPAD], hT_at)]
        w = [[over(f"w_{part}{k}", [P, DT, P], aT_at + (2 * k + m) * ROW) for m, part in enumerate(("hi", "lo"))]
             for k in range(2)]
        raw = [aT[:, 2 * k + 1, 0:DT * P].rearrange("p (c n) -> p c n", c=DT) for k in range(2)]
        ps = [ctx.enter_context(nc.psum_tensor(f"e_ps{k}", [P, 3, 512], F32)) for k in range(2)]
        w_ld = [sem("w_ld0"), sem("w_ld1")]
        squared, stored = sem("squared"), sem("stored")
        h_high, h_split, w_high, w_split, multiplied, taken = (
            sem(n) for n in ("h_high", "h_split", "w_high", "w_split", "multiplied", "taken"))
        block = ctx.enter_context(nc.Block())

        def turns(eng, body):
            body(0, 0)
            body(1, 1)
            with eng.Fori(1, KF // 2) as i:
                for k in range(2):
                    body(2 * i + k, k)

        @block.sync
        def _(sp):
            def load(i, k):
                if not (isinstance(i, int) and i == 0):
                    sp.wait_ge(multiplied, 2 * i + k - 1)
                sp.nop(nofuse=True)
                sp.dma_start(raw[k], d["w_ffn1"][0, :, ds((2 * i + k) * P, P)].rearrange("(c p) n -> p c n", p=P)).then_inc(w_ld[k], 16)

            load(0, 0)
            load(0, 1)
            with sp.Fori(1, KF // 2) as i:
                load(i, 0)
                load(i, 1)

        @block.gpsimd
        def _(pool):
            for n in range(HEAD):
                pool.wait_ge(squared, n + 1)
                pool.dma_start(d["a_head"][:, n, :], aT[:, place(n), :]).then_inc(stored, 16)
            pool.wait_ge(stored, 16 * HEAD)

        @block.tensor
        def _(pe):
            def body(n, k):
                pe.wait_ge(w_split, n + 1)
                if behind(n, 2):
                    pe.wait_ge(taken, n - 1)
                for c in range(DT):
                    if not behind(n, 1):
                        pe.wait_ge(h_split, c + 1)
                    for m, (wp, hp) in enumerate(TERMS):
                        for b, (at, cols) in enumerate(CHUNKS):
                            ins = pe.matmul(ps[k][:, b, 0:cols], w[k][wp][:, c, :], h[hp][:, c, at:at + cols],
                                            start=(c == 0 and m == 0), stop=(c == DT - 1 and m == 2))
                ins.then_inc(multiplied, 1)

            turns(pe, body)

        @block.scalar
        def _(act):
            def high(i, k):
                act.wait_ge(w_ld[k], 16 * i + 16)
                act.activation(w[k][0][:], raw[k], ACT.Copy).then_inc(w_high, 1)

            def take(n, k):
                act.wait_ge(multiplied, n + 1)
                for b, (at, cols) in enumerate(CHUNKS):
                    ins = act.activation(row(aT[:, ds(place(n), 1), at:at + cols]), ps[k][:, b, 0:cols], ACT.Relu)
                ins.then_inc(taken, 1)

            high(0, 0)
            for c in range(DT):
                act.activation(h[0][:, c, :], hT[:, c, 0:TOK], ACT.Copy).then_inc(h_high, 1)
            high(0, 1)
            for n in range(HEAD):
                take(n, n % 2)
                high(n // 2 + 1, n % 2)
            act.wait_ge(stored, 16 * HEAD)
            with act.Fori(HEAD // 2 + 1, KF // 2) as i:
                for k in range(2):
                    take(2 * i + k - 2, k)
                    high(i, k)
            take(KF - 2, 0)
            take(KF - 1, 1)

        @block.vector
        def _(dve):
            def low(n, k):
                dve.wait_ge(w_high, n + 1)
                dve.tensor_tensor(w[k][1][:], raw[k], w[k][0][:].bitcast(F32), ALU.subtract).then_inc(w_split, 1)

            def square(n, k):
                dve.wait_ge(taken, n + 1)
                a = row(aT[:, ds(place(n), 1), :])
                dve.tensor_tensor(a, a, a, ALU.mult).then_inc(squared, 1)

            low(0, 0)
            for c in range(DT):
                dve.wait_ge(h_high, c + 1)
                dve.tensor_tensor(h[1][:, c, 0:TOK], hT[:, c, 0:TOK], h[0][:, c, :].bitcast(F32), ALU.subtract).then_inc(h_split, 1)
            low(1, 1)
            for n in range(HEAD):
                low(n + 2, n % 2)
                square(n, n % 2)
            with dve.Fori(HEAD // 2 + 1, KF // 2) as i:
                for k in range(2):
                    low(2 * i + k, k)
                    square(2 * i + k - 2, k)
            square(KF - 2, 0)
            square(KF - 1, 1)


def phase_ffn2(nc, d, r, aT, hT_at):
    with ExitStack() as ctx:
        sb = lambda name, shape, dt=F32: ctx.enter_context(nc.sbuf_tensor("f_" + name, shape, dt))
        sem = ctx.enter_context(Semaphores(nc, "f_"))
        ident = r["ident"]
        KC, AB = 4, 4
        NK, PASSES = KF // KC, D // 256
        chunks = [(m + 1) % NK for m in range(NK)]
        w_hi = [sb(f"w_hi{k}", [P, KC, 256], F32R) for k in range(2)]
        w_at = []
        raw = []
        for k in range(2):
            w_at.append(nc.sbuf_base)
            raw.append(sb(f"w{k}", [P, KC, 256]))
        w_lo = [nc.alloc_sbuf_tensor_at(f"f_w_lo{k}", [P, KC, 256], F32R, offset=w_at[k]) for k in range(2)]
        hT = r["hT"]
        yT, a_hi = hT[:, 0:2, :], [nc.alloc_sbuf_tensor_at(f"f_a_hi{k}", [P, TOK], F32R, offset=hT_at + (4 + k) * TPAD * 4)
                                 for k in range(AB)]
        x1s = hT[:, 2:4, :].rearrange("p a n -> p (a n)").rearrange("p (t n) -> p t n", n=256)
        a_lo = [sb(f"a_lo{k}", [P, TOK], F32R) for k in range(AB)]
        w = [[w_hi[k], w_lo[k]] for k in range(2)]
        a = [[a_hi[k], a_lo[k]] for k in range(AB)]
        ps = [ctx.enter_context(nc.psum_tensor(f"f_ps{f}", [P, 3, 512], F32)) for f in range(2)]
        back = [ctx.enter_context(nc.psum_tensor(f"f_back{k}", [P, 4, P], F32)) for k in range(2)]
        groups = [(f, t, min(4, NT - t)) for f in range(2) for t in range(0, NT, 4)]
        G = len(groups)
        assert G % 2 == 0 and G < NK
        w_ld, a_ld, x_ld, stored = [sem("w_ld0"), sem("w_ld1")], sem("a_ld"), sem("x_ld"), sem("stored")
        w_high, w_split, a_high, a_split, multiplied = (sem(n) for n in ("w_high", "w_split", "a_high", "a_split", "multiplied"))
        taken, backed, y_set, zeroed = [sem("taken0"), sem("taken1")], sem("backed"), sem("y_set"), sem("zeroed")
        block = ctx.enter_context(nc.Block())
        first = lambda q: isinstance(q, int)

        def passes(eng, body):
            body(0)
            with eng.Fori(1, PASSES) as q:
                body(q)

        @block.sync
        def _(sp):
            def body(q):
                for m, c in enumerate(chunks):
                    if not (first(q) and m < 2):
                        sp.wait_ge(multiplied, KF * q + KC * (m - 1))
                    sp.nop(nofuse=True)
                    sp.dma_start(raw[m % 2][:], d["w_ffn2"][0, c * KC * P:(c + 1) * KC * P, ds(256 * q, 256)]
                                 .rearrange("(c p) n -> p c n", p=P)).then_inc(w_ld[m % 2], 16)

            passes(sp, body)

        @block.gpsimd
        def _(pool):
            pool.dma_start(aT[:, 0:HEAD, :], d["a_head"]).then_inc(a_ld, 16)

            def body(q):
                if not first(q):
                    pool.wait_ge(stored, 32 * q)
                pool.nop(nofuse=True)
                pool.dma_start(x1s, d["x1"].rearrange("(t p) n -> p t n", p=P)[:, :, ds(256 * q, 256)]).then_inc(x_ld, 16)
                pool.wait_ge(y_set, G * q + G)
                pool.nop(nofuse=True)
                pool.dma_start(d["y_prompt"].rearrange("a (t p) n -> p (a t) n", p=P)[:, :, ds(256 * q, 256)], x1s[:, 0:TT, :]).then_inc(stored, 16)
                pool.dma_start(d["y_sample"].rearrange("b t n -> (b t) n")[:, ds(256 * q, 256)], x1s[0:NS, TT, :]).then_inc(stored, 16)

            passes(pool, body)
            pool.wait_ge(stored, 32 * PASSES)

        @block.tensor
        def _(pe):
            def back_to_rows(q, g):
                f, t0, n = groups[g]
                pe.wait_ge(taken[f], q + 1)
                if not (first(q) and g < 2 and q == 0):
                    pe.wait_ge(y_set, G * q + max(g - 1, 0))
                pe.nop(nofuse=True)
                for t in range(n):
                    ins = pe.transpose(back[g % 2][:, t, :], yT[:, f, (t0 + t) * P:(t0 + t + 1) * P], ident[:])
                ins.then_inc(backed, 1)

            def body(q):
                for m, c in enumerate(chunks):
                    pe.wait_ge(w_split, NK * q + m + 1)
                    for k in range(KC):
                        n = KC * m + k
                        pe.wait_ge(a_split, KF * q + n + 1)
                        for f in range(2):
                            if n == 0 and not first(q):
                                pe.wait_ge(taken[f], q)
                            for e, (wp, ap) in enumerate(TERMS):
                                for b, (at, cols) in enumerate(CHUNKS):
                                    ins = pe.matmul(ps[f][:, b, 0:cols], w[m % 2][wp][:, k, f * P:(f + 1) * P],
                                                    a[n % AB][ap][:, at:at + cols],
                                                    start=(n == 0 and e == 0), stop=(n == KF - 1 and e == 2))
                        ins.then_inc(multiplied, 1)
                    if not first(q) and m < G:
                        back_to_rows(q - 1, m)

            pe.wait_ge(zeroed, 1)
            passes(pe, body)
            for g in range(G):
                back_to_rows(PASSES - 1, g)

        def take(eng, copy, q, f):
            eng.wait_ge(multiplied, KF * q + KF)
            if not (first(q) and q == 0):
                eng.wait_ge(backed, G * q)
            for b, (at, cols) in enumerate(CHUNKS):
                ins = copy(yT[:, f, at:at + cols], ps[f][:, b, 0:cols])
            ins.then_inc(taken[f], 1)

        @block.scalar
        def _(act):
            copy = lambda out, in_: act.activation(out, in_, ACT.Copy)

            def body(q):
                for m, c in enumerate(chunks):
                    if c == 0 and first(q):
                        act.wait_ge(a_ld, 16)
                    act.wait_ge(w_ld[m % 2], 16 * (NK // 2 * q + m // 2) + 16)
                    copy(w_hi[m % 2][:], raw[m % 2][:]).then_inc(w_high, 1)
                    for k in range(KC):
                        n = KC * m + k
                        if not (first(q) and n < AB):
                            act.wait_ge(multiplied, KF * q + n - AB + 1)
                        copy(a_hi[n % AB][:], aT[:, KC * c + k, :]).then_inc(a_high, 1)
                    if m == 0 and not first(q):
                        take(act, copy, q - 1, 0)

            passes(act, body)
            take(act, copy, PASSES - 1, 0)

        @block.vector
        def _(dve):
            dve.memset(yT[:, :, TOK:TPAD], 0.0).then_inc(zeroed, 1)

            def add(q, g):
                f, t0, n = groups[g]
                if g == 0:
                    dve.wait_ge(x_ld, 16 * q + 16)
                dve.wait_ge(backed, G * q + g + 1)
                at = x1s[:, t0:t0 + n, f * P:(f + 1) * P]
                dve.tensor_tensor(at, back[g % 2][:, 0:n, :], at, ALU.add).then_inc(y_set, 1)

            def body(q):
                for m, c in enumerate(chunks):
                    dve.wait_ge(w_high, NK * q + m + 1)
                    dve.tensor_tensor(w_lo[m % 2][:], raw[m % 2][:], w_hi[m % 2][:].bitcast(F32), ALU.subtract).then_inc(w_split, 1)
                    for k in range(KC):
                        n = KC * m + k
                        dve.wait_ge(a_high, KF * q + n + 1)
                        dve.tensor_tensor(a_lo[n % AB][:], aT[:, KC * c + k, :], a_hi[n % AB][:].bitcast(F32),
                                          ALU.subtract).then_inc(a_split, 1)
                    if m == 0 and not first(q):
                        take(dve, dve.tensor_copy, q - 1, 1)
                    if not first(q) and 1 <= m <= G:
                        add(q - 1, m - 1)

            passes(dve, body)
            take(dve, dve.tensor_copy, PASSES - 1, 1)
            for g in range(G):
                add(PASSES - 1, g)


def constants():
    half = DH // 2
    inv = np.float32(10000.0) ** (-np.arange(half, dtype=np.float32) / np.float32(half))
    pos = np.zeros(TPAD, np.float32)
    pos[:SEQ] = np.arange(SEQ)
    pos[SEQ:TOK] = PAST + np.arange(NS) % TS
    ang = pos[:, None] * inv[None, :].astype(np.float32)
    rope = np.stack([np.cos(ang.astype(np.float64)), np.sin(ang.astype(np.float64))], 1).astype(np.float32)
    out = {"rope": rope, "identity": np.eye(P, dtype=np.float32)}
    gsum = np.zeros((NKV, NG, TS, NKV, TS), np.float32)
    for g in range(NKV):
        for t in range(TS):
            gsum[g, :, t, g, t] = 1.0
    gsum = gsum.reshape(MR, GT)
    t = np.arange(MR) % TS
    key = 4 * np.arange(P)[None, :] + np.arange(WIN_T)[:, None]
    win_mask = np.where(key.reshape(1, WIN) <= t[:, None], NEG, 0.0).astype(np.float32)
    new_mask = np.where(np.arange(TS)[None, :] > t[:, None], NEG, 0.0).astype(np.float32)
    q, k = np.arange(P)[:, None], np.arange(P)[None, :]
    mask = lambda hidden: np.where(hidden, NEG, 0.0).astype(np.float32)
    ends = CS * np.arange(NC_P) + CL - 1
    out.update(causal=mask(k > q), behind_win=mask(k <= q),
               cmp_mask=mask(ends[None, None, :] > (P * np.arange(TT)[None, :] + q)[:, :, None]),
               any_cmp=(q >= CL - 1).astype(np.float32))
    out.update(win_mask=win_mask, new_mask=new_mask)
    out.update(gsum=gsum, gspread=np.ascontiguousarray(gsum.T), in_page=(np.arange(P, dtype=np.int32) % (PAGE // CS))[:, None])
    return out


SCRATCH = {"x1": (TPAD, D), "a_head": (P, HEAD, TOK), "v_new": (NS, 2 * KVW), "g_new": (NS, 3 * NH)}


def build(nc, d):
    ap = lambda name, dims: bass.AP(d[name].tensor, 0, dims)
    d["normw_q"] = ap("q_norm_w", [(0, P), (0, NH), (1, DH)])
    d["normw_k"] = ap("k_norm_w", [(0, P), (DH, 3), (1, DH)])
    columns = lambda name: lambda j: d[name][0, :, ds(256 * j, 256)].rearrange("(c p) n -> p c n", p=P)
    tokens = lambda t, ft, at, n: row(t[:, ds(ft, 1), at:at + n])
    with ExitStack() as whole:
        ident = whole.enter_context(nc.sbuf_tensor("ident", [P, P], F32))
        hT_at = nc.sbuf_base
        hT = whole.enter_context(nc.sbuf_tensor("hT", [P, DT, TPAD], F32))
        with ExitStack() as mixers:
            sb = lambda name, shape, stack=mixers: stack.enter_context(nc.sbuf_tensor(name, shape, F32))
            yT_at = nc.sbuf_base
            yT = sb("yT", [P, FT, TPAD])
            n_qk, n_v = (NG + 2) * TPAD, NT * 3 * KVW
            kept = sb("kept", [P, n_qk + n_v])
            assert DT * TPAD <= n_qk + n_v
            mergedT = kept[:, 0:DT * TPAD].rearrange("p (c n) -> p c n", c=DT)
            r = {"ident": ident, "hT": hT, "uT": yT, "yT": yT,
                 "qkT": kept[:, 0:n_qk].rearrange("p (c n) -> p c n", n=TPAD),
                 "v_nat": kept[:, n_qk:].rearrange("p (t c w) -> p t c w", c=3, w=KVW),
                 "gates": sb("gates", [P, NT, 3 * NH]), "oTs": sb("oTs", [P, NG, NS]),
                 "kc_p": sb("kc_p", [P, NC_P]), "vc_p": sb("vc_p", [NC_P, KVW])}
            phase_project(nc, d, r)
            phase_s5(nc, d, r)
            with ExitStack() as sampled:
                r["qbd"] = sb("qbd", [P, NB + 1, MR], sampled)
                r["g_rows"] = sb("g_rows", [MR, NB, 3], sampled)
                r["osum"] = sb("osum", [MR, NB, DH], sampled)
                r["sel_bias"] = sb("sel_bias", [MR, NB, NSLC], sampled)
                phase_compress(nc, d, r)
                phase_sampled(nc, d, r)
            r["oT"] = sb("oT", [P, NG, TPAD])
            phase_prompt(nc, d, r)
            yT2 = sb("yT2", [P, FT, TPAD])
            phase_gemm(nc, "glu", columns("s5_w_glu"), 1, FT, yT,
                       lambda act, ft, c, at, n, ps: act.activation(tokens(yT2, ft, at, n), ps, ACT.Tanh, scale=0.5),
                       lambda dve, ft, c, at, n, link: link(dve.scalar_tensor_tensor(
                           tokens(yT2, ft, at, n), tokens(yT2, ft, at, n), 1.0, tokens(yT, ft, at, n), ALU.add, ALU.mult)))
            r["yT"] = yT2
            phase_merge(nc, d, r, mergedT, hT_at, yT_at)
            phase_out(nc, d, r, mergedT, hT)
        aT_at = nc.sbuf_base
        aT = whole.enter_context(nc.sbuf_tensor("aT", [P, KF, TOK], F32))
        phase_ffn1(nc, d, hT, aT, hT_at, aT_at)
        phase_ffn2(nc, d, r, aT, hT_at)


_INS = ["x_prompt", "x_sample", "cache_k_cmp", "cache_v_cmp", "cache_k_slc", "cache_v_slc", "state_k_win", "state_v_win",
        "state_s5_re", "state_s5_im", "page_table", "norm_mix_w", "w_in", "s5_lam_re", "s5_lam_im", "s5_log_dt",
        "s5_b_re", "s5_b_im", "s5_c_re", "s5_c_im", "s5_d", "s5_w_glu", "s5_w_up", "q_norm_w", "k_norm_w", "cmp_pe_k",
        "cmp_wk1", "cmp_wk2", "cmp_pe_v", "cmp_wv1", "cmp_wv2", "nsa_w_up", "w_out", "norm_ffn_w", "w_ffn1", "w_ffn2"]
_KV_P, _KV_S = (1, 1, SEQ, NKV, DH), (1, NB, TS, NKV, DH)
_OUTS = [("y_prompt", (1, SEQ, D)), ("y_sample", (NB, TS, D)), ("k_cmp_p", _KV_P), ("k_cmp_s", _KV_S),
         ("v_cmp_p", _KV_P), ("v_cmp_s", _KV_S), ("k_slc_p", _KV_P), ("k_slc_s", _KV_S), ("v_slc_p", _KV_P),
         ("v_slc_s", _KV_S), ("k_win_p", (1, 1, WIN, NKV, DH)), ("k_win_s", (1, NB, WIN, NKV, DH)),
         ("v_win_p", (1, 1, WIN, NKV, DH)), ("v_win_s", (1, NB, WIN, NKV, DH)), ("s5_re_p", (1, 1, S5G, S5P)),
         ("s5_re_s", (1, NB, S5G, S5P)), ("s5_im_p", (1, 1, S5G, S5P)), ("s5_im_s", (1, NB, S5G, S5P))]


def kernel(**inputs):
    import concourse.bacc as bacc
    from concourse.bass_utils import run_bass_kernel_spmd

    nc = bacc.Bacc("TRN2", target_bir_lowering=False, num_devices=1)
    arrays, d = {}, {}
    given = {name: inputs[name] for name in _INS}
    for name, a in {**given, **constants()}.items():
        a = np.ascontiguousarray(a)
        arrays["in_" + name] = a
        d[name] = nc.dram_tensor("in_" + name, a.shape, mybir.dt.from_np(a.dtype), kind="ExternalInput").ap()
    for name, shape in _OUTS:
        d[name] = nc.dram_tensor("out_" + name, shape, F32, kind="ExternalOutput").ap()
    for name, shape in SCRATCH.items():
        d[name] = nc.dram_tensor("scratch_" + name, shape, F32, kind="Internal").ap()
    build(nc, d)
    result = run_bass_kernel_spmd(nc, [arrays], core_ids=[0])
    return tuple(result.results[0]["out_" + name] for name, _ in _OUTS)
```
